# Optimizing a Trainium2 kernel written in Bass

```python
import jax, jax.numpy as jnp
from jax import lax
import numpy as np

D_MODEL = 1024
BATCH = 1
SEQ = 128
DEPTH = 2
DEC_BATCH = 1
DEC_SEQ = 256
PAST_LEN = 128

F32 = jnp.float32
NEG = -1e30
GRID_W = 64
HEAD_DIM = 64
SCALE = HEAD_DIM ** -0.5
ROPE_BASE = 10000.0
EPS = 1e-6
HG_HEADS = 4
HG_DK = 64
HG_DV = 64
HG_W = HG_HEADS * HG_DK
HG_CHUNK = 16
WIN_HEADS = 6
WIN_KV = 2
WIN = 128
POOL_GROUPS = 4
POOL_GC = 64
POOL_W = POOL_GROUPS * POOL_GC
POOL_SIZES = (2, 4, 8, 16)
NA_HEADS = 4
NA_KH = 8
NA_KW = 16
NA_QW = 16
NA_SPAN = NA_QW + NA_KW
QBLK = 128
N_BRANCH = 4
BRANCH_W = (HG_W, WIN_HEADS * HEAD_DIM, POOL_W, NA_HEADS * HEAD_DIM)
MIX_W = sum(BRANCH_W)
IN_SIZES = (HG_W, HG_W, HG_W, HG_W, HG_W,
            WIN_HEADS * HEAD_DIM, WIN_KV * HEAD_DIM, WIN_KV * HEAD_DIM,
            POOL_W,
            NA_HEADS * HEAD_DIM, NA_HEADS * HEAD_DIM, NA_HEADS * HEAD_DIM)
IN_COLS = sum(IN_SIZES)
N_EXPERTS = 32
TOP_K = 4
D_EXPERT = 256
D_SHARED = 256
ROUTED_SCALE = 2.5
MOE_BLK = 128

kernel_name = 'hybrid_diffusion_ctx_prefix_step'

def _split(x, sizes):
    return jnp.split(x, np.cumsum(sizes)[:-1].tolist(), axis=-1)

def rms_norm(x, g):
    xf = x.astype(F32)
    y = xf * lax.rsqrt(jnp.mean(xf * xf, axis=-1, keepdims=True) + EPS)
    return (y * g.astype(F32)).astype(x.dtype)

def modulation(cvec, w_mod, b_mod):
    m = jax.nn.silu(cvec) @ w_mod + b_mod
    return jnp.split(m[:, None, :], 6, axis=-1)

def axial_rope(x):
    n_ = x.shape[1]
    t = np.arange(n_)
    half = HEAD_DIM // 2
    quarter = half // 2
    inv = (ROPE_BASE ** (-np.arange(quarter) / quarter)).astype(np.float32)
    xf = x.astype(F32)

    def rot(xp, pos):
        ang = pos.astype(np.float32)[:, None] * inv[None]
        cos = jnp.asarray(np.cos(ang), F32)[None, :, None, :]
        sin = jnp.asarray(np.sin(ang), F32)[None, :, None, :]
        x1, x2 = xp[..., :quarter], xp[..., quarter:]
        return jnp.concatenate([x1 * cos - x2 * sin, x2 * cos + x1 * sin], axis=-1)

    out = jnp.concatenate([rot(xf[..., :half], t // GRID_W), rot(xf[..., half:], t % GRID_W)], axis=-1)
    return out.astype(x.dtype)

def hgrn_scan(q, logf, k, v, s0):
    b_, t_, h_, dk = q.shape
    dv = v.shape[-1]
    n = t_ // HG_CHUNK
    q, logf, k = (a.reshape(b_, n, HG_CHUNK, h_, dk) for a in (q, logf, k))
    v = v.reshape(b_, n, HG_CHUNK, h_, dv)
    cum = jnp.cumsum(logf, axis=2)
    last = cum[:, :, -1]
    causal = np.tril(np.ones((HG_CHUNK, HG_CHUNK), dtype=bool))
    diff = cum[:, :, :, None] - cum[:, :, None, :]
    decay = jnp.exp(jnp.where(causal[:, :, None, None], diff, NEG))
    att = jnp.einsum('bntshk,bnshk->bnhts', decay * q[:, :, :, None], k)
    o_intra = jnp.einsum('bnhts,bnshv->bnthv', att, v)
    ds = jnp.einsum('bnshk,bnshv->bnhkv', k * jnp.exp(last[:, :, None] - cum), v)

    def step(s, inp):
        dec, d = inp
        return dec[..., None] * s + d, s

    s_fin, s_start = lax.scan(step, s0, (jnp.moveaxis(jnp.exp(last), 1, 0), jnp.moveaxis(ds, 1, 0)))
    o_inter = jnp.einsum('bnthk,nbhkv->bnthv', q * jnp.exp(cum), s_start)
    return (o_intra + o_inter).reshape(b_, t_, h_, dv), s_fin

def hgrn_mixer(zq, zf_fwd, zf_bwd, zi, zg, lb, onorm, s0):
    b_, t_, _ = zq.shape
    hd = lambda a: a.astype(F32).reshape(b_, t_, HG_HEADS, -1)
    q, i = hd(zq), hd(zi)

    def gate(z, lbd):
        lbd = lbd.astype(F32).reshape(HG_HEADS, HG_DK)
        f = lbd + (1.0 - lbd) * jax.nn.sigmoid(hd(z))
        return jnp.log(f), 1.0 - f

    lf_f, k_f = gate(zf_fwd, lb[0])
    lf_b, k_b = gate(zf_bwd, lb[1])
    o_f, s_f = hgrn_scan(q, lf_f, k_f, i, s0[:, 0])
    rev = lambda a: jnp.flip(a, axis=1)
    o_b, s_b = hgrn_scan(rev(q), rev(lf_b), rev(k_b), rev(i), s0[:, 1])
    o = o_f + rev(o_b)
    o = rms_norm(o, onorm) * jax.nn.silu(hd(zg))
    return o.reshape(b_, t_, HG_W).astype(zq.dtype), jnp.stack([s_f, s_b], axis=1)

def pool_mixer(u, w_pool, scale):
    b_, t_, _ = u.shape
    uf = u.astype(F32).reshape(b_, t_, POOL_GROUPS, POOL_GC)
    csum = jnp.concatenate([jnp.zeros((b_, 1, POOL_GROUPS, POOL_GC), F32), jnp.cumsum(uf, axis=1)], axis=1)
    pos = np.arange(t_)[:, None]
    half = np.array(POOL_SIZES)[None] // 2
    lo = np.clip(pos - half, 0, t_)
    hi = np.clip(pos + half, 0, t_)
    grp = np.arange(POOL_GROUPS)[None]
    win_sum = csum[:, hi, grp] - csum[:, lo, grp]
    mean = win_sum / (hi - lo).astype(np.float32)[None, :, :, None]
    y = jnp.einsum('btgc,gcd->btgd', mean - uf, w_pool.astype(F32))
    y = y * scale.astype(F32).reshape(POOL_GROUPS, POOL_GC)
    return y.reshape(b_, t_, POOL_W).astype(u.dtype)

def full_attn(q, k, v, sink):
    b_, l_, hq, d = q.shape
    hkv = k.shape[2]
    g = hq // hkv
    qb = jnp.moveaxis(q.reshape(b_, l_ // QBLK, QBLK, hkv, g, d), 1, 0)

    def one(qi):
        s = jnp.einsum('bqhgd,bkhd->bhgqk', qi, k, preferred_element_type=F32) * SCALE
        if sink is not None:
            sk = jnp.broadcast_to(sink.astype(F32).reshape(1, hkv, g, 1, 1), s.shape[:-1] + (1,))
            s = jnp.concatenate([s, sk], axis=-1)
        p = jax.nn.softmax(s, axis=-1)[..., :l_].astype(v.dtype)
        return jnp.einsum('bhgqk,bkhd->bqhgd', p, v)

    o = lax.map(one, qb)
    return jnp.moveaxis(o, 0, 1).reshape(b_, l_, hq * d)

def window_attn(q, k, v, kc, vc, sink):
    b_, n_, hq, d = q.shape
    hkv = k.shape[2]
    g = hq // hkv
    nb = n_ // WIN
    qb = q.reshape(b_, nb, WIN, hkv, g, d)

    def band(a):
        ap = jnp.pad(a, ((0, 0), (WIN, WIN), (0, 0), (0, 0))).reshape(b_, nb + 2, WIN, hkv, d)
        return jnp.concatenate([ap[:, :-2], ap[:, 1:-1], ap[:, 2:]], axis=2)

    kb, vb = band(k), band(v)
    qpos = np.arange(nb)[:, None] * WIN + np.arange(WIN)[None]
    kpos = (np.arange(nb)[:, None] - 1) * WIN + np.arange(3 * WIN)[None]
    kp = kpos[:, None, :]
    valid = (np.abs(kp - qpos[:, :, None]) <= WIN) & (kp >= 0) & (kp < n_)
    s_loc = jnp.einsum('bnqhgd,bnkhd->bnhgqk', qb, kb, preferred_element_type=F32) * SCALE
    s_loc = jnp.where(valid[None, :, None, None], s_loc, NEG)
    s_ctx = jnp.einsum('bnqhgd,blhd->bnhgql', qb, kc, preferred_element_type=F32) * SCALE
    s_sink = jnp.broadcast_to(sink.astype(F32).reshape(1, 1, hkv, g, 1, 1), s_loc.shape[:-1] + (1,))
    p = jax.nn.softmax(jnp.concatenate([s_loc, s_ctx, s_sink], axis=-1), axis=-1).astype(v.dtype)
    nk = 3 * WIN
    o = (jnp.einsum('bnhgqk,bnkhd->bnqhgd', p[..., :nk], vb)
         + jnp.einsum('bnhgql,blhd->bnqhgd', p[..., nk:nk + kc.shape[1]], vc))
    return o.reshape(b_, n_, hq * d)

def natten(q, k, v, kc, vc, rpb):
    b_, n_, h_, d = q.shape
    rows = n_ // GRID_W
    kh = min(NA_KH, rows)
    ncb = GRID_W // NA_QW
    r = np.arange(rows)
    krow = np.clip(r - kh // 2, 0, rows - kh)[:, None] + np.arange(kh)[None]
    cb = np.arange(ncb)
    qcol = cb[:, None] * NA_QW + np.arange(NA_QW)[None]
    kcol = np.clip(cb * NA_QW - NA_KW // 2, 0, GRID_W - NA_SPAN)[:, None] + np.arange(NA_SPAN)[None]
    cstart = np.clip(qcol - NA_KW // 2, 0, GRID_W - NA_KW)
    in_win = (kcol[:, None, :] >= cstart[:, :, None]) & (kcol[:, None, :] < cstart[:, :, None] + NA_KW)
    dr = krow - r[:, None] + NA_KH - 1
    dc = np.clip(kcol[:, None, :] - qcol[:, :, None] + NA_KW - 1, 0, 2 * NA_KW - 2)
    nk = kh * NA_SPAN
    bias = rpb.astype(F32)[:, dr[:, None, None, :, None], dc[None, :, :, None, :]]
    bias = jnp.transpose(bias, (1, 2, 0, 3, 4, 5)).reshape(rows, ncb, h_, NA_QW, nk)
    mask = np.broadcast_to(in_win[None, :, None, :, None, :],
                           (rows, ncb, 1, NA_QW, kh, NA_SPAN)).reshape(rows, ncb, 1, NA_QW, nk)

    def gather(a):
        ag = a.reshape(b_, rows, GRID_W, h_, d)[:, krow[:, None, :, None], kcol[None, :, None, :]]
        return ag.reshape(b_, rows, ncb, nk, h_, d)

    kblk, vblk = gather(k), gather(v)
    qb = q.reshape(b_, rows, ncb, NA_QW, h_, d)
    s_loc = jnp.einsum('brcqhd,brckhd->brchqk', qb, kblk, preferred_element_type=F32) * SCALE + bias[None]
    s_loc = jnp.where(mask[None], s_loc, NEG)
    s_ctx = jnp.einsum('brcqhd,blhd->brchql', qb, kc, preferred_element_type=F32) * SCALE
    p = jax.nn.softmax(jnp.concatenate([s_loc, s_ctx], axis=-1), axis=-1).astype(v.dtype)
    o = (jnp.einsum('brchqk,brckhd->brcqhd', p[..., :nk], vblk)
         + jnp.einsum('brchql,blhd->brcqhd', p[..., nk:], vc))
    return o.reshape(b_, n_, h_ * d)

def moe(h, w_router, b_router, w_eg, w_eu, w_ed, w_sg, w_su, w_sd):
    b_, t_, d = h.shape
    tok = h.reshape(-1, d)
    scores = jax.nn.sigmoid(jnp.einsum('nd,de->ne', tok, w_router, preferred_element_type=F32))
    _, idx = lax.top_k(scores + b_router.astype(F32), TOP_K)
    sel = jnp.take_along_axis(scores, idx, axis=-1)
    wts = ROUTED_SCALE * sel / jnp.sum(sel, axis=-1, keepdims=True)
    gate = jnp.einsum('nk,nke->ne', wts, jax.nn.one_hot(idx, N_EXPERTS, dtype=F32)).astype(h.dtype)

    def block(args):
        tb, gb = args
        a = jax.nn.silu(jnp.einsum('nd,edf->nef', tb, w_eg)) * jnp.einsum('nd,edf->nef', tb, w_eu)
        return jnp.einsum('nef,efd->nd', a * gb[..., None], w_ed)

    nblk = tok.shape[0] // MOE_BLK
    routed = lax.map(block, (tok.reshape(nblk, MOE_BLK, d), gate.reshape(nblk, MOE_BLK, N_EXPERTS)))
    shared = (jax.nn.silu(tok @ w_sg) * (tok @ w_su)) @ w_sd
    return (routed.reshape(-1, d) + shared).reshape(b_, t_, d)

def trunk_layer(x, cvec, lw, lb, ctx):
    bsz, t_, _ = x.shape
    sh1, sc1, g1, sh2, sc2, g2 = modulation(cvec, lw['w_mod'], lw['b_mod'])
    h = rms_norm(x, lw['norm1_g']) * (1 + sc1) + sh1
    (aq, af_f, af_b, ai, ag, bq, bk, bv, cu, dq, dk, dv) = _split(h @ lw['w_in'], IN_SIZES)
    heads = lambda a, n: a.reshape(bsz, t_, n, HEAD_DIM)
    latent = ctx is not None
    s0 = ctx[4].astype(F32) if latent else jnp.zeros((bsz, 2, HG_HEADS, HG_DK, HG_DV), F32)
    y_a, s_fin = hgrn_mixer(aq, af_f, af_b, ai, ag, lb, lw['hg_onorm'], s0)
    q_b = rms_norm(heads(bq, WIN_HEADS), lw['win_qn'])
    k_b = rms_norm(heads(bk, WIN_KV), lw['win_kn'])
    v_b = heads(bv, WIN_KV)
    q_d = rms_norm(heads(dq, NA_HEADS), lw['na_qn'])
    k_d = rms_norm(heads(dk, NA_HEADS), lw['na_kn'])
    v_d = heads(dv, NA_HEADS)
    y_c = pool_mixer(cu, lw['pool_w'], lw['pool_scale'])
    if latent:
        y_b = window_attn(axial_rope(q_b), axial_rope(k_b), v_b, ctx[0], ctx[1], lw['win_sink'])
        y_d = natten(q_d, k_d, v_d, ctx[2], ctx[3], lw['na_rpb'])
    else:
        y_b = full_attn(q_b, k_b, v_b, lw['win_sink'])
        y_d = full_attn(q_d, k_d, v_d, None)
    g_a, g_b, g_c, g_d = jnp.split(jax.nn.sigmoid(h @ lw['w_mgate'] + lw['b_mgate']), N_BRANCH, axis=-1)
    offs = np.concatenate([[0], np.cumsum(BRANCH_W)])
    wb = lw['w_branch']
    merged = (g_a * (y_a @ wb[offs[0]:offs[1]]) + g_b * (y_b @ wb[offs[1]:offs[2]])
              + g_c * (y_c @ wb[offs[2]:offs[3]]) + g_d * (y_d @ wb[offs[3]:offs[4]]))
    x = x + g1 * (merged @ lw['w_out'])
    h2 = rms_norm(x, lw['norm2_g']) * (1 + sc2) + sh2
    x = x + g2 * moe(h2, lw['w_router'], lw['b_router'], lw['w_eg'], lw['w_eu'], lw['w_ed'],
                     lw['w_sg'], lw['w_su'], lw['w_sd'])
    return x, (k_b, v_b, k_d, v_d, s_fin)

def setup_inputs(seed: int = 0) -> dict:
    key = jax.random.key(seed)
    ks = iter(jax.random.split(key, 40))
    nrm = lambda shape, s: jax.random.normal(next(ks), shape, F32) * s
    gain = lambda shape: 1.0 + nrm(shape, 0.1)
    D = D_MODEL
    return {
        'x_prompt': nrm((BATCH, SEQ, D), 1.0),
        'x_sample': nrm((DEC_BATCH, DEC_SEQ, D), 1.0),
        'cache_win_k': nrm((DEC_BATCH, DEPTH, PAST_LEN, WIN_KV, HEAD_DIM), 1.0),
        'cache_win_v': nrm((DEC_BATCH, DEPTH, PAST_LEN, WIN_KV, HEAD_DIM), 1.0),
        'cache_na_k': nrm((DEC_BATCH, DEPTH, PAST_LEN, NA_HEADS, HEAD_DIM), 1.0),
        'cache_na_v': nrm((DEC_BATCH, DEPTH, PAST_LEN, NA_HEADS, HEAD_DIM), 1.0),
        'state_hgrn': nrm((DEC_BATCH, DEPTH, 2, HG_HEADS, HG_DK, HG_DV), 0.3),
        'c': nrm((DEC_BATCH, D), 1.0),
        'c_ctx': nrm((D,), 1.0),
        'w_mod': nrm((DEPTH, D, 6 * D), 0.5 * D ** -0.5),
        'b_mod': nrm((DEPTH, 6 * D), 0.02),
        'norm1_g': gain((DEPTH, D)),
        'norm2_g': gain((DEPTH, D)),
        'w_in': nrm((DEPTH, D, IN_COLS), D ** -0.5),
        'w_mgate': nrm((DEPTH, D, N_BRANCH * D), D ** -0.5),
        'b_mgate': nrm((DEPTH, N_BRANCH * D), 0.02),
        'hg_lb': nrm((DEPTH, 2, HG_W), 1.0),
        'hg_onorm': gain((DEPTH, HG_DV)),
        'win_qn': gain((DEPTH, HEAD_DIM)),
        'win_kn': gain((DEPTH, HEAD_DIM)),
        'win_sink': nrm((DEPTH, WIN_HEADS), 1.0),
        'pool_w': nrm((DEPTH, POOL_GROUPS, POOL_GC, POOL_GC), POOL_GC ** -0.5),
        'pool_scale': gain((DEPTH, POOL_W)),
        'na_qn': gain((DEPTH, HEAD_DIM)),
        'na_kn': gain((DEPTH, HEAD_DIM)),
        'na_rpb': nrm((DEPTH, NA_HEADS, 2 * NA_KH - 1, 2 * NA_KW - 1), 0.5),
        'w_branch': nrm((DEPTH, MIX_W, D), (MIX_W // N_BRANCH) ** -0.5),
        'w_out': nrm((DEPTH, D, D), D ** -0.5),
        'w_router': nrm((DEPTH, D, N_EXPERTS), D ** -0.5),
        'b_router': nrm((DEPTH, N_EXPERTS), 0.01),
        'w_eg': nrm((DEPTH, N_EXPERTS, D, D_EXPERT), D ** -0.5),
        'w_eu': nrm((DEPTH, N_EXPERTS, D, D_EXPERT), D ** -0.5),
        'w_ed': nrm((DEPTH, N_EXPERTS, D_EXPERT, D), D_EXPERT ** -0.5),
        'w_sg': nrm((DEPTH, D, D_SHARED), D ** -0.5),
        'w_su': nrm((DEPTH, D, D_SHARED), D ** -0.5),
        'w_sd': nrm((DEPTH, D_SHARED, D), D_SHARED ** -0.5),
    }

def reference(x_prompt, x_sample, cache_win_k, cache_win_v, cache_na_k, cache_na_v, state_hgrn,
              c, c_ctx, w_mod, b_mod, norm1_g, norm2_g, w_in, w_mgate, b_mgate, hg_lb, hg_onorm,
              win_qn, win_kn, win_sink, pool_w, pool_scale, na_qn, na_kn, na_rpb, w_branch, w_out,
              w_router, b_router, w_eg, w_eu, w_ed, w_sg, w_su, w_sd):
    lbp = jax.nn.softmax(hg_lb.astype(F32), axis=0)
    lbs = jnp.cumsum(lbp, axis=0) - lbp[0:1]
    y_p, y_s = x_prompt, x_sample
    ctx_out = []
    for l in range(DEPTH):
        lw = {
            'w_mod': w_mod[l], 'b_mod': b_mod[l], 'norm1_g': norm1_g[l], 'norm2_g': norm2_g[l],
            'w_in': w_in[l], 'w_mgate': w_mgate[l], 'b_mgate': b_mgate[l], 'hg_onorm': hg_onorm[l],
            'win_qn': win_qn[l], 'win_kn': win_kn[l], 'win_sink': win_sink[l],
            'pool_w': pool_w[l], 'pool_scale': pool_scale[l],
            'na_qn': na_qn[l], 'na_kn': na_kn[l], 'na_rpb': na_rpb[l],
            'w_branch': w_branch[l], 'w_out': w_out[l],
            'w_router': w_router[l], 'b_router': b_router[l],
            'w_eg': w_eg[l], 'w_eu': w_eu[l], 'w_ed': w_ed[l],
            'w_sg': w_sg[l], 'w_su': w_su[l], 'w_sd': w_sd[l],
        }
        y_p, outs = trunk_layer(y_p, c_ctx[None], lw, lbs[l], None)
        ctx_out.append(outs)
        y_s, _ = trunk_layer(y_s, c, lw, lbs[l],
                             (cache_win_k[:, l], cache_win_v[:, l], cache_na_k[:, l], cache_na_v[:, l],
                              state_hgrn[:, l]))
    new_win_k = jnp.stack([o[0] for o in ctx_out], axis=1)
    new_win_v = jnp.stack([o[1] for o in ctx_out], axis=1)
    new_na_k = jnp.stack([o[2] for o in ctx_out], axis=1)
    new_na_v = jnp.stack([o[3] for o in ctx_out], axis=1)
    new_hgrn = jnp.stack([o[4] for o in ctx_out], axis=1).astype(x_prompt.dtype)
    return (y_p, y_s, new_win_k, new_win_v, new_na_k, new_na_v, new_hgrn)


_drawn_inputs = setup_inputs


def setup_inputs(seed=0):
    import zlib

    import numpy as np

    out = dict(_drawn_inputs(seed))
    spreads = {}
    factors = {'state_hgrn': 4.034, 'b_mgate': 5.397, 'win_qn': 3.956, 'win_sink': 6.029, 'na_qn': 3.1}
    for name, (base, spread) in spreads.items():
        noise = np.random.default_rng([zlib.crc32(name.encode()), seed]).standard_normal(out[name].shape)
        drawn = base * np.exp(spread * noise) if base else spread * noise
        out[name] = __import__('jax').numpy.asarray(drawn.astype(out[name].dtype))
    for name, factor in factors.items():
        out[name] = (out[name] * factor).astype(out[name].dtype)
    return out
```

```python
import concourse.bass as bass
from concourse import mybir
from contextlib import ExitStack

F32 = mybir.dt.float32
ALU = mybir.AluOpType
ACT = mybir.ActivationFunctionType
AX = mybir.AxisListType

P = 128
D = 1024
KC = D // P
T = 384
NT = T // P
DEPTH = 2
HD = 64
SCALE = HD ** -0.5
EPS = 1e-6
NEG = -1e30
CH = 16
TC = P // CH
NCH = T // CH
NH = 10
NE = 32
DE = 256
TOPK = 4
ROUTED_SCALE = 2.5
SLOT = KC * 512
NSLOT = 4
NBANK = 4
PADU = 416
UPOS = (8, 152, 280)
NATW = 1664
SROW = 26

SM = {}
_at = 0
for _n, _w in (("g1", 8), ("g2", 8), ("bmod", 96), ("bmg", 32), ("onorm", 1), ("pscale", 2), ("brout", 32),
               ("wqn", 64), ("wkn", 64), ("nqn", 64), ("nkn", 64), ("sink", NH), ("lb", 8)):
    SM[_n] = (_at, _at + _w)
    _at += _w
SMW = _at
CN = {}
_at = 0
for _n, _w in (("ident", 128), ("onesD", 128), ("blk64", 128), ("mask0", 128), ("mask1", 128), ("chunk", TC),
               ("first", 2 * T), ("nmask", HD), ("wmask", 2 * T), ("cos", 2 * HD), ("sin", 2 * HD),
               ("inv", 2 * PADU), ("eps", 1)):
    CN[_n] = (_at, _at + _w)
    _at += _w
CNW = _at




class Cursor:

    def __init__(self, n):
        self.n, self.at = n, 0

    def next(self):
        i = self.at
        self.at = (i + 1) % self.n
        return i

    def restart(self):
        self.at = 0


def head_place(i):
    if i < 6:
        g = i // 3
        return i % 3, 3, 0, 64 * g, 768 + 64 * g, 64 * g, 2 + i // 2, 64 * (i % 2)
    h = i - 6
    return 4 + h // 2, 6 + h // 2, 1 + h // 2, 64 * (h % 2), 1408 + 64 * h, 128 + 64 * h, 7 + h // 2, 64 * (h % 2)


BRANCH_CHUNKS = ((0, 1), (2, 3, 4), (5, 6), (7, 8))

PROJ = [[(1, 0, 128), (1, 128, 128), (1, 256, 128), (1, 384, 128)],
        [(1, 512, 128), (1, 640, 128), (0, 768, 256)],
        [(1, 1024, 128), (1, 1152, 128), (0, 1280, 256)],
        [(0, 1536, 384), (1, 1920, 128)],
        [(1, 2048, 128), (0, 2176, 384)],
        [(0, 2560, 384)]]


def nat_col(c):
    if c < 1024:
        return c - 768
    return c - 1280 + 256 if c < 1920 else c - 2176 + 896


def build(nc, A, O):
    ctx = ExitStack()
    with ctx:
        def sb(name, shape):
            return ctx.enter_context(nc.sbuf_tensor(name, shape, F32))

        def sem(name):
            return ctx.enter_context(nc.semaphore(name))

        slots = [sb(f"slot{i}", [P, SLOT]) for i in range(NSLOT)]
        xT = sb("xT", [P, KC, T])
        hT = sb("hT", [P, KC, T])
        nat = sb("nat", [P, NT, NATW])
        qT = sb("qT", [P, 2, T])
        sig = [sb("sigF", [P, 2, T]), sb("sigB", [P, 2, T])]
        gT = sb("gT", [P, 2, T])
        uT = sb("uT", [P, 2, PADU])
        yT = sb("yT", [P, 9, T])
        con = sb("con", [P, CNW])
        sm = sb("sm", [P, SMW])
        kcT = sb("kcT", [P, 3, P])
        vc = sb("vc", [P, T])
        s0 = sb("s0", [P, 4, HD])
        fin = sb("fin", [P, 4, HD])
        poolw = sb("poolw", [P, 2, HD])
        wr = sb("wr", [P, KC, NE])
        cT = sb("cT", [P, KC, 2])
        scT = sb("scT", [P, KC, 2])
        mT = sb("mT", [P, 6, KC, 2])
        modA = sb("modA", [P, 2, KC, 2])
        rstd = sb("rstd", [P, T])
        lb = sb("lb", [P, DEPTH, 4])
        lbw = sb("lbw", [P, 8, 4])
        lbl = sb("lbl", [P, 2, 4])
        small = sb("small", [P, 64])
        sbig = sb("softmax_small", [P, 64])
        sc = sb("sc", [P, NT, NE])
        sbr = sb("sbr", [P, NT, NE + TOPK])
        rep = sb("rep", [P, NT, NE + TOPK])
        top8 = sb("top8", [P, NT, 8])
        gate = sb("gate", [P, NT, NE])
        arena = sb("arena", [P, 11600])
        used = [0]

        def new_phase():
            used[0] = 0

        def ar(*shape):
            n = 1
            for s in shape:
                n *= s
            a = arena[:, used[0]:used[0] + n]
            used[0] += n
            assert used[0] <= 11600, used[0]
            if len(shape) == 2:
                return a.rearrange("p (a b) -> p a b", b=shape[1])
            if len(shape) == 3:
                return a.rearrange("p (a b c) -> p a b c", b=shape[1], c=shape[2])
            return a

        QE, KE, QX, L, C, DD = (ar(2, T) for _ in range(6))
        S = ar(2, SROW, HD)
        kdN = ar(NT, 256)
        VX = ar(4, TC * HD)
        attS = VX[:, 0, :].rearrange("p (a b) -> p a b", b=P)
        oT = ar(2, T)
        new_phase()
        s2, s4, s8, s16, pl = (ar(2, PADU) for _ in range(5))
        new_phase()
        qkr = ar(NT, 512)
        qkT = ar(8, T)
        biasD = ar(8, T)
        sP = [ar(896), ar(896)]
        pT = [ar(7, P), ar(7, P)]
        raw = arena[:, 3584 + 3072 + 1024:3584 + 3072 + 1024 + 2048]
        raw = arena[:, used[0] - 3584:used[0] - 3584 + 2048].rearrange("p (a b) -> p a b", b=256)
        tmp = arena[:, used[0] - 1536:used[0]]
        new_phase()
        merged = ar(KC, T)
        gb = [ar(T), ar(T)]
        mt = ar(T)
        new_phase()
        sq = ar(KC, T)
        new_phase()
        si = [ar(DE), ar(DE)]
        aa = [ar(DE), ar(DE)]
        aT = [ar(2, P), ar(2, P)]
        acc = nat[:, :, 0:D]

        vb = [ctx.enter_context(nc.psum_tensor(f"vb{i}", [P, 512], F32)) for i in range(NBANK)]
        ab = [ctx.enter_context(nc.psum_tensor(f"ab{i}", [P, 512], F32)) for i in range(NBANK)]

        def c_(name):
            return con[:, CN[name][0]:CN[name][1]]

        def s_(name):
            return sm[:, SM[name][0]:SM[name][1]]

        ident = c_("ident")

        vfull = [sem(f"vfull{i}") for i in range(NBANK)]
        vfree = [sem(f"vfree{i}") for i in range(NBANK)]
        afull = [sem(f"afull{i}") for i in range(NBANK)]
        afree = [sem(f"afree{i}") for i in range(NBANK)]
        loaded = [sem(f"slot_loaded{i}") for i in range(NSLOT)]
        freed = [sem(f"slot_freed{i}") for i in range(NSLOT)]
        start_in = sem("start_in")
        params_in = sem("params_in")
        layer_done = sem("layer_done")
        silu_c_ready = sem("silu_c_ready")
        c_loaded = sem("c_loaded")
        x_ready = sem("x_ready")
        sq_ready = sem("sq_ready")
        h_ready = sem("h_ready")
        root_wanted = sem("root_wanted")
        root_ready = sem("root_ready")
        gates_in = sem("recurrence_inputs_evacuated")
        proj_done = sem("projection_evacuated")
        vproj_done = sem("values_evacuated")
        f_ready = sem("f_ready")
        logf_ready = sem("logf_ready")
        exps_wanted = sem("exps_wanted")
        exps_ready = sem("exps_ready")
        rec_ready = sem("rec_operands_ready")
        kdn_ready = sem("kdn_ready")
        vx_ready = sem("vx_ready")
        att_ready = sem("att_ready")
        states_ready = sem("states_ready")
        fin_ready = sem("fin_ready")
        fin_stored = sem("fin_stored")
        o_ready = sem("o_ready")
        osq_ready = sem("osq_ready")
        pooled_ready = sem("pooled_ready")
        kv_ready = sem("kv_ready")
        kv_stored = sem("kv_stored")
        bias_wanted = sem("bias_wanted")
        bias_in = sem("bias_in")
        qk_ready = sem("qk_ready")
        qkt_ready = sem("qkt_ready")
        exp_wanted = sem("exp_wanted")
        exp_ready = sem("exp_ready")
        p_ready = sem("p_ready")
        pt_ready = sem("pt_ready")
        s_free = sem("s_free")
        yv_ready = sem("y_from_vector_ready")
        ya_ready = sem("y_from_scalar_ready")
        gb_ready = sem("gb_ready")
        gb_free = sem("gb_free")
        merged_ready = sem("merged_ready")
        sc_ready = sem("sc_ready")
        hid_full = [sem("hid_full0"), sem("hid_full1")]
        si_ready = sem("si_ready")
        a_ready = sem("a_ready")
        at_ready = sem("at_ready")
        acc_ready = sem("acc_ready")
        y_ready = sem("y_ready")
        y_stored = sem("y_stored")

        block = ctx.enter_context(nc.Block())

        @block.sync
        def _(sp):
            sp.dma_start(con[:, :], A["con"]).then_inc(start_in, 16)
            sp.dma_start(cT[:, :, :], A["cT"]).then_inc(c_loaded, 16)
            sp.dma_start(xT[:, :, :], A["xT"]).then_inc(start_in, 16)
            cur = Cursor(NSLOT)

            def load(parts):
                s = cur.next()
                sp.wait_ge(freed[s], 1).then_inc(freed[s], -1)
                for dst, src in parts(slots[s]):
                    sp.dma_start(dst, src).then_inc(loaded[s], 32 // len(parts(slots[s])))

            with sp.Fori(0, DEPTH) as l:
                cur.restart()

                def layer(name):
                    return A[name][bass.ds(l, 1)].rearrange("l a b -> (l a) b")

                for b in range(12):
                    load(lambda s: [(s[:, :].rearrange("p (c n) -> p c n", c=KC),
                                     layer("w_mod").rearrange("(p c) n -> p c n", c=KC)[:, :, 512 * b:512 * b + 512])])
                    if b == NSLOT - 1:
                        sp.wait_ge(layer_done, 1).then_inc(layer_done, -1)
                        for dst, name in ((sm[:, :], "sm"), (kcT[:, :, :].rearrange("p a b -> p (a b)"), "kcT"),
                                          (vc[:, :], "vc"), (s0[:, :, :].rearrange("p a b -> p (a b)"), "s0"),
                                          (poolw[:, :, :].rearrange("p a b -> p (a b)"), "poolw")):
                            sp.dma_start(dst, A[name][bass.ds(l, 1)].rearrange("l p n -> (l p) n"))\
                                .then_inc(params_in, 16)
                        sp.dma_start(wr[:, :, :], A["w_router"][bass.ds(l, 1)].rearrange("l (p c) n -> (l p) c n", c=KC))\
                            .then_inc(params_in, 16)
                for b in range(6):
                    w = min(512, 2944 - 512 * b)
                    load(lambda s: [(s[:, 0:KC * w].rearrange("p (c n) -> p c n", c=KC),
                                     layer("w_in").rearrange("(p c) n -> p c n", c=KC)[:, :, 512 * b:512 * b + w])])
                for nb in range(4):
                    load(lambda s: [(s[:, 0:9 * 256].rearrange("p (c n) -> p c n", c=9),
                                     layer("w_branch").rearrange("(c p) n -> p c n", c=9)[:, :, 256 * nb:256 * nb + 256])])
                    for half in range(2):
                        load(lambda s: [(s[:, 2048 * k:2048 * (k + 1)].rearrange("p (c n) -> p c n", c=KC),
                                         layer("w_mgate").rearrange("(p c) n -> p c n", c=KC)[
                                             :, :, D * (2 * half + k) + 256 * nb:D * (2 * half + k) + 256 * nb + 256])
                                        for k in range(2)])
                for half in range(2):
                    load(lambda s: [(s[:, :].rearrange("p (c n) -> p c n", c=4),
                                     layer("w_out")[512 * half:512 * half + 512, :].rearrange("(c p) n -> p c n", c=4))])
                load(lambda s: [(s[:, :].rearrange("p (c n) -> p c n", c=KC)[:, :, DE * k:DE * k + DE],
                                 layer(w).rearrange("(p c) n -> p c n", c=KC)) for k, w in enumerate(("w_sg", "w_su"))])
                load(lambda s: [(s[:, 0:2048].rearrange("p (c n) -> p c n", c=2),
                                 layer("w_sd").rearrange("(c p) n -> p c n", c=2))])
                with sp.Fori(0, NE // 2) as j:
                    for k in range(2):
                        def expert(name):
                            return A[name][bass.ds(l * NE + 2 * j + k, 1)].rearrange("l a b -> (l a) b")

                        load(lambda s: [(s[:, :].rearrange("p (c n) -> p c n", c=KC)[:, :, DE * i:DE * i + DE],
                                         expert(w).rearrange("(p c) n -> p c n", c=KC))
                                        for i, w in enumerate(("w_eg", "w_eu"))])
                        load(lambda s: [(s[:, 0:2048].rearrange("p (c n) -> p c n", c=2),
                                         expert("w_ed").rearrange("(c p) n -> p c n", c=2))])
            sp.wait_ge(y_ready, 1).then_inc(y_ready, -1)
            sp.dma_start(O["yT"], xT[:, :, :]).then_inc(y_stored, 16)
            sp.wait_ge(y_stored, 16)

        @block.tensor
        def _(pe):
            v, a, sl = Cursor(NBANK), Cursor(NBANK), Cursor(NSLOT)
            release = []

            def mm(out, lhsT, rhs, start, stop):
                i = nc.tensor.matmul(out, lhsT, rhs, start=start, stop=stop, skip_group_check=True)
                if release:
                    i.then_inc(freed[release.pop(0)], 1)
                return i

            def group(ring, body):
                b = ring.next()
                banks, full, free = (vb, vfull, vfree) if ring is v else (ab, afull, afree)
                pe.wait_ge(free[b], 1).then_inc(free[b], -1)
                last = body(banks[b])
                last.then_inc(full[b], 1)

            def slot():
                s = sl.next()
                pe.wait_ge(loaded[s], 32).then_inc(loaded[s], -32)
                return s, slots[s]

            def flush():
                while release:
                    pe.drain().then_inc(freed[release.pop(0)], 1)

            def run(out, pairs):
                for k, (x, y) in enumerate(pairs):
                    last = mm(out, x, y, k == 0, k == len(pairs) - 1)
                return last

            def trans(bank, blocks):
                for k, x in enumerate(blocks):
                    last = nc.tensor.transpose(bank[:, P * k:P * k + P], x, ident)
                return last

            def norm():
                pe.wait_ge(sq_ready, 1).then_inc(sq_ready, -1)
                group(a, lambda o: run(o[:, 0:T], [(c_("onesD"), sq[:, c, :]) for c in range(KC)]))
                pe.wait_ge(h_ready, 1).then_inc(h_ready, -1)

            def wview(w, c=KC):
                return w[:, 0:c * (SLOT // c)].rearrange("p (c n) -> p c n", c=c)

            def job_g(k, w, t):
                b = k % 2
                pe.wait_ge(vfree[b], 1).then_inc(vfree[b], -1)
                run(vb[b][:, :], [(hT[:, c, P * t:P * t + P], wview(w)[:, c, :]) for c in range(KC)])\
                    .then_inc(hid_full[b], 1)

            def job_d(j, w):
                pe.wait_ge(a_ready, 1).then_inc(a_ready, -1)
                group(a, lambda o: trans(o, [aa[j % 2][:, P * f:P * f + P] for f in range(2)]))
                pe.wait_ge(at_ready, 1).then_inc(at_ready, -1)
                wd = w[:, 0:2048].rearrange("p (c n) -> p c n", c=2)
                for n in range(2):
                    pe.wait_ge(vfree[2 + n], 1).then_inc(vfree[2 + n], -1)
                    run(vb[2 + n][:, :], [(aT[j % 2][:, f, :], wd[:, f, 512 * n:512 * n + 512]) for f in range(2)])\
                        .then_inc(vfull[2 + n], 1)

            def experts(n):
                pend = None
                k = 0
                for _ in range(n):
                    sg, wg = slot()
                    sd = None
                    for t in range(NT):
                        job_g(k, wg, t)
                        if t == NT - 1:
                            release.append(sg)
                        if pend is not None:
                            job_d(*pend[:2])
                            if pend[2] is not None:
                                release.append(pend[2])
                        if sd is None:
                            sd, wdn = slot()
                        pend = (k, wdn, sd if t == NT - 1 else None)
                        k += 1
                job_d(*pend[:2])
                release.append(pend[2])
                flush()

            for s in range(NSLOT):
                pe.sem_inc(freed[s], 1)
            pe.wait_ge(silu_c_ready, 1).then_inc(silu_c_ready, -1)
            with pe.Fori(0, DEPTH):
                v.restart(), a.restart(), sl.restart()

                def modulation(o):
                    for b in range(12):
                        s, w = slot()
                        for n in range(4):
                            last = run(o[:, 8 * b + 2 * n:8 * b + 2 * n + 2],
                                       [(wview(w)[:, c, P * n:P * n + P], scT[:, c, :]) for c in range(KC)])
                        release.append(s)
                    return last
                group(v, modulation)
                norm()
                for b, groups in enumerate(PROJ):
                    s, w = slot()
                    width = min(512, 2944 - 512 * b)
                    wv = w[:, 0:KC * width].rearrange("p (c n) -> p c n", c=KC)
                    for tr, c0, n in groups:
                        o0 = c0 - 512 * b
                        if tr:
                            ring = v if c0 in (1920, 2048) else a
                            group(ring, lambda o: run(o[:, 0:T], [(wv[:, c, o0:o0 + n], hT[:, c, :]) for c in range(KC)]))
                        else:
                            ring = v if c0 == 768 else a
                            for t in range(NT):
                                group(ring, lambda o: run(o[:, 0:n], [(hT[:, c, P * t:P * t + P], wv[:, c, o0:o0 + n])
                                                                      for c in range(KC)]))
                    release.append(s)
                flush()
                pe.wait_ge(vproj_done, 1).then_inc(vproj_done, -1)
                for r in range(2):
                    pe.wait_ge(rec_ready, 1).then_inc(rec_ready, -1)
                    for t in range(NT):
                        group(v, lambda o: trans(o, [L[:, pr, P * t:P * t + P] for pr in range(2)]))
                    pe.wait_ge(kdn_ready, 1).then_inc(kdn_ready, -1)
                    for t in ((0, 1, 2), (0, 2, 1))[r]:
                        pe.wait_ge(vx_ready, 1).then_inc(vx_ready, -1)
                        for pr in range(2):
                            def ds(o):
                                for h2 in range(2):
                                    h = 2 * pr + h2
                                    last = mm(o[64 * h2:64 * h2 + 64, :], kdN[:, t, 64 * h:64 * h + 64], VX[:, h, :],
                                              True, True)
                                return last
                            group(v, ds)
                    pe.wait_ge(states_ready, 1).then_inc(states_ready, -1)
                    for t in range(NT):
                        for h2 in range(2):
                            def att(o):
                                for pr in range(2):
                                    last = mm(o[:, P * pr:P * pr + P], KE[64 * h2:64 * h2 + 64, pr, P * t:P * t + P],
                                              QE[64 * h2:64 * h2 + 64, pr, P * t:P * t + P], True, True)
                                return last
                            group(v, att)
                        pe.wait_ge(att_ready, 1).then_inc(att_ready, -1)

                        def out(o):
                            for pr in range(2):
                                for h2 in range(2):
                                    q = slice(64 * h2, 64 * h2 + 64)
                                    h = 2 * pr + h2
                                    mm(o[q, P * pr:P * pr + P], nat[:, t, 64 * h:64 * h + 64], attS[:, h, :], True, False)
                                    for c in range(TC):
                                        n0 = P * t + CH * c
                                        row = TC * t + c + (t > 0) + r
                                        last = mm(o[q, P * pr + CH * c:P * pr + CH * c + CH], S[q, pr, row, :],
                                                  QX[q, pr, n0:n0 + CH], False, c == TC - 1)
                            return last
                        group(v, out)
                pe.wait_ge(osq_ready, 1).then_inc(osq_ready, -1)
                for pr in range(2):
                    group(a, lambda o: run(o[:, 0:T], [(c_("blk64"), DD[:, pr, :])]))
                pe.wait_ge(pooled_ready, 1).then_inc(pooled_ready, -1)
                for k in range(2):
                    def pmap(o):
                        for h2 in range(2):
                            q = slice(64 * h2, 64 * h2 + 64)
                            mm(o[q, 0:P], poolw[q, k, :], pl[q, k, 8:8 + P], True, True)
                            last = mm(o[q, P:T], poolw[q, k, :], pl[q, k, 152:152 + 256], True, True)
                        return last
                    group(v, pmap)
                pe.wait_ge(qk_ready, 1).then_inc(qk_ready, -1)
                for t in range(NT):
                    group(a, lambda o: trans(o, [qkr[:, t, P * j:P * j + P] for j in range(4)]))
                    group(a, lambda o: trans(o, [nat[:, t, 896 + P * j:896 + P * j + P] for j in range(4)]))
                pe.wait_ge(qkt_ready, 1).then_inc(qkt_ready, -1)

                def scores(i):
                    qc, kc, cc, p0 = head_place(i)[:4]
                    q = slice(p0, p0 + 64)
                    group(v, lambda o: mm(o[:, 0:P], qkT[q, qc, 0:P], qkT[q, kc, 0:P], True, True))
                    for t in (1, 2):
                        def s(o):
                            mm(o[:, 0:256], qkT[q, qc, P * t:P * t + P], qkT[q, kc, P:T], True, True)
                            return mm(o[:, 256:T], qkT[q, qc, P * t:P * t + P], kcT[q, cc, :], True, True)
                        group(v, s)

                scores(0)
                for i in range(NH):
                    if i + 1 < NH:
                        scores(i + 1)
                    vcol, ccol, _, op = head_place(i)[4:]
                    pe.wait_ge(p_ready, 1).then_inc(p_ready, -1)
                    group(a, lambda o: trans(o, [sP[i % 2][:, P * k:P * k + P] for k in range(4)]))
                    group(a, lambda o: trans(o, [sP[i % 2][:, P * k:P * k + P] for k in range(4, 7)]))
                    pe.wait_ge(pt_ready, 1).then_inc(pt_ready, -1)

                    def pv(o):
                        q = slice(op, op + 64)
                        mm(o[q, 0:P], nat[:, 0, vcol:vcol + 64], pT[i % 2][:, 0, :], True, True)
                        for t in (1, 2):
                            k0 = 1 + 3 * (t - 1)
                            last = run(o[q, P * t:P * t + P],
                                       [(nat[:, 1, vcol:vcol + 64], pT[i % 2][:, k0, :]),
                                        (nat[:, 2, vcol:vcol + 64], pT[i % 2][:, k0 + 1, :]),
                                        (vc[:, ccol:ccol + 64], pT[i % 2][:, k0 + 2, :])])
                        return last
                    group(a, pv)
                pe.wait_ge(yv_ready, 1).then_inc(yv_ready, -1)
                pe.wait_ge(ya_ready, 1).then_inc(ya_ready, -1)
                for nb in range(4):
                    sb_, wb = slot()
                    wbv = wb[:, 0:9 * 256].rearrange("p (c n) -> p c n", c=9)
                    for half in range(2):
                        s, w = slot()
                        for k in range(2):
                            wm = w[:, 2048 * k:2048 * (k + 1)].rearrange("p (c n) -> p c n", c=KC)
                            for n in range(2):
                                group(a, lambda o: run(o[:, 0:T], [(wm[:, c, P * n:P * n + P], hT[:, c, :])
                                                                   for c in range(KC)]))
                                group(v, lambda o: run(o[:, 0:T], [(wbv[:, y, P * n:P * n + P], yT[:, y, :])
                                                                   for y in BRANCH_CHUNKS[2 * half + k]]))
                        release.append(s)
                    release.append(sb_)
                    flush()
                pe.wait_ge(merged_ready, 1).then_inc(merged_ready, -1)
                wo = [slot(), slot()]
                for c in range(KC):
                    group(v, lambda o: run(o[:, 0:T], [(wview(wo[k // 4][1], 4)[:, k % 4, c:D:KC], merged[:, k, :])
                                                       for k in range(KC)]))
                release.extend([wo[0][0], wo[1][0]])
                flush()
                norm()
                def router(o):
                    for t in range(NT):
                        last = run(o[:, NE * t:NE * t + NE], [(hT[:, c, P * t:P * t + P], wr[:, c, :]) for c in range(KC)])
                    return last
                group(a, router)
                v.restart(), a.restart()
                experts(1)
                with pe.Fori(0, NE // 2):
                    v.restart(), a.restart()
                    experts(2)
                pe.wait_ge(acc_ready, 1).then_inc(acc_ready, -1)
                v.restart()
                for c in range(KC):
                    group(v, lambda o: trans(o, [acc[:, t, c:D:KC] for t in range(NT)]))

        @block.scalar
        def _(act):
            a = Cursor(NBANK)
            f = nc.scalar.activation

            def empty(body):
                b = a.next()
                act.wait_ge(afull[b], 1).then_inc(afull[b], -1)
                body(ab[b]).then_inc(afree[b], 1)

            def tell(s):
                act.drain().then_inc(s, 1)

            for b in range(NBANK):
                act.sem_inc(afree[b], 1)
            act.wait_ge(c_loaded, 16).then_inc(c_loaded, -16)
            f(scT[:, :, :], cT[:, :, :], ACT.Silu).then_inc(silu_c_ready, 1)
            with act.Fori(0, DEPTH) as l:
                a.restart()
                act.wait_ge(f_ready, 1).then_inc(f_ready, -1)
                f(lbw[:, 1:3, :], lbw[:, 1:3, :], ACT.Exp).then_inc(logf_ready, 1)

                def square():
                    act.wait_ge(x_ready, 1).then_inc(x_ready, -1)
                    f(sq[:, :, :], xT[:, :, :], ACT.Square).then_inc(sq_ready, 1)
                    empty(lambda o: f(rstd[:, :], o[:, 0:T], ACT.Sqrt, bias=c_("eps")))
                    tell(root_ready)

                square()
                for dst, fn in ((qT, ACT.Copy), (sig[0], ACT.Sigmoid), (sig[1], ACT.Sigmoid)):
                    for pr in range(2):
                        empty(lambda o: f(dst[:, pr, :], o[:, 0:T], fn))
                tell(gates_in)
                for pr in range(2):
                    empty(lambda o: f(gT[:, pr, :], o[:, 0:T], ACT.Silu))
                for c0, n in ((1280, 256), (1536, 384), (2176, 384), (2560, 384)):
                    for t in range(NT):
                        empty(lambda o: f(nat[:, t, nat_col(c0):nat_col(c0) + n], o[:, 0:n], ACT.Copy))
                tell(proj_done)
                for r in range(2):
                    act.wait_ge(f_ready, 1).then_inc(f_ready, -1)
                    f(L, sig[r][:, :, :], ACT.Ln).then_inc(logf_ready, 1)
                    act.wait_ge(exps_wanted, 1).then_inc(exps_wanted, -1)
                    f(QE, DD, ACT.Exp)
                    f(KE, DD, ACT.Exp, scale=-1.0)
                    f(QX, C, ACT.Exp)
                    f(L, L, ACT.Exp)
                    f(small[:, 0:48], small[:, 0:48], ACT.Exp)
                    tell(exps_ready)
                act.wait_ge(fin_ready, 1).then_inc(fin_ready, -1)
                act.wait_ge(o_ready, 1).then_inc(o_ready, -1)
                f(DD, oT, ACT.Square).then_inc(osq_ready, 1)
                for pr in range(2):
                    empty(lambda o: f(QE[:, pr, :], o[:, 0:T], ACT.Sqrt, bias=c_("eps")))
                tell(root_ready)
                act.dma_start(O["fin"][bass.ds(l, 1)].rearrange("l p n -> (l p) n"),
                              fin[:, :, :].rearrange("p a b -> p (a b)")).then_inc(fin_stored, 16)
                act.wait_ge(bias_wanted, 1).then_inc(bias_wanted, -1)
                for h in range(4):
                    for t in range(2):
                        for r2 in range(2):
                            src = A["rpb"][bass.ds(l, 1), h, :]
                            ap = bass.AP(tensor=src.tensor, offset=src.offset + (4 + 2 * t + r2) * 31 - 48,
                                         ap=[[1, 64], [31, 4], [1, 64]])
                            act.dma_start(raw[64 * r2:64 * r2 + 64, 2 * h + t, :].rearrange("p (a b) -> p a b", b=64), ap)\
                                .then_inc(bias_in, 16)
                for _ in range(2):
                    act.wait_ge(root_wanted, 1).then_inc(root_wanted, -1)
                    f(small[:, 24:48], small[:, 0:24], ACT.Sqrt, bias=c_("eps"), scale=1.0 / HD).then_inc(root_ready, 1)
                act.wait_ge(kv_ready, 1).then_inc(kv_ready, -1)
                for name, c0, w in (("wk", 640, 128), ("wv", 768, 128), ("nk", 1152, 256), ("nv", 1408, 256)):
                    act.dma_start(O[name][bass.ds(l, 1)].rearrange("l p n -> (l p) n"), nat[:, 0, c0:c0 + w])\
                        .then_inc(kv_stored, 16)
                for t in range(NT):
                    for k in range(2):
                        empty(lambda o: f(qkT[:, 4 * k:4 * k + 4, P * t:P * t + P],
                                          o[:, :].rearrange("p (a b) -> p a b", b=P), ACT.Copy))
                tell(qkt_ready)

                def exps(i):
                    act.wait_ge(exp_wanted, 1).then_inc(exp_wanted, -1)
                    s, k = sP[i % 2], 8 * (i % 2)
                    for t, (c0, n) in enumerate(((0, P), (P, T), (P + T, T))):
                        f(s[:, c0:c0 + n], s[:, c0:c0 + n], ACT.Exp, bias=sbig[:, k + t:k + t + 1],
                          accum_out=sbig[:, 16 + k + t:16 + k + t + 1])
                    f(sbig[:, 32 + k:32 + k + 3], sbig[:, k:k + 3], ACT.Exp, bias=s_("sink")[:, i:i + 1])
                    tell(exp_ready)

                exps(0)
                for i in range(NH):
                    if i + 1 < NH:
                        exps(i + 1)
                    empty(lambda o: f(pT[i % 2][:, 0:4, :], o[:, :].rearrange("p (a b) -> p a b", b=P), ACT.Copy))
                    empty(lambda o: f(pT[i % 2][:, 4:7, :], o[:, 0:T].rearrange("p (a b) -> p a b", b=P), ACT.Copy))
                    tell(pt_ready)
                    tell(s_free)
                    yc, op = head_place(i)[6:]
                    empty(lambda o: f(yT[op:op + 64, yc, :], o[op:op + 64, 0:T], ACT.Copy))
                tell(ya_ready)
                k = 0
                for nb in range(4):
                    for b in range(4):
                        for n in range(2):
                            act.wait_ge(gb_free, 1).then_inc(gb_free, -1)
                            col = b * KC + 2 * nb + n
                            empty(lambda o: f(gb[k % 2], o[:, 0:T], ACT.Sigmoid, bias=s_("bmg")[:, col:col + 1]))
                            tell(gb_ready)
                            k += 1
                square()
                empty(lambda o: f(sc[:, :, :], o[:, 0:NT * NE].rearrange("p (a b) -> p a b", b=NE), ACT.Sigmoid))
                tell(sc_ready)
                a.restart()

                def silus(j):
                    act.wait_ge(hid_full[j % 2], 1).then_inc(hid_full[j % 2], -1)
                    f(si[j % 2], vb[j % 2][:, 0:DE], ACT.Silu).then_inc(si_ready, 1)

                def transposed(j):
                    empty(lambda o: f(aT[j % 2], o[:, 0:DE].rearrange("p (a b) -> p a b", b=P), ACT.Copy))
                    tell(at_ready)

                def experts(n):
                    for j in range(NT * n + 1):
                        if j < NT * n:
                            silus(j)
                        if j > 0:
                            transposed(j - 1)

                experts(1)
                with act.Fori(0, NE // 2):
                    a.restart()
                    experts(2)

        @block.vector
        def _(dve):
            v = Cursor(NBANK)
            vec = nc.vector

            def settle():
                dve.drain()

            def tell(s):
                dve.drain().then_inc(s, 1)

            def empty(body):
                b = v.next()
                dve.wait_ge(vfull[b], 1).then_inc(vfull[b], -1)
                body(vb[b]).then_inc(vfree[b], 1)

            for b in range(NBANK):
                dve.sem_inc(vfree[b], 1)
            dve.sem_inc(layer_done, 1)
            dve.sem_inc(fin_stored, 16)
            for b in range(2):
                dve.sem_inc(gb_free, 1)
            vec.memset(uT[:, :, :], 0.0)
            vec.memset(sbr[:, :, :], NEG)
            dve.wait_ge(start_in, 32).then_inc(start_in, -32)
            tell(x_ready)
            with dve.Fori(0, DEPTH) as l:
                v.restart()
                dve.wait_ge(params_in, 96).then_inc(params_in, -96)
                lbr = s_("lb").rearrange("p (a b) -> p a b", b=4)
                mx, e0, e1, su, c1, lbv = (lbw[:, k, :] for k in range(6))
                vec.tensor_tensor(mx, lbr[:, 0, :], lbr[:, 1, :], ALU.max)
                settle()
                vec.tensor_tensor(e0, lbr[:, 0, :], mx, ALU.subtract)
                vec.tensor_tensor(e1, lbr[:, 1, :], mx, ALU.subtract)
                tell(f_ready)
                dve.wait_ge(logf_ready, 1).then_inc(logf_ready, -1)
                vec.tensor_tensor(su, lbw[:, 1, :], lbw[:, 2, :], ALU.add)
                settle()
                vec.reciprocal(c1, su)
                settle()
                vec.tensor_tensor(e0, e0, c1, ALU.mult)
                vec.tensor_tensor(e1, e1, c1, ALU.mult)
                settle()
                vec.tensor_tensor(su, e0, e1, ALU.add)
                settle()
                vec.tensor_tensor(lb[:, 1, :], su, e0, ALU.subtract)
                vec.tensor_tensor(lb[:, 0, :], e0, e0, ALU.subtract)
                settle()
                vec.tensor_copy(lbl[:, 0, :], lb[:, bass.ds(l, 1), :].rearrange("p a b -> p (a b)"))
                settle()
                vec.tensor_scalar(lbl[:, 1, :], lbl[:, 0, :], -1.0, 1.0, ALU.mult, ALU.add)
                empty(lambda o: vec.tensor_tensor(mT[:, :, :, :].rearrange("p a b c -> p (a b c)"), o[:, 0:96],
                                                  s_("bmod"), ALU.add))
                settle()
                for k, (g, s) in enumerate((("g1", 1), ("g2", 4))):
                    vec.scalar_tensor_tensor(modA[:, k, :, :], mT[:, s, :, :], 1.0,
                                             s_(g).unsqueeze(2).to_broadcast([P, KC, 2]), ALU.add, ALU.mult)

                def norm(k):
                    dve.wait_ge(root_ready, 1).then_inc(root_ready, -1)
                    vec.reciprocal(rstd[:, :], rstd[:, :])
                    settle()
                    vec.tensor_tensor(hT[:, :, :], xT[:, :, :], rstd[:, :].unsqueeze(1).to_broadcast([P, KC, T]), ALU.mult)
                    settle()
                    for c in range(KC):
                        for g, (t0, t1) in enumerate(((0, P), (P, T))):
                            vec.tensor_scalar(hT[:, c, t0:t1], hT[:, c, t0:t1], modA[:, k, c, g:g + 1],
                                              mT[:, 3 * k, c, g:g + 1], ALU.mult, ALU.add)
                    tell(h_ready)

                norm(0)
                for t in range(NT):
                    empty(lambda o: vec.tensor_copy(nat[:, t, 0:256], o[:, 0:256]))
                tell(vproj_done)
                for k in range(2):
                    def padded(o):
                        vec.tensor_copy(uT[:, k, 8:8 + P], o[:, 0:P])
                        return vec.tensor_copy(uT[:, k, 152:152 + 256], o[:, P:T])
                    empty(padded)
                dve.wait_ge(gates_in, 1).then_inc(gates_in, -1)
                chunked = lambda x: x.rearrange("p a (c n) -> p (a c) n", n=CH)
                flat = lambda x: x.rearrange("p a n -> p (a n)")
                tot = small[:, 0:48]
                for r in range(2):
                    for pr in range(2):
                        vec.tensor_scalar(sig[r][:, pr, :], sig[r][:, pr, :], lbl[:, 1, 2 * r + pr:2 * r + pr + 1],
                                          lbl[:, 0, 2 * r + pr:2 * r + pr + 1], ALU.mult, ALU.add)
                    tell(f_ready)
                    dve.wait_ge(logf_ready, 1).then_inc(logf_ready, -1)
                    vec.tensor_scalar(sig[r][:, :, :], sig[r][:, :, :], -1.0, 1.0, ALU.mult, ALU.add)
                    vec.tensor_tensor_scan(flat(C), c_("first"), flat(L), 0.0, ALU.mult, ALU.add)
                    settle()
                    vec.tensor_copy(tot, chunked(C)[:, :, CH - 1])
                    settle()
                    totb = tot.unsqueeze(2).to_broadcast([P, 2 * NCH, CH])
                    if r == 1:
                        vec.tensor_tensor(C, L, C, ALU.subtract)
                        settle()
                        vec.tensor_tensor(chunked(C), chunked(C), totb, ALU.add)
                        settle()
                    mid = CH // 2 - 1 + r
                    vec.tensor_tensor(chunked(DD), chunked(C), chunked(C)[:, :, mid:mid + 1].to_broadcast([P, 2 * NCH, CH]),
                                      ALU.subtract)
                    vec.tensor_tensor(chunked(L), totb, chunked(C), ALU.subtract)
                    settle()
                    vec.tensor_scalar(DD, DD, 80.0, -80.0, ALU.min, ALU.max)
                    tell(exps_wanted)
                    dve.wait_ge(exps_ready, 1).then_inc(exps_ready, -1)
                    vec.tensor_tensor(L, L, sig[r][:, :, :], ALU.mult)
                    vec.tensor_tensor(QE, QE, qT[:, :, :], ALU.mult)
                    vec.tensor_tensor(KE, KE, sig[r][:, :, :], ALU.mult)
                    vec.tensor_tensor(QX, QX, qT[:, :, :], ALU.mult)
                    tell(rec_ready)
                    for t in range(NT):
                        empty(lambda o: vec.tensor_copy(kdN[:, t, :], o[:, 0:256]))
                    tell(kdn_ready)
                    for base, n, src in ((0, 8, None), (9, 16, s0)):
                        row = base + (n if r else 0)
                        if src is None:
                            vec.memset(S[:, :, row, :], 0.0)
                        else:
                            vec.tensor_copy(S[:, :, row, :], s0[:, 2 * r:2 * r + 2, :])
                    for t in ((0, 1, 2), (0, 2, 1))[r]:
                        for h in range(4):
                            vec.tensor_tensor(VX[:, h, :].rearrange("p (c v) -> p c v", v=HD),
                                              nat[:, t, 64 * h:64 * h + 64].unsqueeze(1).to_broadcast([P, TC, HD]),
                                              c_("chunk").unsqueeze(2).to_broadcast([P, TC, HD]), ALU.mult)
                        tell(vx_ready)
                        b0, b1 = v.next(), v.next()
                        dve.wait_ge(vfull[b0], 1).then_inc(vfull[b0], -1)
                        dve.wait_ge(vfull[b1], 1).then_inc(vfull[b1], -1)
                        order = range(TC) if r == 0 else range(TC - 1, -1, -1)
                        for c in order:
                            row = TC * t + c + (t > 0)
                            for pr, b in ((0, b0), (1, b1)):
                                last = vec.scalar_tensor_tensor(
                                    S[:, pr, row + 1 - r, :], S[:, pr, row + r, :],
                                    tot[:, NCH * pr + TC * t + c:NCH * pr + TC * t + c + 1],
                                    vb[b][:, HD * c:HD * c + HD], ALU.mult, ALU.add)
                            settle()
                        dve.sem_inc(vfree[b0], 1)
                        dve.sem_inc(vfree[b1], 1)
                    if r == 0:
                        dve.wait_ge(fin_stored, 16).then_inc(fin_stored, -16)
                    vec.tensor_copy(fin[:, 2 * r:2 * r + 2, :], S[:, :, 0 if r else TC, :])
                    tell(states_ready)
                    if r == 1:
                        tell(fin_ready)
                    for t in range(NT):
                        for h2 in range(2):
                            m = c_("mask1" if r else "mask0")
                            empty(lambda o: vec.tensor_tensor(attS[:, h2:4:2, :], o[:, 0:256].rearrange("p (a b) -> p a b", b=P),
                                                              m.unsqueeze(1).to_broadcast([P, 2, P]), ALU.mult))
                        tell(att_ready)
                        dst = oT[:, :, P * t:P * t + P]
                        if r == 0:
                            empty(lambda o: vec.tensor_copy(dst, o[:, 0:256].rearrange("p (a b) -> p a b", b=P)))
                        else:
                            empty(lambda o: vec.tensor_tensor(dst, o[:, 0:256].rearrange("p (a b) -> p a b", b=P), dst, ALU.add))
                tell(o_ready)
                dve.wait_ge(proj_done, 1).then_inc(proj_done, -1)
                dve.wait_ge(root_ready, 1).then_inc(root_ready, -1)
                vec.reciprocal(QE, QE)
                settle()
                for pr in range(2):
                    vec.scalar_tensor_tensor(oT[:, pr, :], oT[:, pr, :], s_("onorm"), QE[:, pr, :], ALU.mult, ALU.mult)
                    settle()
                    vec.tensor_tensor(yT[:, pr, :], oT[:, pr, :], gT[:, pr, :], ALU.mult)
                    settle()
                for dst, src, h, lo, hi in ((s2, uT[:, :, :], None, 1, PADU), (s4, s2, 1, 2, PADU - 1),
                                            (s8, s4, 2, 4, PADU - 3), (s16, s8, 4, 8, PADU - 7)):
                    if h is None:
                        vec.tensor_tensor(dst[:, :, lo:hi], src[:, :, lo - 1:hi - 1], src[:, :, lo:hi], ALU.add)
                    else:
                        vec.tensor_tensor(dst[:, :, lo:hi], src[:, :, lo - h:hi - h], src[:, :, lo + h:hi + h], ALU.add)
                    settle()
                inv = c_("inv").rearrange("p (a b) -> p a b", b=PADU)
                lo, hi = 8, PADU - 8
                for g, s in enumerate((s2, s4, s8, s16)):
                    q = slice(64 * (g % 2), 64 * (g % 2) + 64)
                    vec.tensor_tensor(pl[q, g // 2, lo:hi], s[q, g // 2, lo:hi], inv[q, g // 2, lo:hi], ALU.mult)
                settle()
                vec.tensor_tensor(pl[:, :, lo:hi], pl[:, :, lo:hi], uT[:, :, lo:hi], ALU.subtract)
                tell(pooled_ready)
                for k in range(2):
                    empty(lambda o: vec.tensor_scalar(yT[:, 5 + k, :], o[:, 0:T], s_("pscale")[:, k:k + 1], None, ALU.mult))
                tell(yv_ready)
                tell(bias_wanted)
                for c0, kb, qn, kn, nq in ((256, 640, "wqn", "wkn", 6), (896, 1152, "nqn", "nkn", 4)):
                    X = nat[:, :, c0:c0 + 512]
                    t3 = tmp.rearrange("p (a b) -> p a b", b=512)
                    vec.tensor_tensor(t3, X, X, ALU.mult)
                    settle()
                    vec.reduce_sum(small[:, 0:24], tmp.rearrange("p (a b) -> p a b", b=HD), axis=AX.X)
                    tell(root_wanted)
                    dve.wait_ge(root_ready, 1).then_inc(root_ready, -1)
                    vec.reciprocal(small[:, 24:48], small[:, 24:48])
                    settle()
                    for t in range(NT):
                        Xt = X[:, t, :].rearrange("p (h d) -> p h d", d=HD)
                        vec.tensor_tensor(Xt, Xt, small[:, 24 + 8 * t:32 + 8 * t].unsqueeze(2).to_broadcast([P, 8, HD]),
                                          ALU.mult)
                    settle()
                    for t in range(NT):
                        Xt = X[:, t, :].rearrange("p (h d) -> p h d", d=HD)
                        for h0, h1, g in ((0, nq, qn), (nq, 8, kn)):
                            vec.tensor_tensor(Xt[:, h0:h1, :], Xt[:, h0:h1, :],
                                              s_(g).unsqueeze(1).to_broadcast([P, h1 - h0, HD]), ALU.mult)
                    settle()
                tell(kv_ready)
                for t in range(NT):
                    X = nat[:, t, 256:768]
                    if t > 0:
                        R = tmp[:, 0:512]
                        R2 = tmp[:, 512:1024]
                        vec.tensor_tensor(R.rearrange("p (h d) -> p h d", d=HD), X.rearrange("p (h d) -> p h d", d=HD),
                                          c_("cos")[:, HD * (t - 1):HD * t].unsqueeze(1).to_broadcast([P, 8, HD]), ALU.mult)
                        xv = X.rearrange("p (h a q) -> p h a q", a=4, q=16)
                        rv = R2.rearrange("p (h a q) -> p h a q", a=4, q=16)
                        sv = c_("sin")[:, HD * (t - 1):HD * t].rearrange("p (a q) -> p a q", q=16)
                        for k in range(4):
                            vec.tensor_tensor(rv[:, :, k, :], xv[:, :, k ^ 1, :],
                                              sv[:, k, :].unsqueeze(1).to_broadcast([P, 8, 16]), ALU.mult)
                        settle()
                        vec.tensor_tensor(R, R, R2, ALU.add)
                        settle()
                        X = R
                    vec.tensor_copy(qkr[:, t, 0:384].rearrange("p (j g d) -> p g j d", g=2, d=HD),
                                    X[:, 0:384].rearrange("p (g j d) -> p g j d", g=2, d=HD))
                    vec.tensor_copy(qkr[:, t, 384:512], X[:, 384:512])
                    settle()
                tell(qk_ready)
                dve.wait_ge(bias_in, 256).then_inc(bias_in, -256)
                nm = c_("nmask").unsqueeze(1).to_broadcast([P, 4, HD])
                for ht in range(8):
                    vec.tensor_tensor(biasD[:, ht, 0:256].rearrange("p (a b) -> p a b", b=HD),
                                      raw[:, ht, ::-1].rearrange("p (a b) -> p a b", b=HD), nm, ALU.add)
                vec.memset(biasD[:, :, 256:T], 0.0)
                settle()
                wm = c_("wmask").rearrange("p (a b) -> p a b", b=T)

                def scaled(i):
                    if i >= 2:
                        dve.wait_ge(s_free, 1).then_inc(s_free, -1)
                    s, k = sP[i % 2], 8 * (i % 2)
                    empty(lambda o: vec.tensor_scalar(s[:, 0:P], o[:, 0:P], SCALE, None, ALU.mult))
                    for t in (1, 2):
                        add = wm[:, t - 1, :] if i < 6 else biasD[:, 2 * (i - 6) + t - 1, :]
                        c0 = P + T * (t - 1)
                        empty(lambda o: vec.scalar_tensor_tensor(s[:, c0:c0 + T], o[:, 0:T], SCALE, add, ALU.mult, ALU.add))
                    settle()
                    vec.reduce_max(sbig[:, k + 3:k + 4], s[:, 0:P], axis=AX.X)
                    vec.reduce_max(sbig[:, k + 4:k + 6], s[:, P:896].rearrange("p (a b) -> p a b", b=T), axis=AX.X)
                    settle()
                    vec.tensor_scalar(sbig[:, k:k + 3], sbig[:, k + 3:k + 6], s_("sink")[:, i:i + 1], -1.0, ALU.max, ALU.mult)
                    tell(exp_wanted)

                def normalised(i):
                    dve.wait_ge(exp_ready, 1).then_inc(exp_ready, -1)
                    s, k = sP[i % 2], 8 * (i % 2)
                    vec.tensor_tensor(sbig[:, 48:51], sbig[:, 16 + k:19 + k], sbig[:, 32 + k:35 + k], ALU.add)
                    settle()
                    vec.reciprocal(sbig[:, 52:55], sbig[:, 48:51])
                    settle()
                    for t, (c0, n) in enumerate(((0, P), (P, T), (P + T, T))):
                        vec.tensor_scalar(s[:, c0:c0 + n], s[:, c0:c0 + n], sbig[:, 52 + t:53 + t], None, ALU.mult)
                    tell(p_ready)

                scaled(0)
                for i in range(NH):
                    if i + 1 < NH:
                        scaled(i + 1)
                    normalised(i)
                dve.wait_ge(s_free, 1).then_inc(s_free, -1)
                dve.wait_ge(s_free, 1).then_inc(s_free, -1)
                k = 0
                for nb in range(4):
                    for b in range(4):
                        for n in range(2):
                            m = merged[:, 2 * nb + n, :]
                            dve.wait_ge(gb_ready, 1).then_inc(gb_ready, -1)
                            if b == 0:
                                empty(lambda o: vec.tensor_tensor(m, o[:, 0:T], gb[k % 2], ALU.mult))
                                tell(gb_free)
                            else:
                                empty(lambda o: vec.tensor_tensor(mt, o[:, 0:T], gb[k % 2], ALU.mult))
                                tell(gb_free)
                                vec.tensor_tensor(m, m, mt, ALU.add)
                                settle()
                            k += 1
                tell(merged_ready)

                def residual(s):
                    for c in range(KC):
                        def add(o):
                            vec.scalar_tensor_tensor(xT[:, c, 0:P], o[:, 0:P], mT[:, s, c, 0:1], xT[:, c, 0:P],
                                                     ALU.mult, ALU.add)
                            return vec.scalar_tensor_tensor(xT[:, c, P:T], o[:, P:T], mT[:, s, c, 1:2], xT[:, c, P:T],
                                                            ALU.mult, ALU.add)
                        empty(add)
                    tell(x_ready)

                residual(2)
                norm(1)
                dve.wait_ge(sc_ready, 1).then_inc(sc_ready, -1)
                vec.tensor_tensor(sbr[:, :, 0:NE], sc[:, :, :], s_("brout").unsqueeze(1).to_broadcast([P, NT, NE]), ALU.add)
                settle()
                for t in range(NT):
                    vec.max(top8[:, t, :], sbr[:, t, :])
                settle()
                vec.memset(top8[:, :, TOPK:8], NEG)
                settle()
                for t in range(NT):
                    vec.match_replace(rep[:, t, :], top8[:, t, :], sbr[:, t, :], -3e38)
                settle()
                vec.scalar_tensor_tensor(gate[:, :, :], rep[:, :, 0:NE], -2e30, sc[:, :, :], ALU.is_lt, ALU.mult)
                settle()
                vec.reduce_sum(small[:, 48:51], gate[:, :, :], axis=AX.X)
                settle()
                vec.reciprocal(small[:, 52:55], small[:, 48:51])
                settle()
                for t in range(NT):
                    vec.tensor_scalar(gate[:, t, :], gate[:, t, :], small[:, 52 + t:53 + t], ROUTED_SCALE, ALU.mult, ALU.mult)
                settle()
                dve.wait_ge(kv_stored, 64).then_inc(kv_stored, -64)

                def weighted(j, g):
                    dve.wait_ge(si_ready, 1).then_inc(si_ready, -1)
                    vec.scalar_tensor_tensor(aa[j % 2], vb[j % 2][:, DE:2 * DE], g, si[j % 2], ALU.mult, ALU.mult)\
                        .then_inc(vfree[j % 2], 1)
                    tell(a_ready)

                def summed(t, first):
                    for n in range(2):
                        dst = acc[:, t, 512 * n:512 * n + 512]
                        dve.wait_ge(vfull[2 + n], 1).then_inc(vfull[2 + n], -1)
                        if first:
                            i = vec.tensor_copy(dst, vb[2 + n][:, :])
                        else:
                            i = vec.tensor_tensor(dst, vb[2 + n][:, :], dst, ALU.add)
                        i.then_inc(vfree[2 + n], 1)

                def experts(n, gate_of, first):
                    for j in range(NT * n + 1):
                        if j < NT * n:
                            weighted(j, gate_of(j // NT, j % NT))
                        if j > 0:
                            summed((j - 1) % NT, first)
                    settle()

                experts(1, lambda e, t: 1.0, True)
                with dve.Fori(0, NE // 2) as j:
                    v.restart()
                    experts(2, lambda e, t: gate[:, t, bass.ds(2 * j + e, 1)], False)
                v.restart()
                tell(acc_ready)
                residual(5)
                tell(layer_done)
            tell(y_ready)
            dve.wait_ge(fin_stored, 16).then_inc(fin_stored, -16)


_OUTS = [("yT", (P, KC, T)), ("wk", (DEPTH, P, 128)), ("wv", (DEPTH, P, 128)), ("nk", (DEPTH, P, 256)),
         ("nv", (DEPTH, P, 256)), ("fin", (DEPTH, P, 256))]


def constants():
    import numpy as np

    con = np.zeros((P, CNW), np.float32)

    def put(name, x):
        con[:, CN[name][0]:CN[name][1]] = np.asarray(x, np.float32).reshape(P, -1)

    i = np.arange(P)
    put("ident", np.eye(P))
    put("onesD", np.full((P, P), 1.0 / D))
    put("blk64", (i[:, None] // 64 == i[None] // 64) / 64.0)
    same = i[:, None] // CH == i[None] // CH
    put("mask0", same & (i[:, None] <= i[None]))
    put("mask1", same & (i[:, None] >= i[None]))
    put("chunk", i[:, None] // CH == np.arange(TC)[None])
    put("first", np.broadcast_to(np.arange(2 * T) % CH != 0, (P, 2 * T)))
    qc = i % 64
    start = np.clip(qc - 8, 0, 48)[:, None]
    kc = np.arange(64)[None]
    put("nmask", np.where((kc >= start) & (kc < start + 16), 0.0, NEG))
    wm = np.zeros((P, 2, T), np.float32)
    qp = i[:, None] + P * np.arange(2)[None]
    wm[:, :, 0:256] = np.where(np.abs(np.arange(256)[None, None] - qp[:, :, None]) <= 128, 0.0, NEG)
    put("wmask", wm)
    t = np.arange(256)
    inv = (10000.0 ** (-np.arange(16) / 16)).astype(np.float32)
    cos = np.zeros((256, 4, 16), np.float32)
    sin = np.zeros((256, 4, 16), np.float32)
    for half, pos in enumerate((t // 64, t % 64)):
        ang = pos.astype(np.float32)[:, None] * inv[None]
        cos[:, 2 * half] = cos[:, 2 * half + 1] = np.cos(ang)
        sin[:, 2 * half], sin[:, 2 * half + 1] = -np.sin(ang), np.sin(ang)
    put("cos", cos.reshape(2, P, 64).transpose(1, 0, 2))
    put("sin", sin.reshape(2, P, 64).transpose(1, 0, 2))
    cnt = np.zeros((4, PADU), np.float32)
    for g, size in enumerate((2, 4, 8, 16)):
        for at, n in ((8, P), (152, 256)):
            pos = np.arange(n)
            cnt[g, at:at + n] = 1.0 / (np.clip(pos + size // 2, 0, n) - np.clip(pos - size // 2, 0, n))
    both = np.zeros((P, 2, PADU), np.float32)
    for g in range(4):
        both[64 * (g % 2):64 * (g % 2) + 64, g // 2] = cnt[g]
    put("inv", both)
    put("eps", np.full((P, 1), EPS))
    return con


def kernel(**inputs):
    import numpy as np
    import concourse.bacc as bacc
    from concourse.bass_utils import run_bass_kernel_spmd as run

    a = {k: np.asarray(v) for k, v in inputs.items()}
    L_ = DEPTH

    def pc(x):
        return x.reshape(x.shape[:-1] + (P, KC))

    def cp(x):
        return np.swapaxes(x.reshape(x.shape[:-1] + (-1, P)), -1, -2)

    def rows(x):
        return np.broadcast_to(x[:, None, :], (L_, P, x.shape[-1]))

    x = np.concatenate([a["x_prompt"][0], a["x_sample"][0]], axis=0)
    h = {"con": constants(),
         "xT": np.transpose(pc(x), (1, 2, 0)),
         "cT": np.stack([pc(a["c_ctx"]), pc(a["c"][0])], axis=-1)}
    wm = a["w_mod"].reshape(L_, D, 6, P, KC)
    h["w_mod"] = np.swapaxes(wm, -1, -2).reshape(L_, D, 6 * D)
    bm = a["b_mod"].reshape(L_, 6, P, KC).transpose(0, 2, 1, 3)
    sink = np.concatenate([a["win_sink"], np.full((L_, 4), NEG, np.float32)], axis=1)
    h["sm"] = np.concatenate([
        pc(a["norm1_g"]), pc(a["norm2_g"]),
        np.repeat(bm.reshape(L_, P, 48), 2, axis=-1),
        cp(a["b_mgate"]),
        np.tile(a["hg_onorm"], (1, 2))[:, :, None],
        cp(a["pool_scale"]),
        rows(a["b_router"]), rows(a["win_qn"]), rows(a["win_kn"]), rows(a["na_qn"]), rows(a["na_kn"]), rows(sink),
        np.broadcast_to(cp(a["hg_lb"]).transpose(2, 0, 1, 3).reshape(1, P, 8), (L_, P, 8)),
    ], axis=2)
    kw = a["cache_win_k"][0].transpose(0, 2, 3, 1).reshape(L_, P, P)
    kn = a["cache_na_k"][0].transpose(0, 2, 3, 1).reshape(L_, 2, P, P).transpose(0, 2, 1, 3).reshape(L_, P, 256)
    h["kcT"] = np.concatenate([kw, kn], axis=2)
    h["vc"] = np.concatenate([a["cache_win_v"][0].reshape(L_, P, P), a["cache_na_v"][0].reshape(L_, P, 256)], axis=2)
    h["s0"] = a["state_hgrn"][0].reshape(L_, 2, 2, 2, HD, HD).transpose(0, 3, 4, 1, 2, 5).reshape(L_, P, 256)
    h["poolw"] = a["pool_w"].reshape(L_, 2, 2, HD, HD).transpose(0, 2, 3, 1, 4).reshape(L_, P, P)
    h["rpb"] = a["na_rpb"][:, :, ::-1, ::-1].reshape(L_, 4, 465)
    for k in ("w_in", "w_mgate", "w_branch", "w_out", "w_router", "w_sg", "w_su", "w_sd"):
        h[k] = a[k]
    for k in ("w_eg", "w_eu", "w_ed"):
        h[k] = a[k].reshape((L_ * NE,) + a[k].shape[2:])

    nc = bacc.Bacc("TRN2", target_bir_lowering=False, num_devices=1)
    arrays, A, O = {}, {}, {}
    for k, arr in h.items():
        arr = np.ascontiguousarray(arr)
        arrays["in_" + k] = arr
        A[k] = nc.dram_tensor("in_" + k, arr.shape, mybir.dt.from_np(arr.dtype), kind="ExternalInput").ap()
    for k, shape in _OUTS:
        O[k] = nc.dram_tensor("out_" + k, shape, F32, kind="ExternalOutput").ap()
    build(nc, A, O)
    r = run(nc, [arrays], core_ids=[0]).results[0]
    o = {k: r["out_" + k] for k, _ in _OUTS}
    y = np.transpose(o["yT"], (2, 0, 1)).reshape(T, D)
    fin = o["fin"].reshape(L_, 2, HD, 2, 2, HD).transpose(0, 3, 4, 1, 2, 5).reshape(1, L_, 2, 4, HD, HD)
    return (y[None, 0:P], y[None, P:T],
            o["wk"].reshape(1, L_, P, 2, HD), o["wv"].reshape(1, L_, P, 2, HD),
            o["nk"].reshape(1, L_, P, 4, HD), o["nv"].reshape(1, L_, P, 4, HD), fin)
```

```python
import concourse.bass as bass
from concourse import mybir
from contextlib import ExitStack

F32 = mybir.dt.float32
ALU = mybir.AluOpType
ACT = mybir.ActivationFunctionType
AX = mybir.AxisListType

P = 128
D = 1024
KC = D // P
T = 384
NT = T // P
DEPTH = 2
HD = 64
SCALE = HD ** -0.5
EPS = 1e-6
NEG = -1e30
CH = 16
TC = P // CH
NCH = T // CH
NH = 10
NE = 32
DE = 256
TOPK = 4
ROUTED_SCALE = 2.5
SLOT = KC * 512
NSLOT = 4
NJ = 48
FAR = 1 << 20
U32 = mybir.dt.uint32
I32 = mybir.dt.int32
NBANK = 4
PADU = 416
UPOS = (8, 152, 280)
NATW = 1664
SROW = 26

SM = {}
_at = 0
for _n, _w in (("g1", 8), ("g2", 8), ("bmod", 96), ("bmg", 32), ("onorm", 1), ("pscale", 2), ("brout", 32),
               ("wqn", 64), ("wkn", 64), ("nqn", 64), ("nkn", 64), ("sink", NH), ("lb", 8)):
    SM[_n] = (_at, _at + _w)
    _at += _w
SMW = _at
CN = {}
_at = 0
for _n, _w in (("ident", 128), ("blk64", 128), ("mask0", 128), ("mask1", 128), ("chunk", TC),
               ("first", 2 * T), ("nmask", HD), ("wmask", 2 * T), ("cos", 2 * HD), ("sin", 2 * HD),
               ("inv", 2 * PADU), ("eps", 1),
               ("before", P), ("ones", P), ("jobs", NJ), ("token", NT)):
    CN[_n] = (_at, _at + _w)
    _at += _w
CNW = _at




class Cursor:

    def __init__(self, order):
        self.order, self.at = order, 0

    def next(self):
        i = self.order[self.at]
        self.at = (self.at + 1) % len(self.order)
        return i

    def restart(self):
        self.at = 0


SLOT_ORDER = (2, 3, 0, 1) * 4 + 2 * (2, 3, 0, 1, 3, 0) + (2, 3, 0, 1) + (2, 3) + (0, 1, 2, 3)


def head_place(i):
    if i < 6:
        g = i // 3
        return i % 3, 3, 0, 64 * g, 768 + 64 * g, 64 * g, 2 + i // 2, 64 * (i % 2)
    h = i - 6
    return 4 + h // 2, 6 + h // 2, 1 + h // 2, 64 * (h % 2), 1408 + 64 * h, 128 + 64 * h, 7 + h // 2, 64 * (h % 2)


BRANCH_CHUNKS = ((0, 1), (2, 3, 4), (5, 6), (7, 8))
PASSES = ((0, 2), (1, 3))
UNITS = 2 * KC

PROJ = [[(1, 0, 128), (1, 128, 128), (1, 256, 128), (1, 384, 128)],
        [(1, 512, 128), (1, 640, 128), (0, 768, 256)],
        [(1, 1024, 128), (1, 1152, 128), (0, 1280, 256)],
        [(0, 1536, 384), (1, 1920, 128)],
        [(1, 2048, 128), (0, 2176, 384)],
        [(0, 2560, 384)]]


GROUPS = [(b, tr, c0, n, t) for b, groups in enumerate(PROJ) for tr, c0, n in groups
          for t in ((None,) if tr else range(NT))]
EARLY = sum(g[0] < 2 for g in GROUPS)
LATE = (len(GROUPS) - EARLY) // 2


def nat_col(c):
    if c < 1024:
        return c - 768
    return c - 1280 + 256 if c < 1920 else c - 2176 + 896


def build(nc, A, O):
    ctx = ExitStack()
    with ctx:
        def sb(name, shape):
            return ctx.enter_context(nc.sbuf_tensor(name, shape, F32))

        def sem(name):
            return ctx.enter_context(nc.semaphore(name))

        slots = [sb(f"slot{i}", [P, SLOT]) for i in range(NSLOT)]
        xT = sb("xT", [P, KC, T])
        hT = sb("hT", [P, KC, T])
        nat = sb("nat", [P, NT, NATW])
        merged = sb("merged", [P, KC, T])
        qT, gT = merged[:, 0:2, :], merged[:, 6:8, :]
        sig = [merged[:, 2:4, :], merged[:, 4:6, :]]
        mod_rows = sb("mod_rows", [P, 512])
        uT = sb("uT", [P, 2, PADU])
        yT = sb("yT", [P, 9, T])
        con = sb("con", [P, CNW])
        sm = sb("sm", [P, SMW])
        kcT = sb("kcT", [P, 3, P])
        vc = sb("vc", [P, T])
        s0 = sb("s0", [P, 4, HD])
        fin = sb("fin", [P, 4, HD])
        poolw = sb("poolw", [P, 2, HD])
        wr = sb("wr", [P, KC, NE])
        scT = sb("scT", [P, KC, 2])
        mT = sb("mT", [P, 6, KC, 2])
        modA = sb("modA", [P, 2, KC, 2])
        rstd = sig[1][:, 0, :]
        lb = sb("lb", [P, DEPTH, 4])
        lbw = sb("lbw", [P, 8, 4])
        lbl = sb("lbl", [P, 2, 4])
        small = sb("small", [P, 64])
        sbig = sb("softmax_small", [P, 64])
        lease = [0]

        def moe(*shape):
            n = shape[0] * (shape[1] if len(shape) > 1 else 1)
            x = sig[0][:, :, :].rearrange("p a b -> p (a b)")[:, lease[0]:lease[0] + n]
            lease[0] += n
            assert lease[0] <= 2 * T
            return x if len(shape) == 1 else x.rearrange("p (a b) -> p a b", b=shape[1])

        sc = moe(NT, NE)
        sbr = sb("sbr", [P, NT, NE + TOPK])
        rep = moe(NT, NE + TOPK)
        top8 = moe(NT, 8)
        gate = moe(NT, NE)
        def ib(name, shape, dt):
            return ctx.enter_context(nc.sbuf_tensor(name, shape, dt))

        chosen = moe(NT, NE)
        place = moe(NT, NE)
        nblk = moe(NE)
        incl = moe(NE)
        first_job = moe(NE)
        top_place = moe(NT, 8)
        place_u = ib("place_u", [P, NT * TOPK], U32)
        entry = ib("entry", [P, NT, TOPK, 2], F32)
        table = ib("table", [P, NJ, 2], F32)
        job_expert = ib("job_expert", [1, NJ], I32)
        job_count = ib("job_count", [1, 2], I32)
        rows_of = [ib(f"rows_of{i}", [P, 2], F32) for i in range(2)]
        sums_of = ib("sums_of", [P, 2], F32)
        table_d = nc.dram_tensor("job_table", [P * NJ, 2], F32, kind="Internal").ap()
        h2_d = nc.dram_tensor("h2_rows", [T, D], F32, kind="Internal").ap()
        sum_d = nc.dram_tensor("expert_sums", [T, D], F32, kind="Internal").ap()
        arena = sb("arena", [P, 11520])
        used = [0]

        def new_phase():
            used[0] = 0

        def ar(*shape):
            n = 1
            for s in shape:
                n *= s
            a = arena[:, used[0]:used[0] + n]
            used[0] += n
            assert used[0] <= 11520, used[0]
            if len(shape) == 2:
                return a.rearrange("p (a b) -> p a b", b=shape[1])
            if len(shape) == 3:
                return a.rearrange("p (a b c) -> p a b c", b=shape[1], c=shape[2])
            return a

        QE, KE, QX, L, C, DD = (ar(2, T) for _ in range(6))
        S = ar(2, SROW, HD)
        kdN = ar(NT, 256)
        VX = ar(4, TC * HD)
        attS = VX[:, 0, :].rearrange("p (a b) -> p a b", b=P)
        oT = ar(2, T)
        new_phase()
        s2, s4, s8, s16, pl = (ar(2, PADU) for _ in range(5))
        new_phase()
        qkr = ar(NT, 512)
        qkT = ar(8, T)
        biasD = ar(8, T)
        sP = [ar(896), ar(896)]
        pT = [ar(7, P), ar(7, P)]
        raw = arena[:, 3584 + 3072 + 1024:3584 + 3072 + 1024 + 2048]
        raw = arena[:, used[0] - 3584:used[0] - 3584 + 2048].rearrange("p (a b) -> p a b", b=256)
        tmp = arena[:, used[0] - 1536:used[0]]
        gb = [uT[:, :, :].rearrange("p a b -> p (a b)")[:, T * k:T * k + T] for k in range(2)]
        new_phase()
        sq = ar(KC, T)
        cT = sq[:, 0, 0:2 * KC].rearrange("p (a b) -> p a b", b=2)
        new_phase()
        si = [ar(DE), ar(DE)]
        aa = [ar(DE), ar(DE)]
        aT = [ar(2, P), ar(2, P)]
        hN = ar(NT, D)
        XG = [ar(D), ar(D)]
        XT = [ar(KC, P), ar(KC, P)]
        Y = [ar(D), ar(D)]
        cmp = arena[0:1, 8704:8704 + NJ * NE].rearrange("p (a b) -> p a b", b=NE)
        eq = ar(NT * TOPK * NE)
        acc = nat[:, :, 0:D]

        vb = [ctx.enter_context(nc.psum_tensor(f"vb{i}", [P, 512], F32)) for i in range(NBANK)]
        ab = [ctx.enter_context(nc.psum_tensor(f"ab{i}", [P, 512], F32)) for i in range(NBANK)]

        def c_(name):
            return con[:, CN[name][0]:CN[name][1]]

        def s_(name):
            return sm[:, SM[name][0]:SM[name][1]]

        ident = c_("ident")

        vfull = [sem(f"vfull{i}") for i in range(NBANK)]
        vfree = [sem(f"vfree{i}") for i in range(NBANK)]
        afull = [sem(f"afull{i}") for i in range(NBANK)]
        afree = [sem(f"afree{i}") for i in range(NBANK)]
        loaded = [sem(f"slot_loaded{i}") for i in range(NSLOT)]
        freed = [sem(f"slot_freed{i}") for i in range(NSLOT)]
        start_in = sem("start_in")
        params_in = sem("params_in")
        layer_done = sem("layer_done")
        mod_rows_ready = sem("mod_rows_ready")
        silu_c_ready = sem("silu_c_ready")
        c_loaded = sem("c_loaded")
        x_ready = sem("x_ready")
        sq_ready = sem("sq_ready")
        h_ready = sem("h_ready")
        root_wanted = sem("root_wanted")
        root_ready = sem("root_ready")
        gates_in = sem("recurrence_inputs_evacuated")
        proj_done = sem("projection_evacuated")
        vproj_done = sem("values_evacuated")
        f_ready = sem("f_ready")
        logf_ready = sem("logf_ready")
        exps_wanted = sem("exps_wanted")
        exps_ready = sem("exps_ready")
        rec_ready = sem("rec_operands_ready")
        kdn_ready = sem("kdn_ready")
        vx_ready = sem("vx_ready")
        att_ready = sem("att_ready")
        states_ready = sem("states_ready")
        fin_ready = sem("fin_ready")
        fin_stored = sem("fin_stored")
        o_ready = sem("o_ready")
        osq_ready = sem("osq_ready")
        pooled_ready = sem("pooled_ready")
        kv_ready = sem("kv_ready")
        kv_stored = sem("kv_stored")
        bias_wanted = sem("bias_wanted")
        bias_in = sem("bias_in")
        qk_ready = sem("qk_ready")
        qkt_ready = sem("qkt_ready")
        exp_wanted = sem("exp_wanted")
        exp_ready = sem("exp_ready")
        p_ready = sem("p_ready")
        pt_ready = sem("pt_ready")
        s_free = sem("s_free")
        yv_ready = sem("y_from_vector_ready")
        ya_ready = sem("y_from_scalar_ready")
        gb_ready = sem("gb_ready")
        gb_free = sem("gb_free")
        merged_ready = sem("merged_ready")
        sc_ready = sem("sc_ready")
        hid_full = [sem("hid_full0"), sem("hid_full1")]
        si_ready = sem("si_ready")
        a_ready = sem("a_ready")
        at_ready = sem("at_ready")
        acc_ready = sem("acc_ready")
        chosen_ready = sem("chosen_ready")
        hn_ready = sem("h2_rows_evacuated")
        h2_stored = sem("h2_stored")
        table_cleared = sem("table_cleared")
        entries_ready = sem("entries_ready")
        entries_out = sem("entries_out")
        table_in = sem("table_in")
        jobs_sp, jobs_pool, jobs_pe, jobs_act = (sem(f"job_list_ready_{e}") for e in ("sp", "pool", "pe", "act"))
        shared_ready = sem("shared_ready")
        shared_stored = sem("shared_stored")
        rows_out = sem("rows_gathered")
        sums_out = sem("sums_added")
        xg_ready = sem("xg_ready")
        table_ready = sem("table_ready")
        xg_free = sem("xg_free")
        xt_ready = sem("xt_ready")
        yj_ready = sem("job_output_ready")
        yj_free = sem("job_output_free")
        routed_done = sem("routed_done")
        acc_in = sem("acc_in")
        y_ready = sem("y_ready")
        y_stored = sem("y_stored")

        block = ctx.enter_context(nc.Block())

        def job_pairs(eng):
            return eng.value_load(job_count[0:1, 0:1], min_val=1, max_val=NJ // 2 - 1)

        @block.sync
        def _(sp):
            sp.dma_start(con[:, :], A["con"]).then_inc(start_in, 16)
            sp.dma_start(cT[:, :, :], A["cT"]).then_inc(c_loaded, 16)
            sp.dma_start(xT[:, :, :], A["xT"]).then_inc(start_in, 16)
            cur = Cursor(SLOT_ORDER)

            def load(parts):
                s = cur.next()
                sp.wait_ge(freed[s], 1).then_inc(freed[s], -1)
                for dst, src in parts(slots[s]):
                    sp.dma_start(dst, src).then_inc(loaded[s], 32 // len(parts(slots[s])))

            with sp.Fori(0, DEPTH) as l:
                cur.restart()

                def layer(name):
                    return A[name][bass.ds(l, 1)].rearrange("l a b -> (l a) b")

                def columns(name, b, w=512):
                    load(lambda s: [(s[:, 0:KC * w].rearrange("p (c n) -> p c n", c=KC),
                                     layer(name).rearrange("(p c) n -> p c n", c=KC)[:, :, 512 * b:512 * b + w])])

                for b in range(4):
                    columns("w_mod", b)
                for b in range(2):
                    columns("w_in", b)
                sp.wait_ge(layer_done, 1).then_inc(layer_done, -1)
                for dst, name in ((sm[:, :], "sm"), (kcT[:, :, :].rearrange("p a b -> p (a b)"), "kcT"),
                                  (vc[:, :], "vc"), (s0[:, :, :].rearrange("p a b -> p (a b)"), "s0"),
                                  (poolw[:, :, :].rearrange("p a b -> p (a b)"), "poolw")):
                    sp.dma_start(dst, A[name][bass.ds(l, 1)].rearrange("l p n -> (l p) n")).then_inc(params_in, 16)
                sp.dma_start(wr[:, :, :], A["w_router"][bass.ds(l, 1)].rearrange("l (p c) n -> (l p) c n", c=KC))\
                    .then_inc(params_in, 16)
                for b in range(2, 6):
                    columns("w_in", b, min(512, 2944 - 512 * b))
                for b in range(4, 10):
                    columns("w_mod", b)
                for two in PASSES:
                    for nb in range(4):
                        if nb % 2 == 0:
                            def rows(s):
                                at, parts = 0, []
                                for b in two:
                                    y0, n = BRANCH_CHUNKS[b][0], len(BRANCH_CHUNKS[b])
                                    parts.append((s[:, 512 * at:512 * (at + n)].rearrange("p (c n) -> p c n", c=n),
                                                  layer("w_branch")[P * y0:P * (y0 + n), :].rearrange(
                                                      "(c p) n -> p c n", c=n)[:, :, 256 * nb:256 * nb + 512]))
                                    at += n
                                return parts
                            load(rows)
                        load(lambda s: [(s[:, 2048 * k:2048 * (k + 1)].rearrange("p (c n) -> p c n", c=KC),
                                         layer("w_mgate").rearrange("(p c) n -> p c n", c=KC)[
                                             :, :, D * b + 256 * nb:D * b + 256 * nb + 256])
                                        for k, b in enumerate(two)])
                for half in range(2):
                    load(lambda s: [(s[:, :].rearrange("p (c n) -> p c n", c=4),
                                     layer("w_out")[512 * half:512 * half + 512, :].rearrange("(c p) n -> p c n", c=4))])
                for b in range(10, 12):
                    columns("w_mod", b)
                load(lambda s: [(s[:, :].rearrange("p (c n) -> p c n", c=KC)[:, :, DE * k:DE * k + DE],
                                 layer(w).rearrange("(p c) n -> p c n", c=KC)) for k, w in enumerate(("w_sg", "w_su"))])
                load(lambda s: [(s[:, 0:2048].rearrange("p (c n) -> p c n", c=2),
                                 layer("w_sd").rearrange("(c p) n -> p c n", c=2))])
                sp.wait_ge(jobs_sp, 1).then_inc(jobs_sp, -1)
                with sp.Fori(0, job_pairs(sp)) as j:
                    for k in range(2):
                        e = sp.value_load(job_expert[0:1, bass.ds(2 * j + k, 1)], min_val=0, max_val=NE - 1)

                        def expert(name):
                            return A[name][bass.ds(l * NE + e, 1)].rearrange("l a b -> (l a) b")

                        load(lambda s: [(s[:, :].rearrange("p (c n) -> p c n", c=KC)[:, :, DE * i:DE * i + DE],
                                         expert(w).rearrange("(p c) n -> p c n", c=KC))
                                        for i, w in enumerate(("w_eg", "w_eu"))])
                        load(lambda s: [(s[:, 0:2048].rearrange("p (c n) -> p c n", c=2),
                                         expert("w_ed").rearrange("(c p) n -> p c n", c=2))])
            sp.wait_ge(y_ready, 1).then_inc(y_ready, -1)
            sp.dma_start(O["yT"], xT[:, :, :]).then_inc(y_stored, 16)
            sp.wait_ge(y_stored, 16)

        @block.gpsimd
        def _(pool):
            def gather(j, b):
                pool.wait_ge(xg_free, 1).then_inc(xg_free, -1)
                nc.gpsimd.tensor_copy(rows_of[b][:, :], table[:, bass.ds(j, 1), :].rearrange("p a b -> p (a b)"))
                pool.drain()
                pool.indirect_dma_start(XG[b], None, h2_d, bass.IndirectOffsetOnAxis(ap=rows_of[b][:, 0:1].bitcast(U32), axis=0),
                                        bounds_check=T - 1, oob_is_err=False).then_inc(rows_out, 16)
                pool.drain().then_inc(xg_ready, 1)

            def add(j, b):
                nc.gpsimd.tensor_copy(sums_of[:, :], table[:, bass.ds(j, 1), :].rearrange("p a b -> p (a b)"))
                pool.wait_ge(yj_ready, 1).then_inc(yj_ready, -1)
                pool.drain()
                pool.indirect_dma_start(sum_d, bass.IndirectOffsetOnAxis(ap=sums_of[:, 0:1].bitcast(U32), axis=0), Y[b], None,
                                        bounds_check=T - 1, oob_is_err=False, compute_op=ALU.add).then_inc(sums_out, 16)
                pool.drain().then_inc(yj_free, 1)

            with pool.Fori(0, DEPTH):
                pool.wait_ge(table_cleared, 16).then_inc(table_cleared, -16)
                pool.wait_ge(entries_ready, 1).then_inc(entries_ready, -1)
                for t in range(NT):
                    for k in range(TOPK):
                        pool.indirect_dma_start(table_d, bass.IndirectOffsetOnAxis(
                            ap=place_u[:, TOPK * t + k:TOPK * t + k + 1], axis=0), entry[:, t, k, :], None)\
                            .then_inc(entries_out, 16)
                pool.drain()
                pool.dma_start(table[:, :, :], table_d.rearrange("(p j) w -> p j w", j=NJ)).then_inc(table_in, 16)
                pool.drain().then_inc(table_ready, 1)
                pool.wait_ge(h2_stored, 16).then_inc(h2_stored, -16)
                for b in range(2):
                    nc.gpsimd.memset(XG[b], 0.0)
                pool.drain()
                pool.wait_ge(jobs_pool, 1).then_inc(jobs_pool, -1)
                gather(0, 0)
                gather(1, 1)
                pool.wait_ge(shared_stored, 16).then_inc(shared_stored, -16)
                with pool.Fori(0, job_pairs(pool)) as j:
                    gather(2 * j + 2, 0)
                    gather(2 * j + 3, 1)
                    add(2 * j, 0)
                    add(2 * j + 1, 1)
                pool.drain().then_inc(routed_done, 1)

        @block.tensor
        def _(pe):
            v, a, sl = Cursor(range(NBANK)), Cursor(range(NBANK)), Cursor(SLOT_ORDER)
            release = []

            def mm(out, lhsT, rhs, start, stop, last=False):
                i = nc.tensor.matmul(out, lhsT, rhs, start=start, stop=stop, skip_group_check=True)
                if release and not last:
                    i.then_inc(freed[release.pop(0)], 1)
                return i

            def group(ring, body):
                b = ring.next()
                banks, full, free = (vb, vfull, vfree) if ring is v else (ab, afull, afree)
                pe.wait_ge(free[b], 1).then_inc(free[b], -1)
                last = body(banks[b])
                last.then_inc(full[b], 1)

            def slot():
                s = sl.next()
                if s in release:
                    flush()
                pe.wait_ge(loaded[s], 32).then_inc(loaded[s], -32)
                return s, slots[s]

            def flush():
                while release:
                    pe.drain().then_inc(freed[release.pop(0)], 1)

            def run(out, pairs):
                for k, (x, y) in enumerate(pairs):
                    last = mm(out, x, y, k == 0, k == len(pairs) - 1, k == len(pairs) - 1)
                return last

            def trans(bank, blocks):
                for k, x in enumerate(blocks):
                    last = nc.tensor.transpose(bank[:, P * k:P * k + P], x, ident)
                return last

            def norm(between=lambda: None):
                pe.wait_ge(sq_ready, 1).then_inc(sq_ready, -1)
                group(a, lambda o: run(o[:, 0:T], [(c_("ones"), sq[:, c, :]) for c in range(KC)]))
                between()
                pe.wait_ge(h_ready, 1).then_inc(h_ready, -1)

            def wview(w, c=KC):
                return w[:, 0:c * (SLOT // c)].rearrange("p (c n) -> p c n", c=c)

            def up(b, x, w):
                pe.wait_ge(vfree[b], 1).then_inc(vfree[b], -1)
                run(vb[b][:, :], [(x(c), wview(w)[:, c, :]) for c in range(KC)]).then_inc(hid_full[b], 1)

            def hidden(b):
                pe.wait_ge(a_ready, 1).then_inc(a_ready, -1)
                group(a, lambda o: trans(o, [aa[b][:, P * f:P * f + P] for f in range(2)]))

            def down(b, w):
                pe.wait_ge(at_ready, 1).then_inc(at_ready, -1)
                wd = w[:, 0:2048].rearrange("p (c n) -> p c n", c=2)
                for n in range(2):
                    pe.wait_ge(vfree[2 + n], 1).then_inc(vfree[2 + n], -1)
                    run(vb[2 + n][:, :], [(aT[b][:, f, :], wd[:, f, 512 * n:512 * n + 512]) for f in range(2)])\
                        .then_inc(vfull[2 + n], 1)

            def turned(b):
                pe.wait_ge(xg_ready, 1).then_inc(xg_ready, -1)
                for g in range(2):
                    group(a, lambda o: trans(o, [XG[b][:, P * c:P * c + P] for c in range(4 * g, 4 * g + 4)]))

            for s in range(NSLOT):
                pe.sem_inc(freed[s], 1)
            pe.wait_ge(silu_c_ready, 1).then_inc(silu_c_ready, -1)
            with pe.Fori(0, DEPTH):
                v.restart(), a.restart(), sl.restart()

                def mod_block(b):
                    s, w = slot()
                    q = 32 * (b % 4)
                    group(a, lambda o: run(o[q:q + 2, :], [(scT[:, c, :], wview(w)[:, c, :]) for c in range(KC)]))
                    release.append(s)

                def mod_turned():
                    pe.wait_ge(mod_rows_ready, 1).then_inc(mod_rows_ready, -1)
                    group(v, lambda o: trans(o, [mod_rows[:, P * n:P * n + P] for n in range(4)]))

                block_slot = {}

                def project(i):
                    b, tr, c0, n, t = GROUPS[i]
                    if b not in block_slot:
                        block_slot[b] = slot()
                    s, w = block_slot[b]
                    width = min(512, 2944 - 512 * b)
                    wv = w[:, 0:KC * width].rearrange("p (c n) -> p c n", c=KC)
                    o0 = c0 - 512 * b
                    if tr:
                        group(a, lambda o: run(o[:, 0:T], [(wv[:, c, o0:o0 + n], hT[:, c, :]) for c in range(KC)]))
                    else:
                        group(v if c0 == 768 else a,
                              lambda o: run(o[:, 0:n], [(hT[:, c, P * t:P * t + P], wv[:, c, o0:o0 + n])
                                                        for c in range(KC)]))
                    if i + 1 == len(GROUPS) or GROUPS[i + 1][0] != b:
                        release.append(s)

                for b in range(4):
                    mod_block(b)
                mod_turned()
                norm()
                for i in range(EARLY):
                    project(i)
                pe.wait_ge(vproj_done, 1).then_inc(vproj_done, -1)
                for r in range(2):
                    late = EARLY + LATE * r
                    for i in range(4):
                        project(late + i)
                    pe.wait_ge(rec_ready, 1).then_inc(rec_ready, -1)
                    for t in range(NT):
                        group(v, lambda o: trans(o, [L[:, pr, P * t:P * t + P] for pr in range(2)]))
                    project(late + 4)
                    pe.wait_ge(kdn_ready, 1).then_inc(kdn_ready, -1)
                    for t in ((0, 1, 2), (0, 2, 1))[r]:
                        pe.wait_ge(vx_ready, 1).then_inc(vx_ready, -1)
                        for pr in range(2):
                            def ds(o):
                                for h2 in range(2):
                                    h = 2 * pr + h2
                                    last = mm(o[64 * h2:64 * h2 + 64, :], kdN[:, t, 64 * h:64 * h + 64], VX[:, h, :],
                                              True, True)
                                return last
                            group(v, ds)
                        project(late + 5 + (t if r == 0 else (0, 2, 1)[t]))
                    pe.wait_ge(states_ready, 1).then_inc(states_ready, -1)
                    for t in range(NT):
                        for h2 in range(2):
                            def att(o):
                                for pr in range(2):
                                    last = mm(o[:, P * pr:P * pr + P], KE[64 * h2:64 * h2 + 64, pr, P * t:P * t + P],
                                              QE[64 * h2:64 * h2 + 64, pr, P * t:P * t + P], True, True)
                                return last
                            group(v, att)
                        pe.wait_ge(att_ready, 1).then_inc(att_ready, -1)

                        def out(o):
                            for pr in range(2):
                                for h2 in range(2):
                                    q = slice(64 * h2, 64 * h2 + 64)
                                    h = 2 * pr + h2
                                    mm(o[q, P * pr:P * pr + P], nat[:, t, 64 * h:64 * h + 64], attS[:, h, :], True, False)
                                    for c in range(TC):
                                        n0 = P * t + CH * c
                                        row = TC * t + c + (t > 0) + r
                                        last = mm(o[q, P * pr + CH * c:P * pr + CH * c + CH], S[q, pr, row, :],
                                                  QX[q, pr, n0:n0 + CH], False, c == TC - 1)
                            return last
                        group(v, out)
                pe.wait_ge(osq_ready, 1).then_inc(osq_ready, -1)
                for pr in range(2):
                    group(a, lambda o: run(o[:, 0:T], [(c_("blk64"), DD[:, pr, :])]))
                for b in range(4, 7):
                    mod_block(b)
                pe.wait_ge(pooled_ready, 1).then_inc(pooled_ready, -1)
                for k in range(2):
                    def pmap(o):
                        for h2 in range(2):
                            q = slice(64 * h2, 64 * h2 + 64)
                            mm(o[q, 0:P], poolw[q, k, :], pl[q, k, 8:8 + P], True, True)
                            last = mm(o[q, P:T], poolw[q, k, :], pl[q, k, 152:152 + 256], True, True)
                        return last
                    group(v, pmap)
                mod_block(7)
                mod_turned()
                for b in range(8, 10):
                    mod_block(b)
                mod_turned()
                pe.wait_ge(qk_ready, 1).then_inc(qk_ready, -1)
                for t in range(NT):
                    group(a, lambda o: trans(o, [qkr[:, t, P * j:P * j + P] for j in range(4)]))
                    group(a, lambda o: trans(o, [nat[:, t, 896 + P * j:896 + P * j + P] for j in range(4)]))
                pe.wait_ge(qkt_ready, 1).then_inc(qkt_ready, -1)

                def scores(i):
                    qc, kc, cc, p0 = head_place(i)[:4]
                    q = slice(p0, p0 + 64)
                    group(v, lambda o: mm(o[:, 0:P], qkT[q, qc, 0:P], qkT[q, kc, 0:P], True, True, True))
                    for t in (1, 2):
                        def s(o):
                            mm(o[:, 0:256], qkT[q, qc, P * t:P * t + P], qkT[q, kc, P:T], True, True)
                            return mm(o[:, 256:T], qkT[q, qc, P * t:P * t + P], kcT[q, cc, :], True, True)
                        group(v, s)

                held = {}

                def gated(two, u):
                    nb, k, n = u // 4, u // 2 % 2, u % 2
                    if u % 8 == 0:
                        held["branch"] = slot()
                    if u % 4 == 0:
                        held["gate"] = slot()
                    ys = BRANCH_CHUNKS[two[k]]
                    wm = held["gate"][1][:, 2048 * k:2048 * (k + 1)].rearrange("p (c n) -> p c n", c=KC)
                    wbv = held["branch"][1][:, :].rearrange("p (c n) -> p c n", n=512)
                    at = k * len(BRANCH_CHUNKS[two[0]])
                    col = 256 * (nb % 2) + P * n
                    group(a, lambda o: run(o[:, 0:T], [(wm[:, c, P * n:P * n + P], hT[:, c, :]) for c in range(KC)]))
                    group(v, lambda o: run(o[:, 0:T], [(wbv[:, at + j, col:col + P], yT[:, y, :])
                                                       for j, y in enumerate(ys)]))
                    if u % 4 == 3:
                        release.append(held["gate"][0])
                    if u % 8 == 7:
                        release.append(held["branch"][0])

                pe.wait_ge(yv_ready, 1).then_inc(yv_ready, -1)
                scores(0)
                for i in range(NH):
                    if i + 1 < NH:
                        scores(i + 1)
                    gated(PASSES[0], i)
                    vcol, ccol, _, op = head_place(i)[4:]
                    pe.wait_ge(p_ready, 1).then_inc(p_ready, -1)
                    group(a, lambda o: trans(o, [sP[i % 2][:, P * k:P * k + P] for k in range(4)]))
                    group(a, lambda o: trans(o, [sP[i % 2][:, P * k:P * k + P] for k in range(4, 7)]))
                    pe.wait_ge(pt_ready, 1).then_inc(pt_ready, -1)

                    def pv(o):
                        q = slice(op, op + 64)
                        mm(o[q, 0:P], nat[:, 0, vcol:vcol + 64], pT[i % 2][:, 0, :], True, True)
                        for t in (1, 2):
                            k0 = 1 + 3 * (t - 1)
                            last = run(o[q, P * t:P * t + P],
                                       [(nat[:, 1, vcol:vcol + 64], pT[i % 2][:, k0, :]),
                                        (nat[:, 2, vcol:vcol + 64], pT[i % 2][:, k0 + 1, :]),
                                        (vc[:, ccol:ccol + 64], pT[i % 2][:, k0 + 2, :])])
                        return last
                    group(a, pv)
                for u in range(NH, UNITS):
                    gated(PASSES[0], u)
                pe.wait_ge(ya_ready, 1).then_inc(ya_ready, -1)
                for u in range(UNITS):
                    gated(PASSES[1], u)
                flush()
                pe.wait_ge(merged_ready, 1).then_inc(merged_ready, -1)
                wo = [slot(), slot()]
                for c in range(KC):
                    group(v, lambda o: run(o[:, 0:T], [(wview(wo[k // 4][1], 4)[:, k % 4, c:D:KC], merged[:, k, :])
                                                       for k in range(KC)]))
                release.extend([wo[0][0], wo[1][0]])
                mod_block(10)
                norm(lambda: mod_block(11))
                mod_turned()
                def router(o):
                    for t in range(NT):
                        last = run(o[:, NE * t:NE * t + NE], [(hT[:, c, P * t:P * t + P], wr[:, c, :]) for c in range(KC)])
                    return last
                group(a, router)
                pe.wait_ge(chosen_ready, 1).then_inc(chosen_ready, -1)

                def places(o):
                    for t in range(NT):
                        run(o[:, NE * t:NE * t + NE],
                            [(c_("ones"), chosen[:, u, :]) for u in range(t)] + [(c_("before"), chosen[:, t, :])])
                    return run(o[:, NE * NT:NE * NT + NE], [(c_("ones"), chosen[:, u, :]) for u in range(NT)])
                group(v, places)
                for t in range(NT):
                    for g in range(2):
                        group(a, lambda o: trans(o, [hT[:, c, P * t:P * t + P] for c in range(4 * g, 4 * g + 4)]))
                v.restart(), a.restart()
                (sg, wg), (sd, wd_) = slot(), slot()
                up(0, lambda c: hT[:, c, 0:P], wg)
                for t in range(1, NT):
                    up(t % 2, lambda c: hT[:, c, P * t:P * t + P], wg)
                    if t == NT - 1:
                        release.append(sg)
                    hidden((t - 1) % 2)
                    down((t - 1) % 2, wd_)
                hidden((NT - 1) % 2)
                down((NT - 1) % 2, wd_)
                release.append(sd)
                flush()
                pe.wait_ge(jobs_pe, 1).then_inc(jobs_pe, -1)
                a.restart()
                turned(0)
                with pe.Fori(0, job_pairs(pe)):
                    a.restart()
                    pe.wait_ge(xt_ready, 1).then_inc(xt_ready, -1)
                    sg0, w = slot()
                    up(0, lambda c: XT[0][:, c, :], w)
                    release.append(sg0)
                    turned(1)
                    hidden(0)
                    sd0, wd0 = slot()
                    pe.wait_ge(xt_ready, 1).then_inc(xt_ready, -1)
                    sg1, w = slot()
                    up(1, lambda c: XT[1][:, c, :], w)
                    release.append(sg1)
                    down(0, wd0)
                    release.append(sd0)
                    turned(0)
                    hidden(1)
                    sd1, wd1 = slot()
                    down(1, wd1)
                    release.append(sd1)
                    flush()
                pe.wait_ge(xt_ready, 1).then_inc(xt_ready, -1)
                pe.wait_ge(xg_ready, 1).then_inc(xg_ready, -1)
                pe.wait_ge(acc_in, 16).then_inc(acc_in, -16)
                v.restart()
                for c in range(KC):
                    group(v, lambda o: trans(o, [acc[:, t, c:D:KC] for t in range(NT)]))

        @block.scalar
        def _(act):
            a = Cursor(range(NBANK))
            f = nc.scalar.activation

            def empty(body):
                b = a.next()
                act.wait_ge(afull[b], 1).then_inc(afull[b], -1)
                body(ab[b]).then_inc(afree[b], 1)

            def tell(s):
                act.drain().then_inc(s, 1)

            for b in range(NBANK):
                act.sem_inc(afree[b], 1)
            act.wait_ge(c_loaded, 16).then_inc(c_loaded, -16)
            f(scT[:, :, :], cT[:, :, :], ACT.Silu).then_inc(silu_c_ready, 1)
            with act.Fori(0, DEPTH) as l:
                a.restart()
                act.wait_ge(f_ready, 1).then_inc(f_ready, -1)
                act.dma_start(table_d.rearrange("(p j) w -> p (j w)", j=NJ), table[:, :, :].rearrange("p a b -> p (a b)"))\
                    .then_inc(table_cleared, 16)
                f(lbw[:, 1:3, :], lbw[:, 1:3, :], ACT.Exp).then_inc(logf_ready, 1)

                def mod_row(b):
                    q = 32 * (b % 4)
                    empty(lambda o: f(mod_rows[q:q + 2, :], o[q:q + 2, :], ACT.Copy))

                def square(between=lambda: None):
                    act.wait_ge(x_ready, 1).then_inc(x_ready, -1)
                    f(sq[:, :, :], xT[:, :, :], ACT.Square).then_inc(sq_ready, 1)
                    between()
                    empty(lambda o: f(rstd[:, :], o[:, 0:T], ACT.Sqrt, bias=c_("eps"), scale=1.0 / D))
                    tell(root_ready)

                for b in range(4):
                    mod_row(b)
                tell(mod_rows_ready)
                square()
                for dst, fn in ((qT, ACT.Copy), (sig[0], ACT.Sigmoid), (sig[1], ACT.Sigmoid)):
                    for pr in range(2):
                        empty(lambda o: f(dst[:, pr, :], o[:, 0:T], fn))
                tell(gates_in)

                def projected(i):
                    _, tr, c0, n, t = GROUPS[i]
                    if c0 in (1024, 1152):
                        empty(lambda o: f(gT[:, (c0 - 1024) // P, :], o[:, 0:T], ACT.Silu))
                    elif tr:
                        k = (c0 - 1920) // P

                        def padded(o):
                            f(uT[:, k, 8:8 + P], o[:, 0:P], ACT.Copy)
                            return f(uT[:, k, 152:152 + 256], o[:, P:T], ACT.Copy)
                        empty(padded)
                    else:
                        empty(lambda o: f(nat[:, t, nat_col(c0):nat_col(c0) + n], o[:, 0:n], ACT.Copy))

                for r in range(2):
                    late = EARLY + LATE * r
                    act.wait_ge(f_ready, 1).then_inc(f_ready, -1)
                    f(L, sig[r][:, :, :], ACT.Ln).then_inc(logf_ready, 1)
                    projected(late)
                    act.wait_ge(exps_wanted, 1).then_inc(exps_wanted, -1)
                    f(QE, DD, ACT.Exp)
                    f(KE, DD, ACT.Exp, scale=-1.0)
                    f(QX, C, ACT.Exp)
                    f(L, L, ACT.Exp)
                    f(small[:, 0:48], small[:, 0:48], ACT.Exp)
                    tell(exps_ready)
                    for i in range(1, LATE):
                        projected(late + i)
                tell(proj_done)
                act.wait_ge(fin_ready, 1).then_inc(fin_ready, -1)
                act.wait_ge(o_ready, 1).then_inc(o_ready, -1)
                f(DD, oT, ACT.Square).then_inc(osq_ready, 1)
                for pr in range(2):
                    empty(lambda o: f(QE[:, pr, :], o[:, 0:T], ACT.Sqrt, bias=c_("eps")))
                tell(root_ready)
                act.dma_start(O["fin"][bass.ds(l, 1)].rearrange("l p n -> (l p) n"),
                              fin[:, :, :].rearrange("p a b -> p (a b)")).then_inc(fin_stored, 16)
                for b in range(4, 7):
                    mod_row(b)
                act.wait_ge(bias_wanted, 1).then_inc(bias_wanted, -1)
                for h in range(4):
                    for t in range(2):
                        for r2 in range(2):
                            src = A["rpb"][bass.ds(l, 1), h, :]
                            ap = bass.AP(tensor=src.tensor, offset=src.offset + (4 + 2 * t + r2) * 31 - 48,
                                         ap=[[1, 64], [31, 4], [1, 64]])
                            act.dma_start(raw[64 * r2:64 * r2 + 64, 2 * h + t, :].rearrange("p (a b) -> p a b", b=64), ap)\
                                .then_inc(bias_in, 16)
                for k in range(2):
                    act.wait_ge(root_wanted, 1).then_inc(root_wanted, -1)
                    f(small[:, 24:48], small[:, 0:24], ACT.Sqrt, bias=c_("eps"), scale=1.0 / HD).then_inc(root_ready, 1)
                    if k == 0:
                        mod_row(7)
                        tell(mod_rows_ready)
                act.wait_ge(kv_ready, 1).then_inc(kv_ready, -1)
                for name, c0, w in (("wk", 640, 128), ("wv", 768, 128), ("nk", 1152, 256), ("nv", 1408, 256)):
                    act.dma_start(O[name][bass.ds(l, 1)].rearrange("l p n -> (l p) n"), nat[:, 0, c0:c0 + w])\
                        .then_inc(kv_stored, 16)
                for b in range(8, 10):
                    mod_row(b)
                tell(mod_rows_ready)
                for t in range(NT):
                    for k in range(2):
                        empty(lambda o: f(qkT[:, 4 * k:4 * k + 4, P * t:P * t + P],
                                          o[:, :].rearrange("p (a b) -> p a b", b=P), ACT.Copy))
                tell(qkt_ready)

                def exps(i):
                    act.wait_ge(exp_wanted, 1).then_inc(exp_wanted, -1)
                    s, k = sP[i % 2], 8 * (i % 2)
                    for t, (c0, n) in enumerate(((0, P), (P, T), (P + T, T))):
                        f(s[:, c0:c0 + n], s[:, c0:c0 + n], ACT.Exp, bias=sbig[:, k + t:k + t + 1],
                          accum_out=sbig[:, 16 + k + t:16 + k + t + 1])
                    f(sbig[:, 32 + k:32 + k + 3], sbig[:, k:k + 3], ACT.Exp, bias=s_("sink")[:, i:i + 1])
                    tell(exp_ready)

                def gates(two, u):
                    act.wait_ge(gb_free, 1).then_inc(gb_free, -1)
                    col = two[u // 2 % 2] * KC + 2 * (u // 4) + u % 2
                    empty(lambda o: f(gb[u % 2], o[:, 0:T], ACT.Sigmoid, bias=s_("bmg")[:, col:col + 1]))
                    tell(gb_ready)

                exps(0)
                for i in range(NH):
                    if i + 1 < NH:
                        exps(i + 1)
                    gates(PASSES[0], i)
                    empty(lambda o: f(pT[i % 2][:, 0:4, :], o[:, :].rearrange("p (a b) -> p a b", b=P), ACT.Copy))
                    empty(lambda o: f(pT[i % 2][:, 4:7, :], o[:, 0:T].rearrange("p (a b) -> p a b", b=P), ACT.Copy))
                    tell(pt_ready)
                    tell(s_free)
                    yc, op = head_place(i)[6:]
                    empty(lambda o: f(yT[op:op + 64, yc, :], o[op:op + 64, 0:T], ACT.Copy))
                tell(ya_ready)
                for u in range(NH, UNITS):
                    gates(PASSES[0], u)
                for u in range(UNITS):
                    gates(PASSES[1], u)
                square(lambda: mod_row(10))
                mod_row(11)
                tell(mod_rows_ready)
                empty(lambda o: f(sc[:, :, :], o[:, 0:NT * NE].rearrange("p (a b) -> p a b", b=NE), ACT.Sigmoid))
                tell(sc_ready)
                for t in range(NT):
                    for g in range(2):
                        empty(lambda o: f(hN[:, t, 512 * g:512 * g + 512], o[:, :], ACT.Copy))
                act.drain()
                act.dma_start(h2_d.rearrange("(t p) n -> p t n", p=P), hN[:, :, :]).then_inc(h2_stored, 16)
                a.restart()

                def silus(b):
                    act.wait_ge(hid_full[b], 1).then_inc(hid_full[b], -1)
                    f(si[b], vb[b][:, 0:DE], ACT.Silu).then_inc(si_ready, 1)

                def transposed(b):
                    empty(lambda o: f(aT[b], o[:, 0:DE].rearrange("p (a b) -> p a b", b=P), ACT.Copy))
                    tell(at_ready)

                def turned(b):
                    for g in range(2):
                        empty(lambda o: f(XT[b][:, 4 * g:4 * g + 4, :], o[:, :].rearrange("p (a b) -> p a b", b=P), ACT.Copy))
                    act.drain().then_inc(xt_ready, 1)
                    tell(xg_free)

                silus(0)
                for t in range(1, NT):
                    silus(t % 2)
                    transposed((t - 1) % 2)
                transposed((NT - 1) % 2)
                act.wait_ge(shared_ready, 1).then_inc(shared_ready, -1)
                act.dma_start(sum_d.rearrange("(t p) n -> p t n", p=P), acc).then_inc(shared_stored, 16)
                act.wait_ge(jobs_act, 1).then_inc(jobs_act, -1)
                a.restart()
                turned(0)
                with act.Fori(0, job_pairs(act)):
                    a.restart()
                    silus(0)
                    turned(1)
                    transposed(0)
                    silus(1)
                    turned(0)
                    transposed(1)
                act.sem_inc(xg_free, 1)
                act.wait_ge(routed_done, 1).then_inc(routed_done, -1)
                act.dma_start(acc, sum_d.rearrange("(t p) n -> p t n", p=P)).then_inc(acc_in, 16)

        @block.vector
        def _(dve):
            v = Cursor(range(NBANK))
            vec = nc.vector

            def settle():
                dve.drain()

            def tell(s):
                dve.drain().then_inc(s, 1)

            def empty(body):
                b = v.next()
                dve.wait_ge(vfull[b], 1).then_inc(vfull[b], -1)
                body(vb[b]).then_inc(vfree[b], 1)

            for b in range(NBANK):
                dve.sem_inc(vfree[b], 1)
            dve.sem_inc(layer_done, 1)
            dve.sem_inc(fin_stored, 16)
            for b in range(2):
                dve.sem_inc(gb_free, 1)
            vec.memset(mod_rows[:, :], 0.0)
            vec.memset(sbr[:, :, :], NEG)
            for b in range(2):
                dve.sem_inc(xg_free, 1)
                dve.sem_inc(yj_free, 1)
            dve.wait_ge(start_in, 32).then_inc(start_in, -32)
            for t in range(NT):
                vec.tensor_copy(entry[:, t, :, 0].bitcast(U32), c_("token")[:, t:t + 1].to_broadcast([P, TOPK]))
            tell(x_ready)
            with dve.Fori(0, DEPTH) as l:
                v.restart()
                vec.memset(uT[:, :, :], 0.0)
                vec.memset(table[:, :, 0].bitcast(I32), FAR)
                vec.memset(table[:, :, 1], 0.0)
                dve.wait_ge(params_in, 96).then_inc(params_in, -96)
                lbr = s_("lb").rearrange("p (a b) -> p a b", b=4)
                mx, e0, e1, su, c1, lbv = (lbw[:, k, :] for k in range(6))
                vec.tensor_tensor(mx, lbr[:, 0, :], lbr[:, 1, :], ALU.max)
                settle()
                vec.tensor_tensor(e0, lbr[:, 0, :], mx, ALU.subtract)
                vec.tensor_tensor(e1, lbr[:, 1, :], mx, ALU.subtract)
                tell(f_ready)
                dve.wait_ge(logf_ready, 1).then_inc(logf_ready, -1)
                vec.tensor_tensor(su, lbw[:, 1, :], lbw[:, 2, :], ALU.add)
                settle()
                vec.reciprocal(c1, su)
                settle()
                vec.tensor_tensor(e0, e0, c1, ALU.mult)
                vec.tensor_tensor(e1, e1, c1, ALU.mult)
                settle()
                vec.tensor_tensor(su, e0, e1, ALU.add)
                settle()
                vec.tensor_tensor(lb[:, 1, :], su, e0, ALU.subtract)
                vec.tensor_tensor(lb[:, 0, :], e0, e0, ALU.subtract)
                settle()
                vec.tensor_copy(lbl[:, 0, :], lb[:, bass.ds(l, 1), :].rearrange("p a b -> p (a b)"))
                settle()
                vec.tensor_scalar(lbl[:, 1, :], lbl[:, 0, :], -1.0, 1.0, ALU.mult, ALU.add)
                def modulated(b0, n):
                    def add(o):
                        rows = o[:, :].rearrange("p (n x) -> p n x", x=P)
                        for b in range(b0, b0 + n):
                            q, at = 32 * (b % 4), 4 * (b % 2)
                            bias = s_("bmod")[:, 8 * b:8 * b + 8].rearrange("p (a g) -> p a g", g=2)
                            last = vec.tensor_tensor(mT[:, b // 2, at:at + 4, :], rows[:, :, q:q + 2], bias, ALU.add)
                        return last
                    empty(add)

                def scales(k):
                    settle()
                    vec.scalar_tensor_tensor(modA[:, k, :, :], mT[:, 3 * k + 1, :, :], 1.0,
                                             s_(("g1", "g2")[k]).unsqueeze(2).to_broadcast([P, KC, 2]), ALU.add, ALU.mult)

                modulated(0, 4)
                scales(0)

                def norm(k):
                    dve.wait_ge(root_ready, 1).then_inc(root_ready, -1)
                    vec.reciprocal(rstd[:, :], rstd[:, :])
                    settle()
                    vec.tensor_tensor(hT[:, :, :], xT[:, :, :], rstd[:, :].unsqueeze(1).to_broadcast([P, KC, T]), ALU.mult)
                    settle()
                    for c in range(KC):
                        for g, (t0, t1) in enumerate(((0, P), (P, T))):
                            vec.tensor_scalar(hT[:, c, t0:t1], hT[:, c, t0:t1], modA[:, k, c, g:g + 1],
                                              mT[:, 3 * k, c, g:g + 1], ALU.mult, ALU.add)
                    tell(h_ready)

                norm(0)
                for t in range(NT):
                    empty(lambda o: vec.tensor_copy(nat[:, t, 0:256], o[:, 0:256]))
                tell(vproj_done)
                dve.wait_ge(gates_in, 1).then_inc(gates_in, -1)
                chunked = lambda x: x.rearrange("p a (c n) -> p (a c) n", n=CH)
                flat = lambda x: x.rearrange("p a n -> p (a n)")
                tot = small[:, 0:48]
                for r in range(2):
                    for pr in range(2):
                        vec.tensor_scalar(sig[r][:, pr, :], sig[r][:, pr, :], lbl[:, 1, 2 * r + pr:2 * r + pr + 1],
                                          lbl[:, 0, 2 * r + pr:2 * r + pr + 1], ALU.mult, ALU.add)
                    tell(f_ready)
                    dve.wait_ge(logf_ready, 1).then_inc(logf_ready, -1)
                    vec.tensor_scalar(sig[r][:, :, :], sig[r][:, :, :], -1.0, 1.0, ALU.mult, ALU.add)
                    vec.tensor_tensor_scan(flat(C), c_("first"), flat(L), 0.0, ALU.mult, ALU.add)
                    settle()
                    vec.tensor_copy(tot, chunked(C)[:, :, CH - 1])
                    settle()
                    totb = tot.unsqueeze(2).to_broadcast([P, 2 * NCH, CH])
                    if r == 1:
                        vec.tensor_tensor(C, L, C, ALU.subtract)
                        settle()
                        vec.tensor_tensor(chunked(C), chunked(C), totb, ALU.add)
                        settle()
                    mid = CH // 2 - 1 + r
                    vec.tensor_tensor(chunked(DD), chunked(C), chunked(C)[:, :, mid:mid + 1].to_broadcast([P, 2 * NCH, CH]),
                                      ALU.subtract)
                    vec.tensor_tensor(chunked(L), totb, chunked(C), ALU.subtract)
                    settle()
                    vec.tensor_scalar(DD, DD, 80.0, -80.0, ALU.min, ALU.max)
                    tell(exps_wanted)
                    dve.wait_ge(exps_ready, 1).then_inc(exps_ready, -1)
                    vec.tensor_tensor(L, L, sig[r][:, :, :], ALU.mult)
                    vec.tensor_tensor(QE, QE, qT[:, :, :], ALU.mult)
                    vec.tensor_tensor(KE, KE, sig[r][:, :, :], ALU.mult)
                    vec.tensor_tensor(QX, QX, qT[:, :, :], ALU.mult)
                    tell(rec_ready)
                    for t in range(NT):
                        empty(lambda o: vec.tensor_copy(kdN[:, t, :], o[:, 0:256]))
                    tell(kdn_ready)
                    for base, n, src in ((0, 8, None), (9, 16, s0)):
                        row = base + (n if r else 0)
                        if src is None:
                            vec.memset(S[:, :, row, :], 0.0)
                        else:
                            vec.tensor_copy(S[:, :, row, :], s0[:, 2 * r:2 * r + 2, :])
                    for t in ((0, 1, 2), (0, 2, 1))[r]:
                        for h in range(4):
                            vec.tensor_tensor(VX[:, h, :].rearrange("p (c v) -> p c v", v=HD),
                                              nat[:, t, 64 * h:64 * h + 64].unsqueeze(1).to_broadcast([P, TC, HD]),
                                              c_("chunk").unsqueeze(2).to_broadcast([P, TC, HD]), ALU.mult)
                        tell(vx_ready)
                        b0, b1 = v.next(), v.next()
                        dve.wait_ge(vfull[b0], 1).then_inc(vfull[b0], -1)
                        dve.wait_ge(vfull[b1], 1).then_inc(vfull[b1], -1)
                        order = range(TC) if r == 0 else range(TC - 1, -1, -1)
                        for c in order:
                            row = TC * t + c + (t > 0)
                            for pr, b in ((0, b0), (1, b1)):
                                last = vec.scalar_tensor_tensor(
                                    S[:, pr, row + 1 - r, :], S[:, pr, row + r, :],
                                    tot[:, NCH * pr + TC * t + c:NCH * pr + TC * t + c + 1],
                                    vb[b][:, HD * c:HD * c + HD], ALU.mult, ALU.add)
                            settle()
                        dve.sem_inc(vfree[b0], 1)
                        dve.sem_inc(vfree[b1], 1)
                    if r == 0:
                        dve.wait_ge(fin_stored, 16).then_inc(fin_stored, -16)
                    vec.tensor_copy(fin[:, 2 * r:2 * r + 2, :], S[:, :, 0 if r else TC, :])
                    tell(states_ready)
                    if r == 1:
                        tell(fin_ready)
                    for t in range(NT):
                        for h2 in range(2):
                            m = c_("mask1" if r else "mask0")
                            empty(lambda o: vec.tensor_tensor(attS[:, h2:4:2, :], o[:, 0:256].rearrange("p (a b) -> p a b", b=P),
                                                              m.unsqueeze(1).to_broadcast([P, 2, P]), ALU.mult))
                        tell(att_ready)
                        dst = oT[:, :, P * t:P * t + P]
                        if r == 0:
                            empty(lambda o: vec.tensor_copy(dst, o[:, 0:256].rearrange("p (a b) -> p a b", b=P)))
                        else:
                            empty(lambda o: vec.tensor_tensor(dst, o[:, 0:256].rearrange("p (a b) -> p a b", b=P), dst, ALU.add))
                tell(o_ready)
                dve.wait_ge(proj_done, 1).then_inc(proj_done, -1)
                dve.wait_ge(root_ready, 1).then_inc(root_ready, -1)
                vec.reciprocal(QE, QE)
                settle()
                for pr in range(2):
                    vec.scalar_tensor_tensor(oT[:, pr, :], oT[:, pr, :], s_("onorm"), QE[:, pr, :], ALU.mult, ALU.mult)
                    settle()
                    vec.tensor_tensor(yT[:, pr, :], oT[:, pr, :], gT[:, pr, :], ALU.mult)
                    settle()
                for dst, src, h, lo, hi in ((s2, uT[:, :, :], None, 1, PADU), (s4, s2, 1, 2, PADU - 1),
                                            (s8, s4, 2, 4, PADU - 3), (s16, s8, 4, 8, PADU - 7)):
                    if h is None:
                        vec.tensor_tensor(dst[:, :, lo:hi], src[:, :, lo - 1:hi - 1], src[:, :, lo:hi], ALU.add)
                    else:
                        vec.tensor_tensor(dst[:, :, lo:hi], src[:, :, lo - h:hi - h], src[:, :, lo + h:hi + h], ALU.add)
                    settle()
                inv = c_("inv").rearrange("p (a b) -> p a b", b=PADU)
                lo, hi = 8, PADU - 8
                for g, s in enumerate((s2, s4, s8, s16)):
                    q = slice(64 * (g % 2), 64 * (g % 2) + 64)
                    vec.tensor_tensor(pl[q, g // 2, lo:hi], s[q, g // 2, lo:hi], inv[q, g // 2, lo:hi], ALU.mult)
                settle()
                vec.tensor_tensor(pl[:, :, lo:hi], pl[:, :, lo:hi], uT[:, :, lo:hi], ALU.subtract)
                tell(pooled_ready)
                for k in range(2):
                    empty(lambda o: vec.tensor_scalar(yT[:, 5 + k, :], o[:, 0:T], s_("pscale")[:, k:k + 1], None, ALU.mult))
                tell(yv_ready)
                tell(bias_wanted)
                for c0, qn, kn, nq in ((256, "wqn", "wkn", 6), (896, "nqn", "nkn", 4)):
                    X = nat[:, :, c0:c0 + 512]
                    t3 = tmp.rearrange("p (a b) -> p a b", b=512)
                    vec.tensor_tensor(t3, X, X, ALU.mult)
                    settle()
                    vec.reduce_sum(small[:, 0:24], tmp.rearrange("p (a b) -> p a b", b=HD), axis=AX.X)
                    tell(root_wanted)
                    dve.wait_ge(root_ready, 1).then_inc(root_ready, -1)
                    vec.reciprocal(small[:, 24:48], small[:, 24:48])
                    settle()
                    for t in range(NT):
                        Xt = X[:, t, :].rearrange("p (h d) -> p h d", d=HD)
                        vec.tensor_tensor(Xt, Xt, small[:, 24 + 8 * t:32 + 8 * t].unsqueeze(2).to_broadcast([P, 8, HD]),
                                          ALU.mult)
                    settle()
                    for t in range(NT):
                        Xt = X[:, t, :].rearrange("p (h d) -> p h d", d=HD)
                        for h0, h1, g in ((0, nq, qn), (nq, 8, kn)):
                            vec.tensor_tensor(Xt[:, h0:h1, :], Xt[:, h0:h1, :],
                                              s_(g).unsqueeze(1).to_broadcast([P, h1 - h0, HD]), ALU.mult)
                    settle()
                tell(kv_ready)
                for t in range(NT):
                    X = nat[:, t, 256:768]
                    if t > 0:
                        R = tmp[:, 0:512]
                        R2 = tmp[:, 512:1024]
                        vec.tensor_tensor(R.rearrange("p (h d) -> p h d", d=HD), X.rearrange("p (h d) -> p h d", d=HD),
                                          c_("cos")[:, HD * (t - 1):HD * t].unsqueeze(1).to_broadcast([P, 8, HD]), ALU.mult)
                        xv = X.rearrange("p (h a q) -> p h a q", a=4, q=16)
                        rv = R2.rearrange("p (h a q) -> p h a q", a=4, q=16)
                        sv = c_("sin")[:, HD * (t - 1):HD * t].rearrange("p (a q) -> p a q", q=16)
                        for k in range(4):
                            vec.tensor_tensor(rv[:, :, k, :], xv[:, :, k ^ 1, :],
                                              sv[:, k, :].unsqueeze(1).to_broadcast([P, 8, 16]), ALU.mult)
                        settle()
                        vec.tensor_tensor(R, R, R2, ALU.add)
                        settle()
                        X = R
                    vec.tensor_copy(qkr[:, t, 0:384].rearrange("p (j g d) -> p g j d", g=2, d=HD),
                                    X[:, 0:384].rearrange("p (g j d) -> p g j d", g=2, d=HD))
                    vec.tensor_copy(qkr[:, t, 384:512], X[:, 384:512])
                    settle()
                tell(qk_ready)
                modulated(4, 4)
                modulated(8, 2)
                scales(1)
                dve.wait_ge(bias_in, 256).then_inc(bias_in, -256)
                nm = c_("nmask").unsqueeze(1).to_broadcast([P, 4, HD])
                for ht in range(8):
                    vec.tensor_tensor(biasD[:, ht, 0:256].rearrange("p (a b) -> p a b", b=HD),
                                      raw[:, ht, ::-1].rearrange("p (a b) -> p a b", b=HD), nm, ALU.add)
                vec.memset(biasD[:, :, 256:T], 0.0)
                settle()
                wm = c_("wmask").rearrange("p (a b) -> p a b", b=T)

                def scaled(i):
                    if i >= 2:
                        dve.wait_ge(s_free, 1).then_inc(s_free, -1)
                    s, k = sP[i % 2], 8 * (i % 2)
                    empty(lambda o: vec.tensor_scalar(s[:, 0:P], o[:, 0:P], SCALE, None, ALU.mult))
                    for t in (1, 2):
                        add = wm[:, t - 1, :] if i < 6 else biasD[:, 2 * (i - 6) + t - 1, :]
                        c0 = P + T * (t - 1)
                        empty(lambda o: vec.scalar_tensor_tensor(s[:, c0:c0 + T], o[:, 0:T], SCALE, add, ALU.mult, ALU.add))
                    settle()
                    vec.reduce_max(sbig[:, k + 3:k + 4], s[:, 0:P], axis=AX.X)
                    vec.reduce_max(sbig[:, k + 4:k + 6], s[:, P:896].rearrange("p (a b) -> p a b", b=T), axis=AX.X)
                    settle()
                    vec.tensor_scalar(sbig[:, k:k + 3], sbig[:, k + 3:k + 6], s_("sink")[:, i:i + 1], -1.0, ALU.max, ALU.mult)
                    tell(exp_wanted)

                def normalised(i):
                    dve.wait_ge(exp_ready, 1).then_inc(exp_ready, -1)
                    s, k = sP[i % 2], 8 * (i % 2)
                    vec.tensor_tensor(sbig[:, 48:51], sbig[:, 16 + k:19 + k], sbig[:, 32 + k:35 + k], ALU.add)
                    settle()
                    vec.reciprocal(sbig[:, 52:55], sbig[:, 48:51])
                    settle()
                    for t, (c0, n) in enumerate(((0, P), (P, T), (P + T, T))):
                        vec.tensor_scalar(s[:, c0:c0 + n], s[:, c0:c0 + n], sbig[:, 52 + t:53 + t], None, ALU.mult)
                    tell(p_ready)

                def gated(p, u):
                    m, g = merged[:, 2 * (u // 4) + u % 2, :], gb[u % 2]
                    dve.wait_ge(gb_ready, 1).then_inc(gb_ready, -1)
                    if p == 0 and u // 2 % 2 == 0:
                        empty(lambda o: vec.tensor_tensor(m, o[:, 0:T], g, ALU.mult))
                    else:
                        empty(lambda o: vec.tensor_tensor(g, o[:, 0:T], g, ALU.mult))
                        settle()
                        vec.tensor_tensor(m, m, g, ALU.add)
                    tell(gb_free)

                scaled(0)
                for i in range(NH):
                    if i + 1 < NH:
                        scaled(i + 1)
                    normalised(i)
                    gated(0, i)
                dve.wait_ge(s_free, 1).then_inc(s_free, -1)
                dve.wait_ge(s_free, 1).then_inc(s_free, -1)
                for u in range(NH, UNITS):
                    gated(0, u)
                for u in range(UNITS):
                    gated(1, u)
                tell(merged_ready)

                def residual(s):
                    for c in range(KC):
                        def add(o):
                            vec.scalar_tensor_tensor(xT[:, c, 0:P], o[:, 0:P], mT[:, s, c, 0:1], xT[:, c, 0:P],
                                                     ALU.mult, ALU.add)
                            return vec.scalar_tensor_tensor(xT[:, c, P:T], o[:, P:T], mT[:, s, c, 1:2], xT[:, c, P:T],
                                                            ALU.mult, ALU.add)
                        empty(add)
                    tell(x_ready)

                residual(2)
                norm(1)
                modulated(10, 2)
                dve.wait_ge(sc_ready, 1).then_inc(sc_ready, -1)
                vec.tensor_tensor(sbr[:, :, 0:NE], sc[:, :, :], s_("brout").unsqueeze(1).to_broadcast([P, NT, NE]), ALU.add)
                settle()
                for t in range(NT):
                    vec.max(top8[:, t, :], sbr[:, t, :])
                settle()
                vec.memset(top8[:, :, TOPK:8], NEG)
                settle()
                for t in range(NT):
                    vec.match_replace(rep[:, t, :], top8[:, t, :], sbr[:, t, :], -3e38)
                settle()
                vec.tensor_scalar(chosen[:, :, :], rep[:, :, 0:NE], -2e30, None, ALU.is_lt)
                tell(chosen_ready)
                vec.scalar_tensor_tensor(gate[:, :, :], rep[:, :, 0:NE], -2e30, sc[:, :, :], ALU.is_lt, ALU.mult)
                settle()
                vec.reduce_sum(small[:, 48:51], gate[:, :, :], axis=AX.X)
                settle()
                vec.reciprocal(small[:, 52:55], small[:, 48:51])
                settle()
                for t in range(NT):
                    vec.tensor_scalar(gate[:, t, :], gate[:, t, :], small[:, 52 + t:53 + t], ROUTED_SCALE, ALU.mult, ALU.mult)
                b = v.next()
                dve.wait_ge(vfull[b], 1).then_inc(vfull[b], -1)
                cnt = vb[b][:, NT * NE:NT * NE + NE]
                pos = vb[b][:, 0:NT * NE].rearrange("p (a b) -> p a b", b=NE)
                vec.tensor_scalar(nblk[:, :], cnt, 1.0, None, ALU.is_ge)
                vec.tensor_scalar(place[:, :, :], pos, float(P), 1.0 - P * NJ, ALU.is_ge, ALU.mult)
                vec.tensor_scalar(rep[:, :, 0:NE], pos, 2.0 * P, 1.0 - P * NJ, ALU.is_ge, ALU.mult)
                settle()
                for k in (1, 2):
                    vec.scalar_tensor_tensor(nblk[:, :], cnt, k * P + 1.0, nblk[:, :], ALU.is_ge, ALU.add)
                    settle()
                vec.tensor_tensor_scan(incl[:, :], c_("ones")[:, 0:NE], nblk[:, :], 0.0, ALU.mult, ALU.add)
                vec.tensor_tensor(place[:, :, :], place[:, :, :], rep[:, :, 0:NE], ALU.add)
                settle()
                vec.scalar_tensor_tensor(place[:, :, :], pos, float(NJ), place[:, :, :], ALU.mult, ALU.add)
                vec.scalar_tensor_tensor(first_job[:, :], incl[:, :], 1.0, nblk[:, :], ALU.add, ALU.subtract)
                settle()
                dve.sem_inc(vfree[b], 1)
                vec.tensor_tensor(place[:, :, :], place[:, :, :], first_job[:, :].unsqueeze(1).to_broadcast([P, NT, NE]),
                                  ALU.add)
                settle()
                vec.tensor_tensor(place[:, :, :], place[:, :, :], chosen[:, :, :], ALU.mult)
                settle()
                for t in range(NT):
                    vec.max(top_place[:, t, :], place[:, t, :])
                settle()
                vec.tensor_scalar(place_u[:, :].rearrange("p (a b) -> p a b", b=TOPK), top_place[:, :, 0:TOPK], -1.0, None,
                                  ALU.add)
                for t in range(NT):
                    e3 = eq[:, TOPK * NE * t:TOPK * NE * (t + 1)].rearrange("p (a b) -> p a b", b=NE)
                    vec.tensor_tensor(e3, place[:, t, :].unsqueeze(1).to_broadcast([P, TOPK, NE]),
                                      top_place[:, t, 0:TOPK].unsqueeze(2).to_broadcast([P, TOPK, NE]), ALU.is_equal)
                settle()
                for t in range(NT):
                    e3 = eq[:, TOPK * NE * t:TOPK * NE * (t + 1)].rearrange("p (a b) -> p a b", b=NE)
                    vec.tensor_tensor(e3, e3, gate[:, t, :].unsqueeze(1).to_broadcast([P, TOPK, NE]), ALU.mult)
                settle()
                vec.reduce_sum(entry[:, :, :, 1], eq.rearrange("p (t a b) -> p t a b", a=TOPK, b=NE), axis=AX.X)
                tell(entries_ready)
                vec.tensor_tensor(cmp, incl[0:1, :].unsqueeze(1).to_broadcast([1, NJ, NE]),
                                  c_("jobs")[0:1, :].unsqueeze(2).to_broadcast([1, NJ, NE]), ALU.is_le)
                settle()
                vec.reduce_sum(small[0:1, 0:NJ], cmp, axis=AX.X)
                settle()
                vec.tensor_scalar(job_expert[:, :], small[0:1, 0:NJ], NE - 1.0, None, ALU.min)
                vec.tensor_scalar(sbig[0:1, 0:NJ // 2], c_("jobs")[0:1, 0:NJ:2], incl[0:1, NE - 1:NE], None, ALU.is_lt)
                settle()
                vec.reduce_sum(sbig[0:1, 60:61], sbig[0:1, 0:NJ // 2], axis=AX.X)
                settle()
                vec.tensor_copy(job_count[:, 0:1], sbig[0:1, 60:61])
                tell(jobs_sp)
                tell(jobs_pool)
                tell(jobs_pe)
                tell(jobs_act)
                dve.wait_ge(kv_stored, 64).then_inc(kv_stored, -64)

                def weighted(b, g):
                    dve.wait_ge(si_ready, 1).then_inc(si_ready, -1)
                    vec.scalar_tensor_tensor(aa[b], vb[b][:, DE:2 * DE], g, si[b], ALU.mult, ALU.mult)\
                        .then_inc(vfree[b], 1)
                    tell(a_ready)

                def out_rows(dst):
                    for n in range(2):
                        dve.wait_ge(vfull[2 + n], 1).then_inc(vfull[2 + n], -1)
                        vec.tensor_copy(dst[:, 512 * n:512 * n + 512], vb[2 + n][:, :]).then_inc(vfree[2 + n], 1)

                weighted(0, 1.0)
                for t in range(1, NT):
                    weighted(t % 2, 1.0)
                    out_rows(acc[:, t - 1, :])
                out_rows(acc[:, NT - 1, :])
                tell(shared_ready)
                dve.wait_ge(table_ready, 1).then_inc(table_ready, -1)
                with dve.Fori(0, job_pairs(dve)) as j:
                    for k in range(2):
                        weighted(k, table[:, bass.ds(2 * j + k, 1), 1])
                    for b in range(2):
                        dve.wait_ge(yj_free, 1).then_inc(yj_free, -1)
                        out_rows(Y[b])
                        tell(yj_ready)
                v.restart()
                residual(5)
                tell(layer_done)
            tell(y_ready)
            dve.wait_ge(fin_stored, 16).then_inc(fin_stored, -16)


_OUTS = [("yT", (P, KC, T)), ("wk", (DEPTH, P, 128)), ("wv", (DEPTH, P, 128)), ("nk", (DEPTH, P, 256)),
         ("nv", (DEPTH, P, 256)), ("fin", (DEPTH, P, 256))]


def constants():
    import numpy as np

    con = np.zeros((P, CNW), np.float32)

    def put(name, x):
        con[:, CN[name][0]:CN[name][1]] = np.asarray(x, np.float32).reshape(P, -1)

    i = np.arange(P)
    put("ident", np.eye(P))
    put("blk64", (i[:, None] // 64 == i[None] // 64) / 64.0)
    same = i[:, None] // CH == i[None] // CH
    put("mask0", same & (i[:, None] <= i[None]))
    put("mask1", same & (i[:, None] >= i[None]))
    put("chunk", i[:, None] // CH == np.arange(TC)[None])
    put("first", np.broadcast_to(np.arange(2 * T) % CH != 0, (P, 2 * T)))
    qc = i % 64
    start = np.clip(qc - 8, 0, 48)[:, None]
    kc = np.arange(64)[None]
    put("nmask", np.where((kc >= start) & (kc < start + 16), 0.0, NEG))
    wm = np.zeros((P, 2, T), np.float32)
    qp = i[:, None] + P * np.arange(2)[None]
    wm[:, :, 0:256] = np.where(np.abs(np.arange(256)[None, None] - qp[:, :, None]) <= 128, 0.0, NEG)
    put("wmask", wm)
    t = np.arange(256)
    inv = (10000.0 ** (-np.arange(16) / 16)).astype(np.float32)
    cos = np.zeros((256, 4, 16), np.float32)
    sin = np.zeros((256, 4, 16), np.float32)
    for half, pos in enumerate((t // 64, t % 64)):
        ang = pos.astype(np.float32)[:, None] * inv[None]
        cos[:, 2 * half] = cos[:, 2 * half + 1] = np.cos(ang)
        sin[:, 2 * half], sin[:, 2 * half + 1] = -np.sin(ang), np.sin(ang)
    put("cos", cos.reshape(2, P, 64).transpose(1, 0, 2))
    put("sin", sin.reshape(2, P, 64).transpose(1, 0, 2))
    cnt = np.zeros((4, PADU), np.float32)
    for g, size in enumerate((2, 4, 8, 16)):
        for at, n in ((8, P), (152, 256)):
            pos = np.arange(n)
            cnt[g, at:at + n] = 1.0 / (np.clip(pos + size // 2, 0, n) - np.clip(pos - size // 2, 0, n))
    both = np.zeros((P, 2, PADU), np.float32)
    for g in range(4):
        both[64 * (g % 2):64 * (g % 2) + 64, g // 2] = cnt[g]
    put("inv", both)
    put("eps", np.full((P, 1), EPS))
    put("before", i[:, None] < i[None])
    put("ones", np.ones((P, P)))
    put("jobs", np.broadcast_to(np.arange(NJ), (P, NJ)))
    put("token", i[:, None] + P * np.arange(NT)[None])
    return con


def kernel(**inputs):
    import numpy as np
    import concourse.bacc as bacc
    from concourse.bass_utils import run_bass_kernel_spmd as run

    a = {k: np.asarray(v) for k, v in inputs.items()}
    L_ = DEPTH

    def pc(x):
        return x.reshape(x.shape[:-1] + (P, KC))

    def cp(x):
        return np.swapaxes(x.reshape(x.shape[:-1] + (-1, P)), -1, -2)

    def rows(x):
        return np.broadcast_to(x[:, None, :], (L_, P, x.shape[-1]))

    x = np.concatenate([a["x_prompt"][0], a["x_sample"][0]], axis=0)
    h = {"con": constants(),
         "xT": np.transpose(pc(x), (1, 2, 0)),
         "cT": np.stack([pc(a["c_ctx"]), pc(a["c"][0])], axis=-1)}
    wm = a["w_mod"].reshape(L_, D, 6, P, KC)
    h["w_mod"] = np.swapaxes(wm, -1, -2).reshape(L_, D, 6 * D)
    bm = a["b_mod"].reshape(L_, 6, P, KC).transpose(0, 2, 1, 3)
    sink = np.concatenate([a["win_sink"], np.full((L_, 4), NEG, np.float32)], axis=1)
    h["sm"] = np.concatenate([
        pc(a["norm1_g"]), pc(a["norm2_g"]),
        np.repeat(bm.reshape(L_, P, 48), 2, axis=-1),
        cp(a["b_mgate"]),
        np.tile(a["hg_onorm"], (1, 2))[:, :, None],
        cp(a["pool_scale"]),
        rows(a["b_router"]), rows(a["win_qn"]), rows(a["win_kn"]), rows(a["na_qn"]), rows(a["na_kn"]), rows(sink),
        np.broadcast_to(cp(a["hg_lb"]).transpose(2, 0, 1, 3).reshape(1, P, 8), (L_, P, 8)),
    ], axis=2)
    kw = a["cache_win_k"][0].transpose(0, 2, 3, 1).reshape(L_, P, P)
    kn = a["cache_na_k"][0].transpose(0, 2, 3, 1).reshape(L_, 2, P, P).transpose(0, 2, 1, 3).reshape(L_, P, 256)
    h["kcT"] = np.concatenate([kw, kn], axis=2)
    h["vc"] = np.concatenate([a["cache_win_v"][0].reshape(L_, P, P), a["cache_na_v"][0].reshape(L_, P, 256)], axis=2)
    h["s0"] = a["state_hgrn"][0].reshape(L_, 2, 2, 2, HD, HD).transpose(0, 3, 4, 1, 2, 5).reshape(L_, P, 256)
    h["poolw"] = a["pool_w"].reshape(L_, 2, 2, HD, HD).transpose(0, 2, 3, 1, 4).reshape(L_, P, P)
    h["rpb"] = a["na_rpb"][:, :, ::-1, ::-1].reshape(L_, 4, 465)
    for k in ("w_in", "w_mgate", "w_branch", "w_out", "w_router", "w_sg", "w_su", "w_sd"):
        h[k] = a[k]
    for k in ("w_eg", "w_eu", "w_ed"):
        h[k] = a[k].reshape((L_ * NE,) + a[k].shape[2:])

    nc = bacc.Bacc("TRN2", target_bir_lowering=False, num_devices=1)
    arrays, A, O = {}, {}, {}
    for k, arr in h.items():
        arr = np.ascontiguousarray(arr)
        arrays["in_" + k] = arr
        A[k] = nc.dram_tensor("in_" + k, arr.shape, mybir.dt.from_np(arr.dtype), kind="ExternalInput").ap()
    for k, shape in _OUTS:
        O[k] = nc.dram_tensor("out_" + k, shape, F32, kind="ExternalOutput").ap()
    build(nc, A, O)
    r = run(nc, [arrays], core_ids=[0]).results[0]
    o = {k: r["out_" + k] for k, _ in _OUTS}
    y = np.transpose(o["yT"], (2, 0, 1)).reshape(T, D)
    fin = o["fin"].reshape(L_, 2, HD, 2, 2, HD).transpose(0, 3, 4, 1, 2, 5).reshape(1, L_, 2, 4, HD, HD)
    return (y[None, 0:P], y[None, P:T],
            o["wk"].reshape(1, L_, P, 2, HD), o["wv"].reshape(1, L_, P, 2, HD),
            o["nk"].reshape(1, L_, P, 4, HD), o["nv"].reshape(1, L_, P, 4, HD), fin)
```

```python
import concourse.bass as bass
from concourse import mybir
from contextlib import ExitStack

F32 = mybir.dt.float32
ALU = mybir.AluOpType
ACT = mybir.ActivationFunctionType
AX = mybir.AxisListType

P = 128
D = 1024
KC = D // P
T = 384
NT = T // P
DEPTH = 2
HD = 64
SCALE = HD ** -0.5
EPS = 1e-6
NEG = -1e30
CH = 16
TC = P // CH
NCH = T // CH
NH = 10
NE = 32
DE = 256
TOPK = 4
ROUTED_SCALE = 2.5
SLOT = KC * 512
NSLOT = 4
NJ = 48
FAR = 1 << 20
U32 = mybir.dt.uint32
I32 = mybir.dt.int32
NBANK = 4
PADU = 416
NATW = 1664
SROW = 26

SM = {}
_at = 0
for _n, _w in (("g1", 8), ("g2", 8), ("bmod", 96), ("bmg", 32), ("onorm", 1), ("pscale", 2), ("brout", 32),
               ("wqn", 64), ("wkn", 64), ("nqn", 64), ("nkn", 64), ("sink", NH), ("lb", 8)):
    SM[_n] = (_at, _at + _w)
    _at += _w
SMW = _at
CN = {}
_at = 0
for _n, _w in (("ident", 128), ("blk64", 128), ("mask0", 128), ("mask1", 128), ("chunk", TC),
               ("first", 2 * T), ("nmask", HD), ("wmask", 2 * T), ("cos", 2 * HD), ("sin", 2 * HD),
               ("inv", 2 * PADU), ("eps", 1),
               ("before", P), ("ones", P), ("jobs", NJ), ("token", NT)):
    CN[_n] = (_at, _at + _w)
    _at += _w
CNW = _at




class Cursor:

    def __init__(self, order):
        self.order, self.at = order, 0

    def next(self):
        i = self.order[self.at]
        self.at = (self.at + 1) % len(self.order)
        return i

    def restart(self):
        self.at = 0


SLOT_ORDER = (2, 3, 0, 1) * 4 + 2 * (2, 3, 0, 1, 3, 0) + (2, 3, 0, 1) + (2, 3)
JOB_SLOTS = ((0, 1), (2, 3))


def head_place(i):
    if i < 6:
        g = i // 3
        return i % 3, 3, 0, 64 * g, 768 + 64 * g, 64 * g, 2 + i // 2, 64 * (i % 2)
    h = i - 6
    return 4 + h // 2, 6 + h // 2, 1 + h // 2, 64 * (h % 2), 1408 + 64 * h, 128 + 64 * h, 7 + h // 2, 64 * (h % 2)


BRANCH_CHUNKS = ((0, 1), (2, 3, 4), (5, 6), (7, 8))
PASSES = ((0, 2), (1, 3))
UNITS = 2 * KC

PROJ = [[(1, 0, 128), (1, 128, 128), (1, 256, 128), (1, 384, 128)],
        [(1, 512, 128), (1, 640, 128), (0, 768, 256)],
        [(1, 1024, 128), (1, 1152, 128), (0, 1280, 256)],
        [(0, 1536, 384), (1, 1920, 128)],
        [(1, 2048, 128), (0, 2176, 384)],
        [(0, 2560, 384)]]


GROUPS = [(b, tr, c0, n, t) for b, groups in enumerate(PROJ) for tr, c0, n in groups
          for t in ((None,) if tr else range(NT))]
EARLY = sum(g[0] < 2 for g in GROUPS)
LATE = (len(GROUPS) - EARLY) // 2


def nat_col(c):
    if c < 1024:
        return c - 768
    return c - 1280 + 256 if c < 1920 else c - 2176 + 896


def build(nc, A, O):
    ctx = ExitStack()
    with ctx:
        def sb(name, shape):
            return ctx.enter_context(nc.sbuf_tensor(name, shape, F32))

        def sem(name):
            return ctx.enter_context(nc.semaphore(name))

        slots = [sb(f"slot{i}", [P, SLOT]) for i in range(NSLOT)]
        xT = sb("xT", [P, KC, T])
        hT = sb("hT", [P, KC, T])
        nat = sb("nat", [P, NT, NATW])
        merged = sb("merged", [P, KC, T])
        qT, gT = merged[:, 0:2, :], merged[:, 6:8, :]
        sig = [merged[:, 2:4, :], merged[:, 4:6, :]]
        mod_rows = sb("mod_rows", [P, 512])
        uT = sb("uT", [P, 2, PADU])
        yT = sb("yT", [P, 9, T])
        con = sb("con", [P, CNW])
        sm = sb("sm", [P, SMW])
        kcT = sb("kcT", [P, 3, P])
        vc = sb("vc", [P, T])
        s0 = sb("s0", [P, 4, HD])
        fin = sb("fin", [P, 4, HD])
        poolw = sb("poolw", [P, 2, HD])
        wr = sb("wr", [P, KC, NE])
        scT = sb("scT", [P, KC, 2])
        mT = sb("mT", [P, 6, KC, 2])
        modA = sb("modA", [P, 2, KC, 2])
        rstd = sig[1][:, 0, :]
        lb = sb("lb", [P, DEPTH, 4])
        lbw = sb("lbw", [P, 8, 4])
        lbl = sb("lbl", [P, 2, 4])
        small = sb("small", [P, 64])
        sbig = sb("softmax_small", [P, 64])
        lease = [0]

        def moe(*shape):
            n = shape[0] * (shape[1] if len(shape) > 1 else 1)
            x = sig[0][:, :, :].rearrange("p a b -> p (a b)")[:, lease[0]:lease[0] + n]
            lease[0] += n
            assert lease[0] <= 2 * T
            return x if len(shape) == 1 else x.rearrange("p (a b) -> p a b", b=shape[1])

        sc = moe(NT, NE)
        sbr = sb("sbr", [P, NT, NE + TOPK])
        rep = moe(NT, NE + TOPK)
        top8 = moe(NT, 8)
        gate = moe(NT, NE)
        def ib(name, shape, dt):
            return ctx.enter_context(nc.sbuf_tensor(name, shape, dt))

        chosen = moe(NT, NE)
        place = moe(NT, NE)
        nblk = moe(NE)
        incl = moe(NE)
        first_job = moe(NE)
        top_place = moe(NT, 8)
        place_u = ib("place_u", [P, NT * TOPK], U32)
        entry = ib("entry", [P, NT, TOPK, 2], F32)
        table = ib("table", [P, NJ, 2], F32)
        job_expert = ib("job_expert", [1, NJ], I32)
        job_count = ib("job_count", [1, 3], I32)
        rows_of = [ib(f"rows_of{i}", [P, 2], F32) for i in range(2)]
        sums_of = ib("sums_of", [P, 2], F32)
        table_d = nc.dram_tensor("job_table", [P * NJ, 2], F32, kind="Internal").ap()
        h2_d = nc.dram_tensor("h2_rows", [T, D], F32, kind="Internal").ap()
        sum_d = nc.dram_tensor("expert_sums", [T, D], F32, kind="Internal").ap()
        arena = sb("arena", [P, 11520])
        used = [0]

        def new_phase():
            used[0] = 0

        def ar(*shape):
            n = 1
            for s in shape:
                n *= s
            a = arena[:, used[0]:used[0] + n]
            used[0] += n
            assert used[0] <= 11520, used[0]
            if len(shape) == 2:
                return a.rearrange("p (a b) -> p a b", b=shape[1])
            if len(shape) == 3:
                return a.rearrange("p (a b c) -> p a b c", b=shape[1], c=shape[2])
            return a

        QE, KE, QX, L, C, DD = (ar(2, T) for _ in range(6))
        S = ar(2, SROW, HD)
        kdN = ar(NT, 256)
        VX = ar(4, TC * HD)
        attS = VX[:, 0, :].rearrange("p (a b) -> p a b", b=P)
        oT = ar(2, T)
        new_phase()
        ar(2, T)
        s2, s4, s8 = (ar(2, PADU) for _ in range(3))
        s16 = s2
        pl = arena[:, 9728:9728 + 2 * PADU].rearrange("p (a b) -> p a b", b=PADU)
        new_phase()
        qkr = ar(NT, 512)
        qkT = ar(8, T)
        biasD = ar(8, T)
        sP = [ar(896), ar(896)]
        pT = [ar(7, P), ar(7, P)]
        raw = arena[:, used[0] - 3584:used[0] - 3584 + 2048].rearrange("p (a b) -> p a b", b=256)
        tmp = arena[:, used[0] - 1536:used[0]]
        head_sq = biasD.rearrange("p a b -> p (a b)").rearrange("p (k n) -> p k n", k=2)
        gb = [uT[:, :, :].rearrange("p a b -> p (a b)")[:, T * k:T * k + T] for k in range(2)]
        new_phase()
        sq = ar(KC, T)
        cT = sq[:, 0, 0:2 * KC].rearrange("p (a b) -> p a b", b=2)
        new_phase()
        si = [ar(DE), ar(DE)]
        aa = [ar(DE), ar(DE)]
        aT = [ar(2, P), ar(2, P)]
        hN = ar(NT, D)
        XG = [ar(D), ar(D)]
        XT = [ar(KC, P), ar(KC, P)]
        Y = [ar(D), ar(D)]
        cmp = arena[0:1, 8704:8704 + NJ * NE].rearrange("p (a b) -> p a b", b=NE)
        eq = ar(NT * TOPK * NE)
        acc = nat[:, :, 0:D]

        vb = [ctx.enter_context(nc.psum_tensor(f"vb{i}", [P, 512], F32)) for i in range(NBANK)]
        ab = [ctx.enter_context(nc.psum_tensor(f"ab{i}", [P, 512], F32)) for i in range(NBANK)]

        def c_(name):
            return con[:, CN[name][0]:CN[name][1]]

        def s_(name):
            return sm[:, SM[name][0]:SM[name][1]]

        ident = c_("ident")

        vfull = [sem(f"vfull{i}") for i in range(NBANK)]
        vfree = [sem(f"vfree{i}") for i in range(NBANK)]
        afull = [sem(f"afull{i}") for i in range(NBANK)]
        afree = [sem(f"afree{i}") for i in range(NBANK)]
        loaded = [sem(f"slot_loaded{i}") for i in range(NSLOT)]
        freed = [sem(f"slot_freed{i}") for i in range(NSLOT)]
        start_in = sem("start_in")
        params_in = sem("params_in")
        mod_rows_ready = sem("mod_rows_ready")
        h_scaled = sem("h_scaled")
        params_fetched = sem("params_fetch_started")
        silu_c_ready = sem("silu_c_ready")
        c_loaded = sem("c_loaded")
        x_ready = sem("x_ready")
        sq_ready = sem("sq_ready")
        h_ready = sem("h_ready")
        root_wanted = sem("root_wanted")
        root_ready = sem("root_ready")
        gates_in = sem("recurrence_inputs_evacuated")
        proj_done = sem("projection_evacuated")
        vproj_done = sem("values_evacuated")
        f_ready = sem("f_ready")
        logf_ready = sem("logf_ready")
        exps_wanted = sem("exps_wanted")
        exps_ready = sem("exps_ready")
        rec_ready = sem("rec_operands_ready")
        kdn_ready = sem("kdn_ready")
        vx_ready = sem("vx_ready")
        att_ready = sem("att_ready")
        states_ready = sem("states_ready")
        fin_ready = sem("fin_ready")
        fin_stored = sem("fin_stored")
        o_ready = sem("o_ready")
        osq_ready = sem("osq_ready")
        pooled_ready = sem("pooled_ready")
        pooled_in = sem("pooled_sequence_and_room_ready")
        head_sq_ready = sem("head_squares_ready")
        head_roots_ready = sem("head_roots_ready")
        na_ready_pe, na_ready_act = sem("neighbourhood_heads_ready_pe"), sem("neighbourhood_heads_ready_act")
        kv_ready = sem("kv_ready")
        kv_stored = sem("kv_stored")
        bias_wanted = sem("bias_wanted")
        bias_in = sem("bias_in")
        qk_ready = sem("qk_ready")
        qkt_ready = sem("qkt_ready")
        exp_wanted = sem("exp_wanted")
        exp_ready = sem("exp_ready")
        p_ready = sem("p_ready")
        pt_ready = sem("pt_ready")
        s_free = sem("s_free")
        yv_ready = sem("y_from_vector_ready")
        ya_ready = sem("y_from_scalar_ready")
        gb_ready = sem("gb_ready")
        gb_free = sem("gb_free")
        merged_ready = sem("merged_ready")
        sc_ready = sem("sc_ready")
        hid_full = [sem("hid_full0"), sem("hid_full1")]
        si_ready = sem("si_ready")
        a_ready = sem("a_ready")
        at_ready = sem("at_ready")
        acc_ready = sem("acc_ready")
        chosen_ready = sem("chosen_ready")
        h2_stored = sem("h2_stored")
        table_cleared = sem("table_cleared")
        entries_ready = sem("entries_ready")
        entries_out = sem("entries_out")
        table_in = sem("table_in")
        jobs_sp, jobs_pool, jobs_pe, jobs_act = (sem(f"job_list_ready_{e}") for e in ("sp", "pool", "pe", "act"))
        shared_ready = sem("shared_ready")
        shared_stored = sem("shared_stored")
        rows_out = sem("rows_gathered")
        sums_out = sem("sums_added")
        xg_ready = sem("xg_ready")
        table_ready = sem("table_ready")
        xg_free = sem("xg_free")
        xt_ready = sem("xt_ready")
        yj_ready = sem("job_output_ready")
        yj_free = sem("job_output_free")
        routed_done = sem("routed_done")
        acc_in = sem("acc_in")
        y_ready = sem("y_ready")
        y_stored = sem("y_stored")

        block = ctx.enter_context(nc.Block())

        def head_scales(eng, ops, k):
            c0, qn, kn, nq = ((256, "wqn", "wkn", 6), (896, "nqn", "nkn", 4))[k]
            for t in range(NT):
                X = nat[:, t, c0:c0 + 512].rearrange("p (h d) -> p h d", d=HD)
                ops.tensor_tensor(X, X, small[:, 24 * k + 8 * t:24 * k + 8 * t + 8].unsqueeze(2)
                                  .to_broadcast([P, 8, HD]), ALU.mult)
            eng.drain()
            for t in range(NT):
                X = nat[:, t, c0:c0 + 512].rearrange("p (h d) -> p h d", d=HD)
                for h0, h1, g in ((0, nq, qn), (nq, 8, kn)):
                    ops.tensor_tensor(X[:, h0:h1, :], X[:, h0:h1, :],
                                      s_(g).unsqueeze(1).to_broadcast([P, h1 - h0, HD]), ALU.mult)

        def job_pairs(eng, less=0):
            return eng.value_load(job_count[0:1, less:less + 1], min_val=T * TOPK // P // 2 - less,
                                  max_val=NJ // 2 - 2 - less)

        @block.sync
        def _(sp):
            cur = Cursor(SLOT_ORDER)

            def load(parts, s=None):
                s = cur.next() if s is None else s
                sp.wait_ge(freed[s], 1).then_inc(freed[s], -1)
                for dst, src in parts(slots[s]):
                    sp.dma_start(dst, src).then_inc(loaded[s], 32 // len(parts(slots[s])))

            with sp.Fori(0, DEPTH) as l:
                cur.restart()

                def layer(name):
                    return A[name][bass.ds(l, 1)].rearrange("l a b -> (l a) b")

                def columns(name, b, w=512):
                    load(lambda s: [(s[:, 0:KC * w].rearrange("p (c n) -> p c n", c=KC),
                                     layer(name).rearrange("(p c) n -> p c n", c=KC)[:, :, 512 * b:512 * b + w])])

                for b in range(4):
                    if b == 1:
                        sp.wait_ge(params_fetched, 1).then_inc(params_fetched, -1)
                    columns("w_mod", b)
                for b in range(6):
                    columns("w_in", b, min(512, 2944 - 512 * b))
                for b in range(4, 8):
                    columns("w_mod", b)
                sp.wait_ge(bias_wanted, 1).then_inc(bias_wanted, -1)
                for h in range(4):
                    for t in range(2):
                        for r2 in range(2):
                            src = A["rpb"][bass.ds(l, 1), h, :]
                            ap = bass.AP(tensor=src.tensor, offset=src.offset + (4 + 2 * t + r2) * 31 - 48,
                                         ap=[[1, 64], [31, 4], [1, 64]])
                            sp.dma_start(raw[64 * r2:64 * r2 + 64, 2 * h + t, :].rearrange("p (a b) -> p a b", b=64), ap)\
                                .then_inc(bias_in, 16)
                for b in range(8, 10):
                    columns("w_mod", b)
                for two in PASSES:
                    for nb in range(4):
                        if nb % 2 == 0:
                            def rows(s):
                                at, parts = 0, []
                                for b in two:
                                    y0, n = BRANCH_CHUNKS[b][0], len(BRANCH_CHUNKS[b])
                                    parts.append((s[:, 512 * at:512 * (at + n)].rearrange("p (c n) -> p c n", c=n),
                                                  layer("w_branch")[P * y0:P * (y0 + n), :].rearrange(
                                                      "(c p) n -> p c n", c=n)[:, :, 256 * nb:256 * nb + 512]))
                                    at += n
                                return parts
                            load(rows)
                        load(lambda s: [(s[:, 2048 * k:2048 * (k + 1)].rearrange("p (c n) -> p c n", c=KC),
                                         layer("w_mgate").rearrange("(p c) n -> p c n", c=KC)[
                                             :, :, D * b + 256 * nb:D * b + 256 * nb + 256])
                                        for k, b in enumerate(two)])
                for half in range(2):
                    load(lambda s: [(s[:, :].rearrange("p (c n) -> p c n", c=4),
                                     layer("w_out")[512 * half:512 * half + 512, :].rearrange("(c p) n -> p c n", c=4))])
                for b in range(10, 12):
                    columns("w_mod", b)
                load(lambda s: [(s[:, :].rearrange("p (c n) -> p c n", c=KC)[:, :, DE * k:DE * k + DE],
                                 layer(w).rearrange("(p c) n -> p c n", c=KC)) for k, w in enumerate(("w_sg", "w_su"))])
                load(lambda s: [(s[:, 0:2048].rearrange("p (c n) -> p c n", c=2),
                                 layer("w_sd").rearrange("(c p) n -> p c n", c=2))])
                def expert_of(j):
                    return sp.value_load(job_expert[0:1, bass.ds(j, 1)], min_val=0, max_val=NE - 1)

                def expert(name, e):
                    return A[name][bass.ds(l * NE + e, 1)].rearrange("l a b -> (l a) b")

                def ups(e, k):
                    load(lambda s: [(s[:, :].rearrange("p (c n) -> p c n", c=KC)[:, :, DE * i:DE * i + DE],
                                     expert(w, e).rearrange("(p c) n -> p c n", c=KC))
                                    for i, w in enumerate(("w_eg", "w_eu"))], JOB_SLOTS[0][k])

                def downs(e, k):
                    load(lambda s: [(s[:, 0:2048].rearrange("p (c n) -> p c n", c=2),
                                     expert("w_ed", e).rearrange("(c p) n -> p c n", c=2))], JOB_SLOTS[1][k])

                sp.wait_ge(jobs_sp, 1).then_inc(jobs_sp, -1)
                ups(expert_of(0), 0)
                ups(expert_of(1), 1)
                downs(expert_of(0), 0)
                rounds = job_pairs(sp, 1)
                with sp.Fori(0, rounds) as j:
                    for k in range(2):
                        ups(expert_of(2 * j + 2 + k), k)
                        downs(expert_of(2 * j + 1 + k), 1 - k)
                downs(expert_of(2 * rounds + 1), 1)
            sp.wait_ge(y_ready, 1).then_inc(y_ready, -1)
            sp.dma_start(O["yT"], xT[:, :, :]).then_inc(y_stored, 16)
            sp.wait_ge(y_stored, 16)

        @block.gpsimd
        def _(pool):
            def gather(j, b):
                pool.wait_ge(xg_free, 1).then_inc(xg_free, -1)
                nc.gpsimd.tensor_copy(rows_of[b][:, :], table[:, bass.ds(j, 1), :].rearrange("p a b -> p (a b)"))
                pool.drain()
                pool.indirect_dma_start(XG[b], None, h2_d, bass.IndirectOffsetOnAxis(ap=rows_of[b][:, 0:1].bitcast(U32), axis=0),
                                        bounds_check=T - 1, oob_is_err=False).then_inc(rows_out, 16)
                pool.drain().then_inc(xg_ready, 1)

            def gather_and_add(jg, ja, b):
                nc.gpsimd.tensor_copy(sums_of[:, :], table[:, bass.ds(ja, 1), :].rearrange("p a b -> p (a b)"))
                nc.gpsimd.tensor_copy(rows_of[b][:, :], table[:, bass.ds(jg, 1), :].rearrange("p a b -> p (a b)"))
                pool.wait_ge(xg_free, 1).then_inc(xg_free, -1)
                pool.wait_ge(yj_ready, 1).then_inc(yj_ready, -1)
                pool.drain()
                pool.indirect_dma_start(XG[b], None, h2_d, bass.IndirectOffsetOnAxis(ap=rows_of[b][:, 0:1].bitcast(U32), axis=0),
                                        bounds_check=T - 1, oob_is_err=False).then_inc(rows_out, 16)
                pool.indirect_dma_start(sum_d, bass.IndirectOffsetOnAxis(ap=sums_of[:, 0:1].bitcast(U32), axis=0), Y[b], None,
                                        bounds_check=T - 1, oob_is_err=False, compute_op=ALU.add).then_inc(sums_out, 16)
                pool.drain().then_inc(xg_ready, 1)
                pool.sem_inc(yj_free, 1)

            def add(j, b):
                nc.gpsimd.tensor_copy(sums_of[:, :], table[:, bass.ds(j, 1), :].rearrange("p a b -> p (a b)"))
                pool.wait_ge(yj_ready, 1).then_inc(yj_ready, -1)
                pool.drain()
                pool.indirect_dma_start(sum_d, bass.IndirectOffsetOnAxis(ap=sums_of[:, 0:1].bitcast(U32), axis=0), Y[b], None,
                                        bounds_check=T - 1, oob_is_err=False, compute_op=ALU.add).then_inc(sums_out, 16)
                pool.drain().then_inc(yj_free, 1)

            with pool.Fori(0, DEPTH):
                pool.wait_ge(pooled_in, 2).then_inc(pooled_in, -2)
                inv = c_("inv").rearrange("p (a b) -> p a b", b=PADU)
                u = uT[:, :, :]
                lo, hi = 8, PADU - 8

                def window(dst, k, src, h, edge):
                    n = PADU - edge + 1
                    nc.gpsimd.tensor_tensor(dst[:, k:2, edge:n], src[:, k:2, edge - h:n - h],
                                            src[:, k:2, edge + h:n + h], ALU.add)
                    pool.drain()

                def mean(g, s):
                    q = slice(64 * (g % 2), 64 * (g % 2) + 64)
                    nc.gpsimd.tensor_tensor(pl[q, g // 2, lo:hi], s[q, g // 2, lo:hi], inv[q, g // 2, lo:hi], ALU.mult)
                    pool.drain()

                nc.gpsimd.tensor_tensor(s2[:, :, 1:PADU], u[:, :, 0:PADU - 1], u[:, :, 1:PADU], ALU.add)
                pool.drain()
                mean(0, s2)
                window(s4, 0, s2, 1, 2)
                mean(1, s4)
                window(s8, 1, s4, 2, 4)
                mean(2, s8)
                window(s16, 1, s8, 4, 8)
                mean(3, s16)
                nc.gpsimd.tensor_tensor(pl[:, :, lo:hi], pl[:, :, lo:hi], u[:, :, lo:hi], ALU.subtract)
                pool.drain().then_inc(pooled_ready, 1)
                pool.wait_ge(head_roots_ready, 1).then_inc(head_roots_ready, -1)
                head_scales(pool, nc.gpsimd, 1)
                pool.drain().then_inc(na_ready_pe, 1)
                pool.sem_inc(na_ready_act, 1)
                pool.wait_ge(table_cleared, 16).then_inc(table_cleared, -16)
                pool.wait_ge(entries_ready, 1).then_inc(entries_ready, -1)
                for t in range(NT):
                    for k in range(TOPK):
                        pool.indirect_dma_start(table_d, bass.IndirectOffsetOnAxis(
                            ap=place_u[:, TOPK * t + k:TOPK * t + k + 1], axis=0), entry[:, t, k, :], None)\
                            .then_inc(entries_out, 16)
                pool.drain()
                pool.dma_start(table[:, :, :], table_d.rearrange("(p j) w -> p j w", j=NJ)).then_inc(table_in, 16)
                pool.drain().then_inc(table_ready, 1)
                pool.wait_ge(h2_stored, 16).then_inc(h2_stored, -16)
                for b in range(2):
                    nc.gpsimd.memset(XG[b], 0.0)
                pool.drain()
                pool.wait_ge(jobs_pool, 1).then_inc(jobs_pool, -1)
                for j in range(4):
                    gather(j, j % 2)
                pool.wait_ge(shared_stored, 16).then_inc(shared_stored, -16)
                rounds = job_pairs(pool, 2)
                with pool.Fori(0, rounds) as j:
                    for b in range(2):
                        gather_and_add(2 * j + 4 + b, 2 * j + b, b)
                for k in range(4):
                    add(2 * rounds + k, k % 2)
                pool.drain().then_inc(routed_done, 1)

        @block.tensor
        def _(pe):
            v, a, sl = Cursor(range(NBANK)), Cursor(range(NBANK)), Cursor(SLOT_ORDER)
            release = []

            def mm(out, lhsT, rhs, start, stop, last=False):
                i = nc.tensor.matmul(out, lhsT, rhs, start=start, stop=stop, skip_group_check=True)
                if release and not last:
                    i.then_inc(freed[release.pop(0)], 1)
                return i

            def group(ring, body):
                b = ring.next()
                banks, full, free = (vb, vfull, vfree) if ring is v else (ab, afull, afree)
                pe.wait_ge(free[b], 1).then_inc(free[b], -1)
                last = body(banks[b])
                last.then_inc(full[b], 1)

            def slot():
                s = sl.next()
                if s in release:
                    flush()
                pe.wait_ge(loaded[s], 32).then_inc(loaded[s], -32)
                return s, slots[s]

            def flush():
                while release:
                    pe.drain().then_inc(freed[release.pop(0)], 1)

            def run(out, pairs, chunks=False):
                for k, (x, y) in enumerate(pairs):
                    if chunks:
                        pe.wait_ge(h_ready, 1).then_inc(h_ready, -1)
                    last = mm(out, x, y, k == 0, k == len(pairs) - 1, k == len(pairs) - 1)
                return last

            def trans(bank, blocks):
                for k, x in enumerate(blocks):
                    last = nc.tensor.transpose(bank[:, P * k:P * k + P], x, ident)
                return last

            def mean_square():
                def squares(o):
                    for c in range(KC):
                        pe.wait_ge(sq_ready, 1).then_inc(sq_ready, -1)
                        last = mm(o[:, 0:T], c_("ones"), sq[:, c, :], c == 0, c == KC - 1, c == KC - 1)
                    return last
                group(a, squares)

            def wview(w, c=KC):
                return w[:, 0:c * (SLOT // c)].rearrange("p (c n) -> p c n", c=c)

            def up(b, x, w):
                pe.wait_ge(vfree[b], 1).then_inc(vfree[b], -1)
                run(vb[b][:, :], [(x(c), wview(w)[:, c, :]) for c in range(KC)]).then_inc(hid_full[b], 1)

            def hidden(b):
                pe.wait_ge(a_ready, 1).then_inc(a_ready, -1)
                group(a, lambda o: trans(o, [aa[b][:, P * f:P * f + P] for f in range(2)]))

            def down(b, w):
                pe.wait_ge(at_ready, 1).then_inc(at_ready, -1)
                wd = w[:, 0:2048].rearrange("p (c n) -> p c n", c=2)
                for n in range(2):
                    pe.wait_ge(vfree[2 + n], 1).then_inc(vfree[2 + n], -1)
                    run(vb[2 + n][:, :], [(aT[b][:, f, :], wd[:, f, 512 * n:512 * n + 512]) for f in range(2)])\
                        .then_inc(vfull[2 + n], 1)

            def turned(b):
                pe.wait_ge(xg_ready, 1).then_inc(xg_ready, -1)
                for g in range(2):
                    group(a, lambda o: trans(o, [XG[b][:, P * c:P * c + P] for c in range(4 * g, 4 * g + 4)]))

            for s in range(NSLOT):
                pe.sem_inc(freed[s], 1)
            pe.wait_ge(silu_c_ready, 1).then_inc(silu_c_ready, -1)
            with pe.Fori(0, DEPTH):
                v.restart(), a.restart(), sl.restart()

                def mod_block(b):
                    s, w = slot()
                    q = 32 * (b % 4)
                    group(a, lambda o: run(o[q:q + 2, :], [(scT[:, c, :], wview(w)[:, c, :]) for c in range(KC)]))
                    release.append(s)

                def mod_turned():
                    pe.wait_ge(mod_rows_ready, 1).then_inc(mod_rows_ready, -1)
                    group(v, lambda o: trans(o, [mod_rows[:, P * n:P * n + P] for n in range(4)]))

                block_slot = {}

                def project(i):
                    b, tr, c0, n, t = GROUPS[i]
                    if b not in block_slot:
                        block_slot[b] = slot()
                    s, w = block_slot[b]
                    width = min(512, 2944 - 512 * b)
                    wv = w[:, 0:KC * width].rearrange("p (c n) -> p c n", c=KC)
                    o0 = c0 - 512 * b
                    if tr:
                        group(a, lambda o: run(o[:, 0:T], [(wv[:, c, o0:o0 + n], hT[:, c, :]) for c in range(KC)],
                                               chunks=i == 0))
                    else:
                        group(v if c0 == 768 else a,
                              lambda o: run(o[:, 0:n], [(hT[:, c, P * t:P * t + P], wv[:, c, o0:o0 + n])
                                                        for c in range(KC)]))
                    if i + 1 == len(GROUPS) or GROUPS[i + 1][0] != b:
                        release.append(s)

                mean_square()
                for b in range(4):
                    mod_block(b)
                mod_turned()
                for i in range(EARLY):
                    project(i)
                pe.wait_ge(vproj_done, 1).then_inc(vproj_done, -1)
                for r in range(2):
                    late = EARLY + LATE * r
                    for i in range(4):
                        project(late + i)
                    pe.wait_ge(rec_ready, 1).then_inc(rec_ready, -1)
                    for t in range(NT):
                        group(v, lambda o: trans(o, [L[:, pr, P * t:P * t + P] for pr in range(2)]))
                    project(late + 4)
                    pe.wait_ge(kdn_ready, 1).then_inc(kdn_ready, -1)
                    for t in ((0, 1, 2), (0, 2, 1))[r]:
                        pe.wait_ge(vx_ready, 1).then_inc(vx_ready, -1)
                        for pr in range(2):
                            def ds(o):
                                for h2 in range(2):
                                    h = 2 * pr + h2
                                    last = mm(o[64 * h2:64 * h2 + 64, :], kdN[:, t, 64 * h:64 * h + 64], VX[:, h, :],
                                              True, True)
                                return last
                            group(v, ds)
                        project(late + 5 + (t if r == 0 else (0, 2, 1)[t]))
                    pe.wait_ge(states_ready, 1).then_inc(states_ready, -1)
                    for t in range(NT):
                        for h2 in range(2):
                            def att(o):
                                for pr in range(2):
                                    last = mm(o[:, P * pr:P * pr + P], KE[64 * h2:64 * h2 + 64, pr, P * t:P * t + P],
                                              QE[64 * h2:64 * h2 + 64, pr, P * t:P * t + P], True, True)
                                return last
                            group(v, att)
                        pe.wait_ge(att_ready, 1).then_inc(att_ready, -1)

                        def out(o):
                            for pr in range(2):
                                for h2 in range(2):
                                    q = slice(64 * h2, 64 * h2 + 64)
                                    h = 2 * pr + h2
                                    mm(o[q, P * pr:P * pr + P], nat[:, t, 64 * h:64 * h + 64], attS[:, h, :], True, False)
                                    for c in range(TC):
                                        n0 = P * t + CH * c
                                        row = TC * t + c + (t > 0) + r
                                        last = mm(o[q, P * pr + CH * c:P * pr + CH * c + CH], S[q, pr, row, :],
                                                  QX[q, pr, n0:n0 + CH], False, c == TC - 1)
                            return last
                        group(v, out)
                pe.wait_ge(osq_ready, 1).then_inc(osq_ready, -1)
                for pr in range(2):
                    group(a, lambda o: run(o[:, 0:T], [(c_("blk64"), DD[:, pr, :])]))
                for b in range(4, 8):
                    mod_block(b)
                mod_turned()
                pe.wait_ge(pooled_ready, 1).then_inc(pooled_ready, -1)
                for k in range(2):
                    def pmap(o):
                        for h2 in range(2):
                            q = slice(64 * h2, 64 * h2 + 64)
                            mm(o[q, 0:P], poolw[q, k, :], pl[q, k, 8:8 + P], True, True)
                            last = mm(o[q, P:T], poolw[q, k, :], pl[q, k, 152:152 + 256], True, True)
                        return last
                    group(v, pmap)
                for b in range(8, 10):
                    mod_block(b)
                mod_turned()
                pe.wait_ge(qk_ready, 1).then_inc(qk_ready, -1)
                pe.wait_ge(na_ready_pe, 1).then_inc(na_ready_pe, -1)
                for t in range(NT):
                    group(a, lambda o: trans(o, [qkr[:, t, P * j:P * j + P] for j in range(4)]))
                    group(a, lambda o: trans(o, [nat[:, t, 896 + P * j:896 + P * j + P] for j in range(4)]))
                pe.wait_ge(qkt_ready, 1).then_inc(qkt_ready, -1)

                def scores(i):
                    qc, kc, cc, p0 = head_place(i)[:4]
                    q = slice(p0, p0 + 64)
                    group(v, lambda o: mm(o[:, 0:P], qkT[q, qc, 0:P], qkT[q, kc, 0:P], True, True, True))
                    for t in (1, 2):
                        def s(o):
                            mm(o[:, 0:256], qkT[q, qc, P * t:P * t + P], qkT[q, kc, P:T], True, True)
                            return mm(o[:, 256:T], qkT[q, qc, P * t:P * t + P], kcT[q, cc, :], True, True)
                        group(v, s)

                held = {}

                def gated(two, u):
                    nb, k, n = u // 4, u // 2 % 2, u % 2
                    if u % 8 == 0:
                        held["branch"] = slot()
                    if u % 4 == 0:
                        held["gate"] = slot()
                    ys = BRANCH_CHUNKS[two[k]]
                    wm = held["gate"][1][:, 2048 * k:2048 * (k + 1)].rearrange("p (c n) -> p c n", c=KC)
                    wbv = held["branch"][1][:, :].rearrange("p (c n) -> p c n", n=512)
                    at = k * len(BRANCH_CHUNKS[two[0]])
                    col = 256 * (nb % 2) + P * n
                    group(a, lambda o: run(o[:, 0:T], [(wm[:, c, P * n:P * n + P], hT[:, c, :]) for c in range(KC)]))
                    group(v, lambda o: run(o[:, 0:T], [(wbv[:, at + j, col:col + P], yT[:, y, :])
                                                       for j, y in enumerate(ys)]))
                    if u % 4 == 3:
                        release.append(held["gate"][0])
                    if u % 8 == 7:
                        release.append(held["branch"][0])

                pe.wait_ge(yv_ready, 1).then_inc(yv_ready, -1)
                scores(0)
                gated(PASSES[0], 0)
                for i in range(NH):
                    if i + 1 < NH:
                        scores(i + 1)
                    vcol, ccol, _, op = head_place(i)[4:]
                    pe.wait_ge(p_ready, 1).then_inc(p_ready, -1)
                    group(a, lambda o: trans(o, [sP[i % 2][:, P * k:P * k + P] for k in range(4)]))
                    group(a, lambda o: trans(o, [sP[i % 2][:, P * k:P * k + P] for k in range(4, 7)]))
                    gated(PASSES[0], i + 1)
                    pe.wait_ge(pt_ready, 1).then_inc(pt_ready, -1)

                    def pv(o):
                        q = slice(op, op + 64)
                        mm(o[q, 0:P], nat[:, 0, vcol:vcol + 64], pT[i % 2][:, 0, :], True, True)
                        for t in (1, 2):
                            k0 = 1 + 3 * (t - 1)
                            last = run(o[q, P * t:P * t + P],
                                       [(nat[:, 1, vcol:vcol + 64], pT[i % 2][:, k0, :]),
                                        (nat[:, 2, vcol:vcol + 64], pT[i % 2][:, k0 + 1, :]),
                                        (vc[:, ccol:ccol + 64], pT[i % 2][:, k0 + 2, :])])
                        return last
                    group(a, pv)
                for u in range(NH + 1, UNITS):
                    gated(PASSES[0], u)
                pe.wait_ge(ya_ready, 1).then_inc(ya_ready, -1)
                for u in range(UNITS):
                    gated(PASSES[1], u)
                flush()
                pe.wait_ge(merged_ready, 1).then_inc(merged_ready, -1)
                wo = [slot(), slot()]
                for c in range(KC):
                    group(v, lambda o: run(o[:, 0:T], [(wview(wo[k // 4][1], 4)[:, k % 4, c:D:KC], merged[:, k, :])
                                                       for k in range(KC)]))
                release.extend([wo[0][0], wo[1][0]])
                mean_square()
                mod_block(10)
                mod_block(11)
                def router(o):
                    for t in range(NT):
                        last = run(o[:, NE * t:NE * t + NE], [(hT[:, c, P * t:P * t + P], wr[:, c, :]) for c in range(KC)],
                                   chunks=t == 0)
                    return last
                group(a, router)
                mod_turned()
                pe.wait_ge(chosen_ready, 1).then_inc(chosen_ready, -1)

                def places(o):
                    for t in range(NT):
                        run(o[:, NE * t:NE * t + NE],
                            [(c_("ones"), chosen[:, u, :]) for u in range(t)] + [(c_("before"), chosen[:, t, :])])
                    return run(o[:, NE * NT:NE * NT + NE], [(c_("ones"), chosen[:, u, :]) for u in range(NT)])
                group(v, places)
                for t in range(NT):
                    for g in range(2):
                        group(a, lambda o: trans(o, [hT[:, c, P * t:P * t + P] for c in range(4 * g, 4 * g + 4)]))
                v.restart(), a.restart()
                (sg, wg), (sd, wd_) = slot(), slot()
                up(0, lambda c: hT[:, c, 0:P], wg)
                for t in range(1, NT):
                    up(t % 2, lambda c: hT[:, c, P * t:P * t + P], wg)
                    if t == NT - 1:
                        release.append(sg)
                    hidden((t - 1) % 2)
                    down((t - 1) % 2, wd_)
                hidden((NT - 1) % 2)
                down((NT - 1) % 2, wd_)
                release.append(sd)
                flush()
                pe.wait_ge(jobs_pe, 1).then_inc(jobs_pe, -1)
                a.restart()
                turned(0)
                turned(1)

                def job_slot(s):
                    pe.wait_ge(loaded[s], 32).then_inc(loaded[s], -32)
                    return s

                def job_up(b):
                    pe.wait_ge(xt_ready, 1).then_inc(xt_ready, -1)
                    s = job_slot(JOB_SLOTS[0][b])
                    up(b, lambda c: XT[b][:, c, :], slots[s])
                    release.append(s)

                def job_down(b):
                    s = job_slot(JOB_SLOTS[1][b])
                    down(b, slots[s])
                    release.append(s)

                def job_turn(b):
                    hidden(b)
                    turned(b)

                a.restart()
                job_up(0)
                job_turn(0)
                job_up(1)
                job_down(0)
                job_turn(1)
                flush()
                with pe.Fori(0, job_pairs(pe, 2)):
                    a.restart()
                    job_up(0)
                    job_down(1)
                    job_turn(0)
                    job_up(1)
                    job_down(0)
                    job_turn(1)
                    flush()
                a.restart()
                job_up(0)
                job_down(1)
                hidden(0)
                job_up(1)
                job_down(0)
                hidden(1)
                job_down(1)
                flush()
                pe.wait_ge(acc_in, 16).then_inc(acc_in, -16)
                v.restart()
                for c in range(KC):
                    group(v, lambda o: trans(o, [acc[:, t, c:D:KC] for t in range(NT)]))

        @block.scalar
        def _(act):
            a = Cursor(range(NBANK))
            f = nc.scalar.activation

            def empty(body):
                b = a.next()
                act.wait_ge(afull[b], 1).then_inc(afull[b], -1)
                body(ab[b]).then_inc(afree[b], 1)

            def tell(s):
                act.drain().then_inc(s, 1)

            for b in range(NBANK):
                act.sem_inc(afree[b], 1)
            act.dma_start(cT[:, :, :], A["cT"]).then_inc(c_loaded, 16)
            act.dma_start(xT[:, :, :], A["xT"]).then_inc(start_in, 16)
            act.dma_start(con[:, :], A["con"]).then_inc(start_in, 16)
            act.wait_ge(c_loaded, 16).then_inc(c_loaded, -16)
            f(scT[:, :, :], cT[:, :, :], ACT.Silu)
            tell(silu_c_ready)
            with act.Fori(0, DEPTH) as l:
                a.restart()
                for dst, name in ((sm[:, :], "sm"), (kcT[:, :, :].rearrange("p a b -> p (a b)"), "kcT"),
                                  (vc[:, :], "vc"), (s0[:, :, :].rearrange("p a b -> p (a b)"), "s0"),
                                  (poolw[:, :, :].rearrange("p a b -> p (a b)"), "poolw")):
                    act.dma_start(dst, A[name][bass.ds(l, 1)].rearrange("l p n -> (l p) n")).then_inc(params_in, 16)
                act.dma_start(wr[:, :, :], A["w_router"][bass.ds(l, 1)].rearrange("l (p c) n -> (l p) c n", c=KC))\
                    .then_inc(params_in, 16)
                act.sem_inc(params_fetched, 1)

                def squares():
                    for c in range(KC):
                        act.wait_ge(x_ready, 1).then_inc(x_ready, -1)
                        f(sq[:, c, :], xT[:, c, :], ACT.Square).then_inc(sq_ready, 1)

                def root():
                    empty(lambda o: f(rstd[:, :], o[:, 0:T], ACT.Sqrt, bias=c_("eps"), scale=1.0 / D))
                    tell(root_ready)

                def shift(k):
                    for c in range(KC):
                        act.wait_ge(h_scaled, 1).then_inc(h_scaled, -1)
                        f(hT[:, c, 0:P], hT[:, c, 0:P], ACT.Identity, bias=mT[:, 3 * k, c, 0:1])
                        f(hT[:, c, P:T], hT[:, c, P:T], ACT.Identity, bias=mT[:, 3 * k, c, 1:2]).then_inc(h_ready, 1)

                squares()
                root()
                act.wait_ge(f_ready, 1).then_inc(f_ready, -1)
                act.dma_start(table_d.rearrange("(p j) w -> p (j w)", j=NJ), table[:, :, :].rearrange("p a b -> p (a b)"))\
                    .then_inc(table_cleared, 16)
                f(lbw[:, 1:3, :], lbw[:, 1:3, :], ACT.Exp).then_inc(logf_ready, 1)

                def mod_row(b):
                    q = 32 * (b % 4)
                    empty(lambda o: f(mod_rows[q:q + 2, :], o[q:q + 2, :], ACT.Copy))

                for b in range(4):
                    mod_row(b)
                tell(mod_rows_ready)
                shift(0)
                for dst, fn in ((qT, ACT.Copy), (sig[0], ACT.Sigmoid), (sig[1], ACT.Sigmoid)):
                    for pr in range(2):
                        empty(lambda o: f(dst[:, pr, :], o[:, 0:T], fn))
                tell(gates_in)

                def projected(i):
                    _, tr, c0, n, t = GROUPS[i]
                    if c0 in (1024, 1152):
                        empty(lambda o: f(gT[:, (c0 - 1024) // P, :], o[:, 0:T], ACT.Silu))
                    elif tr:
                        k = (c0 - 1920) // P

                        def padded(o):
                            f(uT[:, k, 8:8 + P], o[:, 0:P], ACT.Copy)
                            return f(uT[:, k, 152:152 + 256], o[:, P:T], ACT.Copy)
                        empty(padded)
                    else:
                        empty(lambda o: f(nat[:, t, nat_col(c0):nat_col(c0) + n], o[:, 0:n], ACT.Copy))

                for r in range(2):
                    late = EARLY + LATE * r
                    act.wait_ge(f_ready, 1).then_inc(f_ready, -1)
                    f(L, sig[r][:, :, :], ACT.Ln).then_inc(logf_ready, 1)
                    projected(late)
                    act.wait_ge(exps_wanted, 1).then_inc(exps_wanted, -1)
                    f(QE, DD, ACT.Exp)
                    f(KE, DD, ACT.Exp, scale=-1.0)
                    f(QX, C, ACT.Exp)
                    f(L, L, ACT.Exp)
                    f(small[:, 0:48], small[:, 0:48], ACT.Exp)
                    tell(exps_ready)
                    for i in range(1, LATE):
                        projected(late + i)
                tell(proj_done)
                act.sem_inc(pooled_in, 1)
                act.wait_ge(fin_ready, 1).then_inc(fin_ready, -1)
                act.wait_ge(o_ready, 1).then_inc(o_ready, -1)
                f(DD, oT, ACT.Square).then_inc(osq_ready, 1)
                for pr in range(2):
                    empty(lambda o: f(QE[:, pr, :], o[:, 0:T], ACT.Sqrt, bias=c_("eps")))
                tell(root_ready)
                act.dma_start(O["fin"][bass.ds(l, 1)].rearrange("l p n -> (l p) n"),
                              fin[:, :, :].rearrange("p a b -> p (a b)")).then_inc(fin_stored, 16)
                for k, c0 in enumerate((256, 896)):
                    f(head_sq[:, k, :].rearrange("p (t n) -> p t n", n=512), nat[:, :, c0:c0 + 512], ACT.Square)
                tell(head_sq_ready)
                for b in range(4, 8):
                    mod_row(b)
                tell(mod_rows_ready)
                act.wait_ge(root_wanted, 1).then_inc(root_wanted, -1)
                f(small[:, 0:48], small[:, 0:48], ACT.Sqrt, bias=c_("eps"), scale=1.0 / HD).then_inc(root_ready, 1)
                for b in range(8, 10):
                    mod_row(b)
                tell(mod_rows_ready)
                act.wait_ge(kv_ready, 1).then_inc(kv_ready, -1)
                act.wait_ge(na_ready_act, 1).then_inc(na_ready_act, -1)
                for name, c0, w in (("wk", 640, 128), ("wv", 768, 128), ("nk", 1152, 256), ("nv", 1408, 256)):
                    act.dma_start(O[name][bass.ds(l, 1)].rearrange("l p n -> (l p) n"), nat[:, 0, c0:c0 + w])\
                        .then_inc(kv_stored, 16)
                for t in range(NT):
                    for k in range(2):
                        empty(lambda o: f(qkT[:, 4 * k:4 * k + 4, P * t:P * t + P],
                                          o[:, :].rearrange("p (a b) -> p a b", b=P), ACT.Copy))
                tell(qkt_ready)

                def exps(i):
                    act.wait_ge(exp_wanted, 1).then_inc(exp_wanted, -1)
                    s, k = sP[i % 2], 8 * (i % 2)
                    for t, (c0, n) in enumerate(((0, P), (P, T), (P + T, T))):
                        f(s[:, c0:c0 + n], s[:, c0:c0 + n], ACT.Exp, bias=sbig[:, k + t:k + t + 1],
                          accum_out=sbig[:, 16 + k + t:16 + k + t + 1])
                    f(sbig[:, 32 + k:32 + k + 3], sbig[:, k:k + 3], ACT.Exp, bias=s_("sink")[:, i:i + 1])
                    tell(exp_ready)

                def gates(two, u):
                    act.wait_ge(gb_free, 1).then_inc(gb_free, -1)
                    col = two[u // 2 % 2] * KC + 2 * (u // 4) + u % 2
                    empty(lambda o: f(gb[u % 2], o[:, 0:T], ACT.Sigmoid, bias=s_("bmg")[:, col:col + 1]))
                    tell(gb_ready)

                exps(0)
                gates(PASSES[0], 0)
                for i in range(NH):
                    empty(lambda o: f(pT[i % 2][:, 0:4, :], o[:, :].rearrange("p (a b) -> p a b", b=P), ACT.Copy))
                    empty(lambda o: f(pT[i % 2][:, 4:7, :], o[:, 0:T].rearrange("p (a b) -> p a b", b=P), ACT.Copy))
                    tell(pt_ready)
                    act.sem_inc(s_free, 1)
                    if i + 1 < NH:
                        exps(i + 1)
                    gates(PASSES[0], i + 1)
                    yc, op = head_place(i)[6:]
                    empty(lambda o: f(yT[op:op + 64, yc, :], o[op:op + 64, 0:T], ACT.Copy))
                tell(ya_ready)
                for u in range(NH + 1, UNITS):
                    gates(PASSES[0], u)
                for u in range(UNITS):
                    gates(PASSES[1], u)
                squares()
                root()
                shift(1)
                mod_row(10)
                mod_row(11)
                tell(mod_rows_ready)
                empty(lambda o: f(sc[:, :, :], o[:, 0:NT * NE].rearrange("p (a b) -> p a b", b=NE), ACT.Sigmoid))
                tell(sc_ready)
                for t in range(NT):
                    for g in range(2):
                        empty(lambda o: f(hN[:, t, 512 * g:512 * g + 512], o[:, :], ACT.Copy))
                act.drain()
                act.dma_start(h2_d.rearrange("(t p) n -> p t n", p=P), hN[:, :, :]).then_inc(h2_stored, 16)
                a.restart()

                def silus(b):
                    act.wait_ge(hid_full[b], 1).then_inc(hid_full[b], -1)
                    f(si[b], vb[b][:, 0:DE], ACT.Silu).then_inc(si_ready, 1)

                def transposed(b):
                    empty(lambda o: f(aT[b], o[:, 0:DE].rearrange("p (a b) -> p a b", b=P), ACT.Copy))
                    tell(at_ready)

                def turned(b):
                    for g in range(2):
                        empty(lambda o: f(XT[b][:, 4 * g:4 * g + 4, :], o[:, :].rearrange("p (a b) -> p a b", b=P), ACT.Copy))
                    act.drain().then_inc(xt_ready, 1)
                    tell(xg_free)

                silus(0)
                for t in range(1, NT):
                    silus(t % 2)
                    transposed((t - 1) % 2)
                transposed((NT - 1) % 2)
                act.wait_ge(shared_ready, 1).then_inc(shared_ready, -1)
                act.dma_start(sum_d.rearrange("(t p) n -> p t n", p=P), acc).then_inc(shared_stored, 16)
                act.wait_ge(jobs_act, 1).then_inc(jobs_act, -1)
                a.restart()
                turned(0)
                turned(1)
                with act.Fori(0, job_pairs(act, 1)):
                    a.restart()
                    for b in range(2):
                        silus(b)
                        transposed(b)
                        turned(b)
                a.restart()
                for b in range(2):
                    silus(b)
                    transposed(b)
                act.wait_ge(routed_done, 1).then_inc(routed_done, -1)
                act.dma_start(acc, sum_d.rearrange("(t p) n -> p t n", p=P)).then_inc(acc_in, 16)

        @block.vector
        def _(dve):
            v = Cursor(range(NBANK))
            vec = nc.vector

            def settle():
                dve.drain()

            def tell(s):
                dve.drain().then_inc(s, 1)

            def empty(body):
                b = v.next()
                dve.wait_ge(vfull[b], 1).then_inc(vfull[b], -1)
                body(vb[b]).then_inc(vfree[b], 1)

            for b in range(NBANK):
                dve.sem_inc(vfree[b], 1)
            dve.sem_inc(fin_stored, 16)
            for b in range(2):
                dve.sem_inc(gb_free, 1)
            vec.memset(mod_rows[:, :], 0.0)
            vec.memset(sbr[:, :, :], NEG)
            for b in range(2):
                dve.sem_inc(xg_free, 1)
                dve.sem_inc(yj_free, 1)
            dve.wait_ge(start_in, 32).then_inc(start_in, -32)
            for t in range(NT):
                vec.tensor_copy(entry[:, t, :, 0].bitcast(U32), c_("token")[:, t:t + 1].to_broadcast([P, TOPK]))
            dve.drain().then_inc(x_ready, KC)
            with dve.Fori(0, DEPTH) as l:
                v.restart()
                vec.memset(uT[:, :, :], 0.0)
                vec.memset(table[:, :, 0].bitcast(I32), FAR)
                vec.memset(table[:, :, 1], 0.0)
                dve.wait_ge(params_in, 96).then_inc(params_in, -96)
                lbr = s_("lb").rearrange("p (a b) -> p a b", b=4)
                mx, e0, e1, su, c1, lbv = (lbw[:, k, :] for k in range(6))
                vec.tensor_tensor(mx, lbr[:, 0, :], lbr[:, 1, :], ALU.max)
                settle()
                vec.tensor_tensor(e0, lbr[:, 0, :], mx, ALU.subtract)
                vec.tensor_tensor(e1, lbr[:, 1, :], mx, ALU.subtract)
                tell(f_ready)
                dve.wait_ge(logf_ready, 1).then_inc(logf_ready, -1)
                vec.tensor_tensor(su, lbw[:, 1, :], lbw[:, 2, :], ALU.add)
                settle()
                vec.reciprocal(c1, su)
                settle()
                vec.tensor_tensor(e0, e0, c1, ALU.mult)
                vec.tensor_tensor(e1, e1, c1, ALU.mult)
                settle()
                vec.tensor_tensor(su, e0, e1, ALU.add)
                settle()
                vec.tensor_tensor(lb[:, 1, :], su, e0, ALU.subtract)
                vec.tensor_tensor(lb[:, 0, :], e0, e0, ALU.subtract)
                settle()
                vec.tensor_copy(lbl[:, 0, :], lb[:, bass.ds(l, 1), :].rearrange("p a b -> p (a b)"))
                settle()
                vec.tensor_scalar(lbl[:, 1, :], lbl[:, 0, :], -1.0, 1.0, ALU.mult, ALU.add)
                def modulated(b0, n):
                    def add(o):
                        rows = o[:, :].rearrange("p (n x) -> p n x", x=P)
                        for b in range(b0, b0 + n):
                            q, at = 32 * (b % 4), 4 * (b % 2)
                            bias = s_("bmod")[:, 8 * b:8 * b + 8].rearrange("p (a g) -> p a g", g=2)
                            last = vec.tensor_tensor(mT[:, b // 2, at:at + 4, :], rows[:, :, q:q + 2], bias, ALU.add)
                        return last
                    empty(add)

                def scales(k):
                    settle()
                    vec.scalar_tensor_tensor(modA[:, k, :, :], mT[:, 3 * k + 1, :, :], 1.0,
                                             s_(("g1", "g2")[k]).unsqueeze(2).to_broadcast([P, KC, 2]), ALU.add, ALU.mult)

                def inverse_root():
                    dve.wait_ge(root_ready, 1).then_inc(root_ready, -1)
                    vec.reciprocal(rstd[:, :], rstd[:, :])
                    settle()

                def norm(k):
                    for c in range(KC):
                        for g, (t0, t1) in enumerate(((0, P), (P, T))):
                            last = vec.scalar_tensor_tensor(hT[:, c, t0:t1], xT[:, c, t0:t1], modA[:, k, c, g:g + 1],
                                                            rstd[:, t0:t1], ALU.mult, ALU.mult)
                        last.then_inc(h_scaled, 1)

                inverse_root()
                modulated(0, 4)
                scales(0)
                settle()
                norm(0)
                for t in range(NT):
                    empty(lambda o: vec.tensor_copy(nat[:, t, 0:256], o[:, 0:256]))
                tell(vproj_done)
                dve.wait_ge(gates_in, 1).then_inc(gates_in, -1)
                chunked = lambda x: x.rearrange("p a (c n) -> p (a c) n", n=CH)
                flat = lambda x: x.rearrange("p a n -> p (a n)")
                tot = small[:, 0:48]
                for r in range(2):
                    for pr in range(2):
                        vec.tensor_scalar(sig[r][:, pr, :], sig[r][:, pr, :], lbl[:, 1, 2 * r + pr:2 * r + pr + 1],
                                          lbl[:, 0, 2 * r + pr:2 * r + pr + 1], ALU.mult, ALU.add)
                    tell(f_ready)
                    dve.wait_ge(logf_ready, 1).then_inc(logf_ready, -1)
                    vec.tensor_scalar(sig[r][:, :, :], sig[r][:, :, :], -1.0, 1.0, ALU.mult, ALU.add)
                    vec.tensor_tensor_scan(flat(C), c_("first"), flat(L), 0.0, ALU.mult, ALU.add)
                    settle()
                    vec.tensor_copy(tot, chunked(C)[:, :, CH - 1])
                    settle()
                    totb = tot.unsqueeze(2).to_broadcast([P, 2 * NCH, CH])
                    if r == 1:
                        vec.tensor_tensor(C, L, C, ALU.subtract)
                        settle()
                        vec.tensor_tensor(chunked(C), chunked(C), totb, ALU.add)
                        settle()
                    mid = CH // 2 - 1 + r
                    vec.tensor_tensor(chunked(DD), chunked(C), chunked(C)[:, :, mid:mid + 1].to_broadcast([P, 2 * NCH, CH]),
                                      ALU.subtract)
                    vec.tensor_tensor(chunked(L), totb, chunked(C), ALU.subtract)
                    settle()
                    vec.tensor_scalar(DD, DD, 80.0, -80.0, ALU.min, ALU.max)
                    tell(exps_wanted)
                    dve.wait_ge(exps_ready, 1).then_inc(exps_ready, -1)
                    vec.tensor_tensor(L, L, sig[r][:, :, :], ALU.mult)
                    vec.tensor_tensor(QE, QE, qT[:, :, :], ALU.mult)
                    vec.tensor_tensor(KE, KE, sig[r][:, :, :], ALU.mult)
                    vec.tensor_tensor(QX, QX, qT[:, :, :], ALU.mult)
                    tell(rec_ready)
                    for t in range(NT):
                        empty(lambda o: vec.tensor_copy(kdN[:, t, :], o[:, 0:256]))
                    tell(kdn_ready)
                    for base, n, src in ((0, 8, None), (9, 16, s0)):
                        row = base + (n if r else 0)
                        if src is None:
                            vec.memset(S[:, :, row, :], 0.0)
                        else:
                            vec.tensor_copy(S[:, :, row, :], s0[:, 2 * r:2 * r + 2, :])
                    for t in ((0, 1, 2), (0, 2, 1))[r]:
                        for h in range(4):
                            vec.tensor_tensor(VX[:, h, :].rearrange("p (c v) -> p c v", v=HD),
                                              nat[:, t, 64 * h:64 * h + 64].unsqueeze(1).to_broadcast([P, TC, HD]),
                                              c_("chunk").unsqueeze(2).to_broadcast([P, TC, HD]), ALU.mult)
                        tell(vx_ready)
                        b0, b1 = v.next(), v.next()
                        dve.wait_ge(vfull[b0], 1).then_inc(vfull[b0], -1)
                        dve.wait_ge(vfull[b1], 1).then_inc(vfull[b1], -1)
                        order = range(TC) if r == 0 else range(TC - 1, -1, -1)
                        for c in order:
                            row = TC * t + c + (t > 0)
                            for pr, b in ((0, b0), (1, b1)):
                                last = vec.scalar_tensor_tensor(
                                    S[:, pr, row + 1 - r, :], S[:, pr, row + r, :],
                                    tot[:, NCH * pr + TC * t + c:NCH * pr + TC * t + c + 1],
                                    vb[b][:, HD * c:HD * c + HD], ALU.mult, ALU.add)
                            settle()
                        dve.sem_inc(vfree[b0], 1)
                        dve.sem_inc(vfree[b1], 1)
                    if r == 0:
                        dve.wait_ge(fin_stored, 16).then_inc(fin_stored, -16)
                    vec.tensor_copy(fin[:, 2 * r:2 * r + 2, :], S[:, :, 0 if r else TC, :])
                    tell(states_ready)
                    if r == 1:
                        tell(fin_ready)
                    for t in range(NT):
                        for h2 in range(2):
                            m = c_("mask1" if r else "mask0")
                            empty(lambda o: vec.tensor_tensor(attS[:, h2:4:2, :], o[:, 0:256].rearrange("p (a b) -> p a b", b=P),
                                                              m.unsqueeze(1).to_broadcast([P, 2, P]), ALU.mult))
                        tell(att_ready)
                        dst = oT[:, :, P * t:P * t + P]
                        if r == 0:
                            empty(lambda o: vec.tensor_copy(dst, o[:, 0:256].rearrange("p (a b) -> p a b", b=P)))
                        else:
                            empty(lambda o: vec.tensor_tensor(dst, o[:, 0:256].rearrange("p (a b) -> p a b", b=P), dst, ALU.add))
                tell(o_ready)
                dve.sem_inc(pooled_in, 1)
                dve.sem_inc(bias_wanted, 1)
                dve.wait_ge(proj_done, 1).then_inc(proj_done, -1)
                dve.wait_ge(root_ready, 1).then_inc(root_ready, -1)
                vec.reciprocal(QE, QE)
                settle()
                for pr in range(2):
                    vec.scalar_tensor_tensor(oT[:, pr, :], oT[:, pr, :], s_("onorm"), QE[:, pr, :], ALU.mult, ALU.mult)
                    settle()
                    vec.tensor_tensor(yT[:, pr, :], oT[:, pr, :], gT[:, pr, :], ALU.mult)
                    settle()
                dve.wait_ge(head_sq_ready, 1).then_inc(head_sq_ready, -1)
                vec.reduce_sum(small[:, 0:48], head_sq.rearrange("p k (a b) -> p (k a) b", b=HD), axis=AX.X)
                tell(root_wanted)
                dve.wait_ge(root_ready, 1).then_inc(root_ready, -1)
                vec.reciprocal(small[:, 0:48], small[:, 0:48])
                tell(head_roots_ready)
                head_scales(dve, vec, 0)
                tell(kv_ready)
                modulated(4, 4)
                for k in range(2):
                    empty(lambda o: vec.tensor_scalar(yT[:, 5 + k, :], o[:, 0:T], s_("pscale")[:, k:k + 1], None, ALU.mult))
                tell(yv_ready)
                for t in range(NT):
                    X = nat[:, t, 256:768]
                    if t > 0:
                        R = tmp[:, 0:512]
                        R2 = tmp[:, 512:1024]
                        vec.tensor_tensor(R.rearrange("p (h d) -> p h d", d=HD), X.rearrange("p (h d) -> p h d", d=HD),
                                          c_("cos")[:, HD * (t - 1):HD * t].unsqueeze(1).to_broadcast([P, 8, HD]), ALU.mult)
                        xv = X.rearrange("p (h a q) -> p h a q", a=4, q=16)
                        rv = R2.rearrange("p (h a q) -> p h a q", a=4, q=16)
                        sv = c_("sin")[:, HD * (t - 1):HD * t].rearrange("p (a q) -> p a q", q=16)
                        for k in range(4):
                            vec.tensor_tensor(rv[:, :, k, :], xv[:, :, k ^ 1, :],
                                              sv[:, k, :].unsqueeze(1).to_broadcast([P, 8, 16]), ALU.mult)
                        settle()
                        vec.tensor_tensor(R, R, R2, ALU.add)
                        settle()
                        X = R
                    vec.tensor_copy(qkr[:, t, 0:384].rearrange("p (j g d) -> p g j d", g=2, d=HD),
                                    X[:, 0:384].rearrange("p (g j d) -> p g j d", g=2, d=HD))
                    vec.tensor_copy(qkr[:, t, 384:512], X[:, 384:512])
                    settle()
                tell(qk_ready)
                modulated(8, 2)
                scales(1)
                dve.wait_ge(bias_in, 256).then_inc(bias_in, -256)
                nm = c_("nmask").unsqueeze(1).to_broadcast([P, 4, HD])
                for ht in range(8):
                    vec.tensor_tensor(biasD[:, ht, 0:256].rearrange("p (a b) -> p a b", b=HD),
                                      raw[:, ht, ::-1].rearrange("p (a b) -> p a b", b=HD), nm, ALU.add)
                vec.memset(biasD[:, :, 256:T], 0.0)
                settle()
                wm = c_("wmask").rearrange("p (a b) -> p a b", b=T)

                def scaled(i):
                    if i >= 2:
                        dve.wait_ge(s_free, 1).then_inc(s_free, -1)
                    s, k = sP[i % 2], 8 * (i % 2)
                    empty(lambda o: vec.tensor_scalar(s[:, 0:P], o[:, 0:P], SCALE, None, ALU.mult))
                    for t in (1, 2):
                        add = wm[:, t - 1, :] if i < 6 else biasD[:, 2 * (i - 6) + t - 1, :]
                        c0 = P + T * (t - 1)
                        empty(lambda o: vec.scalar_tensor_tensor(s[:, c0:c0 + T], o[:, 0:T], SCALE, add, ALU.mult, ALU.add))
                    settle()
                    vec.reduce_max(sbig[:, k + 3:k + 4], s[:, 0:P], axis=AX.X)
                    vec.reduce_max(sbig[:, k + 4:k + 6], s[:, P:896].rearrange("p (a b) -> p a b", b=T), axis=AX.X)
                    settle()
                    vec.tensor_scalar(sbig[:, k:k + 3], sbig[:, k + 3:k + 6], s_("sink")[:, i:i + 1], -1.0, ALU.max, ALU.mult)
                    tell(exp_wanted)

                def normalised(i):
                    dve.wait_ge(exp_ready, 1).then_inc(exp_ready, -1)
                    s, k = sP[i % 2], 8 * (i % 2)
                    vec.tensor_tensor(sbig[:, 48:51], sbig[:, 16 + k:19 + k], sbig[:, 32 + k:35 + k], ALU.add)
                    settle()
                    vec.reciprocal(sbig[:, 52:55], sbig[:, 48:51])
                    settle()
                    for t, (c0, n) in enumerate(((0, P), (P, T), (P + T, T))):
                        vec.tensor_scalar(s[:, c0:c0 + n], s[:, c0:c0 + n], sbig[:, 52 + t:53 + t], None, ALU.mult)
                    tell(p_ready)

                def gated(p, u):
                    m, g = merged[:, 2 * (u // 4) + u % 2, :], gb[u % 2]
                    dve.wait_ge(gb_ready, 1).then_inc(gb_ready, -1)
                    if p == 0 and u // 2 % 2 == 0:
                        empty(lambda o: vec.tensor_tensor(m, o[:, 0:T], g, ALU.mult))
                    else:
                        empty(lambda o: vec.tensor_tensor(g, o[:, 0:T], g, ALU.mult))
                        settle()
                        vec.tensor_tensor(m, m, g, ALU.add)
                    tell(gb_free)

                scaled(0)
                normalised(0)
                gated(0, 0)
                for i in range(NH):
                    if i + 1 < NH:
                        scaled(i + 1)
                        normalised(i + 1)
                    gated(0, i + 1)
                dve.wait_ge(s_free, 1).then_inc(s_free, -1)
                dve.wait_ge(s_free, 1).then_inc(s_free, -1)
                for u in range(NH + 1, UNITS):
                    gated(0, u)
                for u in range(UNITS):
                    gated(1, u)
                tell(merged_ready)

                def residual(s):
                    for c in range(KC):
                        def add(o):
                            vec.scalar_tensor_tensor(xT[:, c, 0:P], o[:, 0:P], mT[:, s, c, 0:1], xT[:, c, 0:P],
                                                     ALU.mult, ALU.add)
                            return vec.scalar_tensor_tensor(xT[:, c, P:T], o[:, P:T], mT[:, s, c, 1:2], xT[:, c, P:T],
                                                            ALU.mult, ALU.add)
                        empty(add)
                        tell(x_ready)

                residual(2)
                inverse_root()
                norm(1)
                dve.wait_ge(sc_ready, 1).then_inc(sc_ready, -1)
                vec.tensor_tensor(sbr[:, :, 0:NE], sc[:, :, :], s_("brout").unsqueeze(1).to_broadcast([P, NT, NE]), ALU.add)
                settle()
                for t in range(NT):
                    vec.max(top8[:, t, :], sbr[:, t, :])
                settle()
                vec.memset(top8[:, :, TOPK:8], NEG)
                settle()
                for t in range(NT):
                    vec.match_replace(rep[:, t, :], top8[:, t, :], sbr[:, t, :], -3e38)
                settle()
                vec.tensor_scalar(chosen[:, :, :], rep[:, :, 0:NE], -2e30, None, ALU.is_lt)
                tell(chosen_ready)
                vec.scalar_tensor_tensor(gate[:, :, :], rep[:, :, 0:NE], -2e30, sc[:, :, :], ALU.is_lt, ALU.mult)
                settle()
                vec.reduce_sum(small[:, 48:51], gate[:, :, :], axis=AX.X)
                settle()
                vec.reciprocal(small[:, 52:55], small[:, 48:51])
                settle()
                for t in range(NT):
                    vec.tensor_scalar(gate[:, t, :], gate[:, t, :], small[:, 52 + t:53 + t], ROUTED_SCALE, ALU.mult, ALU.mult)
                modulated(10, 2)
                b = v.next()
                dve.wait_ge(vfull[b], 1).then_inc(vfull[b], -1)
                cnt = vb[b][:, NT * NE:NT * NE + NE]
                pos = vb[b][:, 0:NT * NE].rearrange("p (a b) -> p a b", b=NE)
                vec.tensor_scalar(nblk[:, :], cnt, 1.0, None, ALU.is_ge)
                vec.tensor_scalar(place[:, :, :], pos, float(P), 1.0 - P * NJ, ALU.is_ge, ALU.mult)
                vec.tensor_scalar(rep[:, :, 0:NE], pos, 2.0 * P, 1.0 - P * NJ, ALU.is_ge, ALU.mult)
                settle()
                for k in (1, 2):
                    vec.scalar_tensor_tensor(nblk[:, :], cnt, k * P + 1.0, nblk[:, :], ALU.is_ge, ALU.add)
                    settle()
                vec.tensor_tensor_scan(incl[:, :], c_("ones")[:, 0:NE], nblk[:, :], 0.0, ALU.mult, ALU.add)
                vec.tensor_tensor(place[:, :, :], place[:, :, :], rep[:, :, 0:NE], ALU.add)
                settle()
                vec.scalar_tensor_tensor(place[:, :, :], pos, float(NJ), place[:, :, :], ALU.mult, ALU.add)
                vec.scalar_tensor_tensor(first_job[:, :], incl[:, :], 1.0, nblk[:, :], ALU.add, ALU.subtract)
                settle()
                dve.sem_inc(vfree[b], 1)
                vec.tensor_tensor(place[:, :, :], place[:, :, :], first_job[:, :].unsqueeze(1).to_broadcast([P, NT, NE]),
                                  ALU.add)
                settle()
                vec.tensor_tensor(place[:, :, :], place[:, :, :], chosen[:, :, :], ALU.mult)
                settle()
                for t in range(NT):
                    vec.max(top_place[:, t, :], place[:, t, :])
                settle()
                vec.tensor_scalar(place_u[:, :].rearrange("p (a b) -> p a b", b=TOPK), top_place[:, :, 0:TOPK], -1.0, None,
                                  ALU.add)
                for t in range(NT):
                    e3 = eq[:, TOPK * NE * t:TOPK * NE * (t + 1)].rearrange("p (a b) -> p a b", b=NE)
                    vec.tensor_tensor(e3, place[:, t, :].unsqueeze(1).to_broadcast([P, TOPK, NE]),
                                      top_place[:, t, 0:TOPK].unsqueeze(2).to_broadcast([P, TOPK, NE]), ALU.is_equal)
                settle()
                for t in range(NT):
                    e3 = eq[:, TOPK * NE * t:TOPK * NE * (t + 1)].rearrange("p (a b) -> p a b", b=NE)
                    vec.tensor_tensor(e3, e3, gate[:, t, :].unsqueeze(1).to_broadcast([P, TOPK, NE]), ALU.mult)
                settle()
                vec.reduce_sum(entry[:, :, :, 1], eq.rearrange("p (t a b) -> p t a b", a=TOPK, b=NE), axis=AX.X)
                tell(entries_ready)
                vec.tensor_tensor(cmp, incl[0:1, :].unsqueeze(1).to_broadcast([1, NJ, NE]),
                                  c_("jobs")[0:1, :].unsqueeze(2).to_broadcast([1, NJ, NE]), ALU.is_le)
                settle()
                vec.reduce_sum(small[0:1, 0:NJ], cmp, axis=AX.X)
                settle()
                vec.tensor_scalar(job_expert[:, :], small[0:1, 0:NJ], NE - 1.0, None, ALU.min)
                vec.tensor_scalar(sbig[0:1, 0:NJ // 2], c_("jobs")[0:1, 0:NJ:2], incl[0:1, NE - 1:NE], None, ALU.is_lt)
                settle()
                vec.reduce_sum(sbig[0:1, 60:61], sbig[0:1, 0:NJ // 2], axis=AX.X)
                settle()
                for k in range(3):
                    vec.tensor_scalar(job_count[:, k:k + 1], sbig[0:1, 60:61], float(-k), None, ALU.add)
                tell(jobs_sp)
                tell(jobs_pool)
                tell(jobs_pe)
                tell(jobs_act)
                dve.wait_ge(kv_stored, 64).then_inc(kv_stored, -64)

                def weighted(b, g):
                    dve.wait_ge(si_ready, 1).then_inc(si_ready, -1)
                    vec.scalar_tensor_tensor(aa[b], vb[b][:, DE:2 * DE], g, si[b], ALU.mult, ALU.mult)\
                        .then_inc(vfree[b], 1)
                    tell(a_ready)

                def out_rows(dst):
                    for n in range(2):
                        dve.wait_ge(vfull[2 + n], 1).then_inc(vfull[2 + n], -1)
                        vec.tensor_copy(dst[:, 512 * n:512 * n + 512], vb[2 + n][:, :]).then_inc(vfree[2 + n], 1)

                weighted(0, 1.0)
                for t in range(1, NT):
                    weighted(t % 2, 1.0)
                    out_rows(acc[:, t - 1, :])
                out_rows(acc[:, NT - 1, :])
                tell(shared_ready)
                dve.wait_ge(table_ready, 1).then_inc(table_ready, -1)

                def job_rows(b):
                    dve.wait_ge(yj_free, 1).then_inc(yj_free, -1)
                    out_rows(Y[b])
                    tell(yj_ready)

                weighted(0, table[:, 0, 1:2])
                weighted(1, table[:, 1, 1:2])
                job_rows(0)
                with dve.Fori(0, job_pairs(dve, 1)) as j:
                    for b in range(2):
                        weighted(b, table[:, bass.ds(2 * j + 2 + b, 1), 1])
                        job_rows(1 - b)
                job_rows(1)
                v.restart()
                residual(5)
            tell(y_ready)
            dve.wait_ge(fin_stored, 16).then_inc(fin_stored, -16)


_OUTS = [("yT", (P, KC, T)), ("wk", (DEPTH, P, 128)), ("wv", (DEPTH, P, 128)), ("nk", (DEPTH, P, 256)),
         ("nv", (DEPTH, P, 256)), ("fin", (DEPTH, P, 256))]


def constants():
    import numpy as np

    con = np.zeros((P, CNW), np.float32)

    def put(name, x):
        con[:, CN[name][0]:CN[name][1]] = np.asarray(x, np.float32).reshape(P, -1)

    i = np.arange(P)
    put("ident", np.eye(P))
    put("blk64", (i[:, None] // 64 == i[None] // 64) / 64.0)
    same = i[:, None] // CH == i[None] // CH
    put("mask0", same & (i[:, None] <= i[None]))
    put("mask1", same & (i[:, None] >= i[None]))
    put("chunk", i[:, None] // CH == np.arange(TC)[None])
    put("first", np.broadcast_to(np.arange(2 * T) % CH != 0, (P, 2 * T)))
    qc = i % 64
    start = np.clip(qc - 8, 0, 48)[:, None]
    kc = np.arange(64)[None]
    put("nmask", np.where((kc >= start) & (kc < start + 16), 0.0, NEG))
    wm = np.zeros((P, 2, T), np.float32)
    qp = i[:, None] + P * np.arange(2)[None]
    wm[:, :, 0:256] = np.where(np.abs(np.arange(256)[None, None] - qp[:, :, None]) <= 128, 0.0, NEG)
    put("wmask", wm)
    t = np.arange(256)
    inv = (10000.0 ** (-np.arange(16) / 16)).astype(np.float32)
    cos = np.zeros((256, 4, 16), np.float32)
    sin = np.zeros((256, 4, 16), np.float32)
    for half, pos in enumerate((t // 64, t % 64)):
        ang = pos.astype(np.float32)[:, None] * inv[None]
        cos[:, 2 * half] = cos[:, 2 * half + 1] = np.cos(ang)
        sin[:, 2 * half], sin[:, 2 * half + 1] = -np.sin(ang), np.sin(ang)
    put("cos", cos.reshape(2, P, 64).transpose(1, 0, 2))
    put("sin", sin.reshape(2, P, 64).transpose(1, 0, 2))
    cnt = np.zeros((4, PADU), np.float32)
    for g, size in enumerate((2, 4, 8, 16)):
        for at, n in ((8, P), (152, 256)):
            pos = np.arange(n)
            cnt[g, at:at + n] = 1.0 / (np.clip(pos + size // 2, 0, n) - np.clip(pos - size // 2, 0, n))
    both = np.zeros((P, 2, PADU), np.float32)
    for g in range(4):
        both[64 * (g % 2):64 * (g % 2) + 64, g // 2] = cnt[g]
    put("inv", both)
    put("eps", np.full((P, 1), EPS))
    put("before", i[:, None] < i[None])
    put("ones", np.ones((P, P)))
    put("jobs", np.broadcast_to(np.arange(NJ), (P, NJ)))
    put("token", i[:, None] + P * np.arange(NT)[None])
    return con


def kernel(**inputs):
    import numpy as np
    import concourse.bacc as bacc
    from concourse.bass_utils import run_bass_kernel_spmd as run

    a = {k: np.asarray(v) for k, v in inputs.items()}
    L_ = DEPTH

    def pc(x):
        return x.reshape(x.shape[:-1] + (P, KC))

    def cp(x):
        return np.swapaxes(x.reshape(x.shape[:-1] + (-1, P)), -1, -2)

    def rows(x):
        return np.broadcast_to(x[:, None, :], (L_, P, x.shape[-1]))

    x = np.concatenate([a["x_prompt"][0], a["x_sample"][0]], axis=0)
    h = {"con": constants(),
         "xT": np.transpose(pc(x), (1, 2, 0)),
         "cT": np.stack([pc(a["c_ctx"]), pc(a["c"][0])], axis=-1)}
    wm = a["w_mod"].reshape(L_, D, 6, P, KC)
    h["w_mod"] = np.swapaxes(wm, -1, -2).reshape(L_, D, 6 * D)
    bm = a["b_mod"].reshape(L_, 6, P, KC).transpose(0, 2, 1, 3)
    sink = np.concatenate([a["win_sink"], np.full((L_, 4), NEG, np.float32)], axis=1)
    h["sm"] = np.concatenate([
        pc(a["norm1_g"]), pc(a["norm2_g"]),
        np.repeat(bm.reshape(L_, P, 48), 2, axis=-1),
        cp(a["b_mgate"]),
        np.tile(a["hg_onorm"], (1, 2))[:, :, None],
        cp(a["pool_scale"]),
        rows(a["b_router"]), rows(a["win_qn"]), rows(a["win_kn"]), rows(a["na_qn"]), rows(a["na_kn"]), rows(sink),
        np.broadcast_to(cp(a["hg_lb"]).transpose(2, 0, 1, 3).reshape(1, P, 8), (L_, P, 8)),
    ], axis=2)
    kw = a["cache_win_k"][0].transpose(0, 2, 3, 1).reshape(L_, P, P)
    kn = a["cache_na_k"][0].transpose(0, 2, 3, 1).reshape(L_, 2, P, P).transpose(0, 2, 1, 3).reshape(L_, P, 256)
    h["kcT"] = np.concatenate([kw, kn], axis=2)
    h["vc"] = np.concatenate([a["cache_win_v"][0].reshape(L_, P, P), a["cache_na_v"][0].reshape(L_, P, 256)], axis=2)
    h["s0"] = a["state_hgrn"][0].reshape(L_, 2, 2, 2, HD, HD).transpose(0, 3, 4, 1, 2, 5).reshape(L_, P, 256)
    h["poolw"] = a["pool_w"].reshape(L_, 2, 2, HD, HD).transpose(0, 2, 3, 1, 4).reshape(L_, P, P)
    h["rpb"] = a["na_rpb"][:, :, ::-1, ::-1].reshape(L_, 4, 465)
    for k in ("w_in", "w_mgate", "w_branch", "w_out", "w_router", "w_sg", "w_su", "w_sd"):
        h[k] = a[k]
    for k in ("w_eg", "w_eu", "w_ed"):
        h[k] = a[k].reshape((L_ * NE,) + a[k].shape[2:])

    nc = bacc.Bacc("TRN2", target_bir_lowering=False, num_devices=1)
    arrays, A, O = {}, {}, {}
    for k, arr in h.items():
        arr = np.ascontiguousarray(arr)
        arrays["in_" + k] = arr
        A[k] = nc.dram_tensor("in_" + k, arr.shape, mybir.dt.from_np(arr.dtype), kind="ExternalInput").ap()
    for k, shape in _OUTS:
        O[k] = nc.dram_tensor("out_" + k, shape, F32, kind="ExternalOutput").ap()
    build(nc, A, O)
    r = run(nc, [arrays], core_ids=[0]).results[0]
    o = {k: r["out_" + k] for k, _ in _OUTS}
    y = np.transpose(o["yT"], (2, 0, 1)).reshape(T, D)
    fin = o["fin"].reshape(L_, 2, HD, 2, 2, HD).transpose(0, 3, 4, 1, 2, 5).reshape(1, L_, 2, 4, HD, HD)
    return (y[None, 0:P], y[None, P:T],
            o["wk"].reshape(1, L_, P, 2, HD), o["wv"].reshape(1, L_, P, 2, HD),
            o["nk"].reshape(1, L_, P, 4, HD), o["nv"].reshape(1, L_, P, 4, HD), fin)
```
